# Optimizing a Trainium2 kernel written in Bass

```python
import math
import jax, jax.numpy as jnp
from jax import lax
import numpy as np

D_MODEL = 1024
BATCH = 1
SEQ = 512
DEPTH = 2

CHUNK = 64
QBLOCK = 128
EPS = 1e-6
ADA_STD = 0.2

D_FF = 4 * D_MODEL

MIX_A = D_MODEL // 2
POOL_WINDOWS = (2, 4, 8, 16)
POOL_GROUPS = len(POOL_WINDOWS)
POOL_CH = MIX_A // POOL_GROUPS
MIX_B = D_MODEL - MIX_A
SSM_GROUP = 16
SSM_GROUPS = MIX_B // SSM_GROUP
SSM_STATE = 64
DT_MIN = 1e-3
DT_MAX = 1e-1

HEAD_DIM = 64
C_HEADS = (D_MODEL // 2) // HEAD_DIM
D_HEADS = (D_MODEL // 2) // HEAD_DIM
C_W = C_HEADS * HEAD_DIM
D_W = D_HEADS * HEAD_DIM
IDX_HEADS = 8
IDX_DIM = 64
IDX_SCALE = (IDX_HEADS ** -0.5) * (IDX_DIM ** -0.5)
TOPK_MAX = 256
IN_CD_WIDTHS = (C_W, C_W, C_W, IDX_HEADS * IDX_DIM, IDX_DIM, IDX_HEADS, D_W, D_W, D_W)
IN_CD = sum(IN_CD_WIDTHS)

N_EVEN = (DEPTH + 1) // 2
N_ODD = DEPTH // 2

kernel_name = "hybrid_pool_s5_dsa_stickbreak_trunk"

def _rmsnorm(x, g):
    xf = x.astype(jnp.float32)
    y = xf * lax.rsqrt(jnp.mean(xf * xf, axis=-1, keepdims=True) + EPS)
    return (y * g.astype(jnp.float32)).astype(x.dtype)

def _modulate(x, c, g, w, b):
    m = (c @ w + b)[:, None, :]
    shift, scale, gate = jnp.split(m, 3, axis=-1)
    h = _rmsnorm(x, g) * (1.0 + scale) + shift
    return h, 1.0 + gate

def _to_blocks(a):
    b, l = a.shape[:2]
    return jnp.moveaxis(a.reshape(b, l // QBLOCK, QBLOCK, *a.shape[2:]), 1, 0)

def _from_blocks(a):
    a = jnp.moveaxis(a, 0, 1)
    return a.reshape(a.shape[0], a.shape[1] * a.shape[2], -1)

def _pool_mixer(u, w_pool, scale):
    bsz, L, _ = u.shape
    ug = u.astype(jnp.float32).reshape(bsz, L, POOL_GROUPS, POOL_CH)
    cs = jnp.concatenate([jnp.zeros((bsz, 1, POOL_GROUPS, POOL_CH), jnp.float32),
                          jnp.cumsum(ug, axis=1)], axis=1)
    t = jnp.arange(L)
    pooled = []
    for g, win in enumerate(POOL_WINDOWS):
        lo = jnp.maximum(t + 1 - win, 0)
        cnt = jnp.minimum(t + 1, win).astype(jnp.float32)
        pooled.append((cs[:, 1:, g] - cs[:, lo, g]) / cnt[None, :, None])
    p = jnp.stack(pooled, axis=2) - ug
    y = jnp.einsum('blgc,gcd->blgd', p, w_pool.astype(jnp.float32))
    return (y.reshape(bsz, L, MIX_A) * scale.astype(jnp.float32)).astype(u.dtype)

def _ssm_combine(e1, e2):
    a1r, a1i, b1r, b1i = e1
    a2r, a2i, b2r, b2i = e2
    return (a2r * a1r - a2i * a1i,
            a2r * a1i + a2i * a1r,
            a2r * b1r - a2i * b1i + b2r,
            a2r * b1i + a2i * b1r + b2i)

def _s5_mixer(u, lam_re, lam_im, log_dt, b_re, b_im, c_re, c_im, d_skip, w_glu, b_glu):
    bsz, L, _ = u.shape
    f32 = jnp.float32
    ug = u.astype(f32).reshape(bsz, L, SSM_GROUPS, SSM_GROUP)
    lr, li = lam_re.astype(f32), lam_im.astype(f32)
    dt = jnp.exp(log_dt.astype(f32))[:, None]
    mag = jnp.exp(lr * dt)
    ar, ai = mag * jnp.cos(li * dt), mag * jnp.sin(li * dt)
    den = lr * lr + li * li
    zr = ((ar - 1.0) * lr + ai * li) / den
    zi = (ai * lr - (ar - 1.0) * li) / den
    br, bi = b_re.astype(f32), b_im.astype(f32)
    bbr = zr[..., None] * br - zi[..., None] * bi
    bbi = zr[..., None] * bi + zi[..., None] * br
    xr = jnp.einsum('blgc,gpc->blgp', ug, bbr)
    xi = jnp.einsum('blgc,gpc->blgp', ug, bbi)
    a_r = jnp.broadcast_to(ar, (1, L, SSM_GROUPS, SSM_STATE))
    a_i = jnp.broadcast_to(ai, (1, L, SSM_GROUPS, SSM_STATE))
    _, _, hr, hi = lax.associative_scan(_ssm_combine, (a_r, a_i, xr, xi), axis=1)
    y = (jnp.einsum('gcp,blgp->blgc', c_re.astype(f32), hr)
         - jnp.einsum('gcp,blgp->blgc', c_im.astype(f32), hi)
         + d_skip.astype(f32).reshape(SSM_GROUPS, SSM_GROUP) * ug)
    y = jax.nn.gelu(y.reshape(bsz, L, MIX_B))
    y = y * jax.nn.sigmoid(y @ w_glu.astype(f32) + b_glu.astype(f32))
    return y.astype(u.dtype)

def _alibi_slopes(n_heads):
    return jnp.exp2(-8.0 * jnp.arange(1, n_heads + 1, dtype=jnp.float32) / n_heads)

def _dsa_mixer(q, k, v, qi, ki, wi):
    L = q.shape[1]
    topk = min(TOPK_MAX, L // 4)
    key_chunk = jnp.arange(L) // CHUNK
    slopes = _alibi_slopes(C_HEADS)
    nb = L // QBLOCK

    def step(args):
        qb, qib, wib, t0 = args
        t = t0 + jnp.arange(QBLOCK)
        q_chunk = t // CHUNK
        adm = key_chunk[None, :] <= q_chunk[:, None]
        rel = jax.nn.relu(jnp.einsum('bqhd,bsd->bqhs', qib, ki))
        score = jnp.einsum('bqhs,bqh->bqs', rel, wib) * IDX_SCALE
        score = jnp.where(adm[None], score, -jnp.inf)
        _, sel = lax.top_k(score, topk)
        valid = (sel // CHUNK) <= q_chunk[None, :, None]
        kg = jax.vmap(lambda kb, ib: kb[ib])(k, sel)
        vg = jax.vmap(lambda vb, ib: vb[ib])(v, sel)
        logits = jnp.einsum('bqhd,bqkhd->bhqk', qb, kg) * (HEAD_DIM ** -0.5)
        dist = jnp.abs(t[None, :, None] - sel).astype(jnp.float32)
        logits = logits - slopes[None, :, None, None] * dist[:, None]
        logits = jnp.where(valid[:, None], logits, -jnp.inf)
        p = jax.nn.softmax(logits, axis=-1)
        return jnp.einsum('bhqk,bqkhd->bqhd', p, vg)

    out = lax.map(step, (_to_blocks(q), _to_blocks(qi), _to_blocks(wi),
                         jnp.arange(nb, dtype=jnp.int32) * QBLOCK))
    return _from_blocks(out)

def _stick_breaking_mixer(q, k, v):
    L = q.shape[1]
    pos = jnp.arange(L)
    nb = L // QBLOCK

    def step(args):
        qb, t0 = args
        t = t0 + jnp.arange(QBLOCK)
        z = jnp.einsum('bqhd,bshd->bhqs', qb, k) * (HEAD_DIM ** -0.5)
        causal = (pos[None, :] < t[:, None])[None, None]
        log_keep = jnp.where(causal, jax.nn.log_sigmoid(-z), 0.0)
        after = lax.cumsum(log_keep, axis=3, reverse=True) - log_keep
        w = jnp.where(causal, jnp.exp(jax.nn.log_sigmoid(z) + after), 0.0)
        return jnp.einsum('bhqs,bshd->bqhd', w, v)

    out = lax.map(step, (_to_blocks(q), jnp.arange(nb, dtype=jnp.int32) * QBLOCK))
    return _from_blocks(out)

def _ab_mixer(h, w_in, w_out, pool_w, pool_scale, lam_re, lam_im, log_dt,
              b_re, b_im, c_re, c_im, d_skip, w_glu, b_glu):
    proj = h @ w_in
    ua, ub = proj[..., :MIX_A], proj[..., MIX_A:]
    ya = _pool_mixer(ua, pool_w, pool_scale)
    yb = _s5_mixer(ub, lam_re, lam_im, log_dt, b_re, b_im, c_re, c_im, d_skip, w_glu, b_glu)
    return jnp.concatenate([ya, yb], axis=-1) @ w_out

def _cd_mixer(h, w_in, w_out):
    bsz, L, _ = h.shape
    f32 = jnp.float32
    proj = (h @ w_in).astype(f32)
    offs = np.cumsum(IN_CD_WIDTHS)[:-1].tolist()
    qc, kc, vc, qi, ki, wi, qd, kd, vd = jnp.split(proj, offs, axis=-1)
    hd = lambda a, n: a.reshape(bsz, L, n, -1)
    oc = _dsa_mixer(hd(qc, C_HEADS), hd(kc, C_HEADS), hd(vc, C_HEADS),
                    hd(qi, IDX_HEADS), ki, wi)
    od = _stick_breaking_mixer(hd(qd, D_HEADS), hd(kd, D_HEADS), hd(vd, D_HEADS))
    y = jnp.concatenate([oc, od], axis=-1).astype(h.dtype)
    return y @ w_out

def _sq_relu_mlp(h, w1, w2):
    a = jax.nn.relu(h @ w1)
    return (a * a) @ w2

def setup_inputs(seed: int = 0) -> dict:
    key = jax.random.key(seed)
    ks = jax.random.split(key, 26)
    f32 = jnp.float32
    nrm = lambda k, shape, s: jax.random.normal(k, shape, f32) * s
    D = D_MODEL
    G, P, C = SSM_GROUPS, SSM_STATE, SSM_GROUP
    return {
        "x": nrm(ks[0], (BATCH, SEQ, D), 1.0),
        "c": nrm(ks[1], (BATCH, D), 1.0),
        "norm_g": 1.0 + nrm(ks[2], (DEPTH, 2, D), 0.1),
        "ada_w": nrm(ks[3], (DEPTH, 2, D, 3 * D), ADA_STD * D ** -0.5),
        "ada_b": nrm(ks[4], (DEPTH, 2, 3 * D), 0.01),
        "mlp_w1": nrm(ks[5], (DEPTH, D, D_FF), D ** -0.5),
        "mlp_w2": nrm(ks[6], (DEPTH, D_FF, D), D_FF ** -0.5),
        "ab_w_in": nrm(ks[7], (N_EVEN, D, MIX_A + MIX_B), D ** -0.5),
        "ab_w_out": nrm(ks[8], (N_EVEN, MIX_A + MIX_B, D), (MIX_A + MIX_B) ** -0.5),
        "pool_w": nrm(ks[9], (N_EVEN, POOL_GROUPS, POOL_CH, POOL_CH), POOL_CH ** -0.5),
        "pool_scale": 1.0 + nrm(ks[10], (N_EVEN, MIX_A), 0.1),
        "ssm_lam_re": -0.5 + nrm(ks[11], (N_EVEN, G, P), 0.01),
        "ssm_lam_im": jnp.pi * jnp.arange(P, dtype=f32) + nrm(ks[12], (N_EVEN, G, P), 0.01),
        "ssm_log_dt": jax.random.uniform(ks[13], (N_EVEN, G), f32, math.log(DT_MIN), math.log(DT_MAX)),
        "ssm_b_re": nrm(ks[14], (N_EVEN, G, P, C), (2 * C) ** -0.5),
        "ssm_b_im": nrm(ks[15], (N_EVEN, G, P, C), (2 * C) ** -0.5),
        "ssm_c_re": nrm(ks[16], (N_EVEN, G, C, P), (2 * P) ** -0.5),
        "ssm_c_im": nrm(ks[17], (N_EVEN, G, C, P), (2 * P) ** -0.5),
        "ssm_d": nrm(ks[18], (N_EVEN, MIX_B), 1.0),
        "glu_w": nrm(ks[19], (N_EVEN, MIX_B, MIX_B), MIX_B ** -0.5),
        "glu_b": nrm(ks[20], (N_EVEN, MIX_B), 0.01),
        "cd_w_in": nrm(ks[21], (N_ODD, D, IN_CD), D ** -0.5),
        "cd_w_out": nrm(ks[22], (N_ODD, C_W + D_W, D), (C_W + D_W) ** -0.5),
        "final_g": 1.0 + nrm(ks[23], (D,), 0.1),
    }

def reference(x, c, norm_g, ada_w, ada_b, mlp_w1, mlp_w2, ab_w_in, ab_w_out, pool_w, pool_scale,
              ssm_lam_re, ssm_lam_im, ssm_log_dt, ssm_b_re, ssm_b_im, ssm_c_re, ssm_c_im, ssm_d,
              glu_w, glu_b, cd_w_in, cd_w_out, final_g):
    for i in range(DEPTH):
        j = i // 2
        h, gate = _modulate(x, c, norm_g[i, 0], ada_w[i, 0], ada_b[i, 0])
        if i % 2 == 0:
            y = _ab_mixer(h, ab_w_in[j], ab_w_out[j], pool_w[j], pool_scale[j],
                          ssm_lam_re[j], ssm_lam_im[j], ssm_log_dt[j], ssm_b_re[j], ssm_b_im[j],
                          ssm_c_re[j], ssm_c_im[j], ssm_d[j], glu_w[j], glu_b[j])
        else:
            y = _cd_mixer(h, cd_w_in[j], cd_w_out[j])
        x = x + gate * y
        h, gate = _modulate(x, c, norm_g[i, 1], ada_w[i, 1], ada_b[i, 1])
        x = x + gate * _sq_relu_mlp(h, mlp_w1[i], mlp_w2[i])
    return _rmsnorm(x, final_g)


_drawn_inputs = setup_inputs


def setup_inputs(seed=0):
    import zlib

    import numpy as np

    out = dict(_drawn_inputs(seed))
    spreads = {}
    factors = {'ssm_lam_re': 64.0,
     'ssm_b_re': 3.076,
     'ssm_b_im': 3.373,
     'ssm_c_re': 3.248,
     'ssm_c_im': 3.056,
     'glu_b': 25.979}
    for name, (base, spread) in spreads.items():
        noise = np.random.default_rng([zlib.crc32(name.encode()), seed]).standard_normal(out[name].shape)
        drawn = base * np.exp(spread * noise) if base else spread * noise
        out[name] = __import__('jax').numpy.asarray(drawn.astype(out[name].dtype))
    for name, factor in factors.items():
        out[name] = (out[name] * factor).astype(out[name].dtype)
    return out
```

```python
import math

import concourse.bass as bass
from concourse import mybir

ALU = mybir.AluOpType
ACT = mybir.ActivationFunctionType
F32 = mybir.dt.float32
F32R = mybir.dt.float32r
I32 = mybir.dt.int32
AX_X = mybir.AxisListType.X

P = 128
D = 1024
L = 512
KC = D // P
NB = L // P
FF = 4 * D
SLOT = 256
QUARTERS = 4
QT = FF // QUARTERS // P
EPS = 1e-6
CHUNK = 64
HALF = D // 2

G, S, C = 32, 64, 16
RUN = P // C
NRUN = L // RUN
GT = G // 2
WINDOWS = (2, 4, 8, 16)
PAD = 16

H, HD = 8, 64
TOPK = 128
IDX_SCALE = (8 ** -0.5) * (64 ** -0.5)
SLOPES = [2.0 ** (-8.0 * (h + 1) / H) for h in range(H)]
UNSEEN = -1.0e30
TAKEN = -3.0e38
FAR = 1.0e30
ADA_Q = 3 * D // 4
ADA_RING = 3


def trunk(nc, x, c, norm_g, ada_w, ada_b, mlp_w1, mlp_w2, ab_w_in, ab_w_out, pool_w, pool_scale,
          ssm_lam_re, ssm_lam_im, ssm_log_dt, ssm_b_re, ssm_b_im, ssm_c_re, ssm_c_im, ssm_d,
          glu_w, glu_b, cd_w_in, cd_w_out, final_g, out):

    cursor = [(nc.sbuf_base + 63) // 64 * 64]

    def place(name, shape, dt=F32, offset=None):
        size = 4 * math.prod(shape[1:])
        if offset is None:
            offset = cursor[0]
            cursor[0] += (size + 31) // 32 * 32
        return nc.alloc_sbuf_tensor_at(name, shape, dt, offset=offset)

    xT = place("xT", [P, KC, L])
    h_at = cursor[0]
    h_hi = place("h_hi", [P, KC, L], F32R)
    h_lo = place("h_lo", [P, KC, L], F32R)
    raw = [place(f"w_raw{i}", [P, 8, SLOT]) for i in range(2)]
    w_hi = [place(f"w_hi{i}", [P, 8, SLOT], F32R) for i in range(2)]
    w_lo = [place(f"w_lo{i}", [P, 8, SLOT], F32R) for i in range(2)]
    ada_ring = place("ada_ring", [P, ADA_RING, ADA_Q])
    ada_acc = place("ada_acc", [P, ADA_Q])
    ident = place("ident", [P, P])
    ones = place("ones", [P, P])
    pa = place("pa", [P, P])
    pb = place("pb", [P, 72])
    mods = place("mods", [P, 4, 24])
    eps_t = place("eps_t", [P, 8])
    recip = place("recip", [P, PAD])
    small = place("small", [P, 64])
    wi_t = place("wi_t", [P, NB, 8])
    work = [place(f"work{i}", [P, L + PAD]) for i in range(4)]
    sumsq = place("sumsq", [P, L])
    rstd = place("rstd", [P, L])
    pool_w_t = place("pool_w_t", [P, 4, P])
    arena = cursor[0]

    def lay(at, name, shape, dt=F32):
        t = place(name, shape, dt, offset=at[0])
        at[0] += (4 * math.prod(shape[1:]) + 31) // 32 * 32
        return t

    at = [h_at]
    x_nat = lay(at, "x_nat", [P, NB, D])
    kr = place("kr", [C, G, P], F32, offset=h_at)
    g_tmp = lay(at, "g_tmp", [P, GT, RUN + 1, C])
    raw_a = lay(at, "raw_a", [P, P])
    raw_b = lay(at, "raw_b", [56, P])
    raw_dt2 = lay(at, "raw_dt2", [GT, 2])
    raw_dt = lay(at, "raw_dt", [GT, P])
    c_nat = lay(at, "c_nat", [P, 4, P])
    at = [arena]
    f_at = arena
    f_re = lay(at, "f_re", [P, GT, RUN, C])
    f_im = lay(at, "f_im", [P, GT, RUN, C])
    at[0] += 512
    g_re = lay(at, "g_re", [P, GT, RUN + 1, C])
    g_ni = lay(at, "g_ni", [P, GT, RUN + 1, C])
    toep = lay(at, "toep", [P, G, P])
    e_at = at[0]
    e_re = lay(at, "e_re", [P, GT, P])
    e_im = lay(at, "e_im", [P, GT, P])
    u_at = at[0]
    u_run = lay(at, "u_run", [P, G, NRUN])
    rot_c = lay(at, "rot_c", [P, GT, NRUN])
    rot_s = lay(at, "rot_s", [P, GT, NRUN])
    assert at[0] <= nc.sbuf_usable_end, (at[0], nc.sbuf_usable_end)
    at = [f_at]
    ub = lay(at, "ub", [P, 4, RUN, NRUN])
    ua = lay(at, "ua", [P, 4, L + PAD])
    at = [f_at]
    b_re = lay(at, "b_re", [P, GT, NRUN])
    b_im = lay(at, "b_im", [P, GT, NRUN])
    y_act = place("y_act", [P, 4, L], F32, offset=f_at)
    at = [e_at]
    s_re = lay(at, "s_re", [P, GT, NRUN])
    s_im = lay(at, "s_im", [P, GT, NRUN])
    s_t1 = lay(at, "s_t1", [P, GT, NRUN])
    s_t2 = lay(at, "s_t2", [P, GT, NRUN])
    f_tmp = place("f_tmp", [P, GT, RUN, C], F32, offset=e_at)
    y_run = place("y_run", [P, G, NRUN], F32, offset=e_at)
    at = [e_at]
    yg_hi = lay(at, "yg_hi", [P, 4, L], F32R)
    yg_lo = lay(at, "yg_lo", [P, 4, L], F32R)
    y_t = place("y_t", [P, 4, L], F32, offset=u_at)
    gate_t = place("gate_t", [P, 4, L], F32, offset=u_at)
    cat_f = place("cat_f", [P, 4, L], F32, offset=u_at + 8192)
    at = [u_at]
    sm = lay(at, "sm", [P, 32, GT])
    pw_re = lay(at, "pw_re", [P, GT, RUN + 1])
    pw_im = lay(at, "pw_im", [P, GT, RUN + 1])
    cb = [lay(at, f"cb{i}", [P, GT, C]) for i in range(2)]
    bb = [lay(at, f"bb{i}", [P, GT, C]) for i in range(2)]
    bz = [place(f"bz{i}", [P, GT, C], F32, offset=u_at + 8192 + i * 1024) for i in range(2)]
    skip = place("skip", [C, G], F32, offset=u_at + 8192 + 2048)
    skip_d = place("skip_d", [C, G, C], F32, offset=u_at + 8192 + 2048 + 128)
    assert at[0] <= u_at + 8192
    at = [arena]
    a_hi = lay(at, "a_hi", [P, QT, L], F32R)
    a_lo = lay(at, "a_lo", [P, QT, L], F32R)
    at = [arena]
    qk = {}
    for name in ("qd", "kd", "vd", "qc", "kc", "vc"):
        qk[name] = lay(at, name, [P, 4, L])
    sel_at = [0, P, P + 2 * P, P + 2 * P + 3 * P]
    dsel = lay(at, "dsel", [P, sum((i + 1) * P for i in range(NB))])
    tri = lay(at, "tri", [P, P])
    idx_at = at[0]
    qi_t = lay(at, "qi_t", [P, 4, L])
    ki_t = lay(at, "ki_t", [P, L])
    dist = lay(at, "dist", [P, L])
    sc_at = [0, 0, 2 * P, 5 * P]
    score = lay(at, "score", [P, 9 * P])
    at = [idx_at]
    W1 = sum((NB - j) * P for j in range(NB))
    z_at = [0, 4 * P, 7 * P, 9 * P]
    z_sb = [lay(at, f"z_sb{i}", [P, W1]) for i in range(2)]
    sp_sb = [lay(at, f"sp_sb{i}", [P, W1]) for i in range(2)]
    pT = lay(at, "pT", [P, NB, L])
    assert at[0] <= nc.sbuf_usable_end, (at[0], nc.sbuf_usable_end)
    y_out = place("y_out", [P, NB, D], F32, offset=arena)

    psum = nc.alloc_psum_tensor("psum", [P, 8 * L], F32)
    bank = [psum[:, i * L:(i + 1) * L] for i in range(8)]

    u_dram = nc.dram_tensor("u_scratch", (HALF, L), F32, kind="Internal").ap()
    y_dram = nc.dram_tensor("y_scratch", (HALF, L), F32, kind="Internal").ap()

    def sem(name):
        return nc.alloc_semaphore(name)

    def cols(w, c0, n=SLOT):
        return w.rearrange("(k p) n -> p k n", p=P)[:, :, c0:c0 + n]

    slots = []
    AB_IN = len(slots)
    slots += [cols(ab_w_in[0], c0) for c0 in (HALF, HALF + SLOT, 0, SLOT)]
    GLU = len(slots)
    slots += [glu_w[0].rearrange("(k p) n -> p k n", p=P)]
    AB_OUT = len(slots)
    slots += [cols(ab_w_out[0], c0) for c0 in range(0, D, SLOT)]
    MLP = [len(slots)]
    slots += [None] * (8 * QUARTERS)
    CD_IN = len(slots)
    CD = dict(qc=0, kc=512, vc=1024, qi=1536, ki=2048, wi=2112, qd=2120, kd=2632, vd=3144)
    cd_order = ["qi", "ki", "qd", "kd", "vd", "qc", "kc", "vc"]
    cd_slots = []
    for name in cd_order:
        for half in range(1 if name == "ki" else 2):
            cd_slots.append((name, half))
            slots.append(None if name == "ki" else cols(cd_w_in[0], CD[name] + half * SLOT))
    KI = CD_IN + cd_slots.index(("ki", 0))
    CD_OUT = len(slots)
    slots += [cols(cd_w_out[0], c0) for c0 in range(0, D, SLOT)]
    MLP.append(len(slots))
    slots += [None] * (8 * QUARTERS)
    NSLOT = len(slots)

    landed = []
    total = [0, 0]
    for n in range(NSLOT):
        total[n % 2] += 48 if n == KI else 16
        landed.append(total[n % 2])

    tiles_of = {n: 2 for n in range(NSLOT)}
    tiles_of[GLU] = 4
    for i, (name, _) in enumerate(cd_slots):
        if name in ("vd", "vc"):
            tiles_of[CD_IN + i] = NB
    first_tile, drains = [], []
    drained = {False: 0, True: 0}
    for n in range(NSLOT):
        first_tile.append(len(drains))
        for _ in range(tiles_of[n]):
            by_dve = AB_OUT <= n < AB_OUT + 4 or CD_OUT <= n < CD_OUT + 4 or \
                any(m <= n < m + 32 and (n - m) % 8 >= 4 for m in MLP)
            drained[by_dve] += 1
            drains.append((by_dve, drained[by_dve]))

    raw_in = [sem("raw_in0"), sem("raw_in1")]
    hi_ready = sem("w_hi_ready")
    lo_ready = sem("w_lo_ready")
    tile_done = sem("tile_done")
    act_drain = sem("act_drained")
    dve_drain = sem("dve_drained")
    square_done = sem("square_done")
    a_ready = sem("a_ready")
    sumsq_ready = sem("sumsq_ready")
    norm_sum = sem("norm_sum")
    rstd_ready = sem("rstd_ready")
    xn_ready = sem("xn_ready")
    hh_ready = sem("h_hi_ready")
    h_ready = sem("h_ready")
    ada_in = [sem(f"ada_in{i}") for i in range(ADA_RING)]
    ada_in_1 = [sem(f"ada_in_1_{i}") for i in range(ADA_RING)]
    ada_used = sem("ada_used")
    ada_sum = sem("ada_sum")
    mods_part = sem("mods_part")
    mods_ready = sem("mods_ready")
    small_in = sem("small_in")
    b_in = sem("b_in")
    d_in = sem("d_in")
    dt_in = sem("dt_in")
    dt_rows = sem("dt_rows")
    poolw_in = sem("poolw_in")
    x_in = sem("x_in")
    consts = sem("consts")
    params_ps = sem("params_ps")
    params = sem("params")
    xT_ps = sem("xT_ps")
    x_ready = sem("x_ready")
    act_own = sem("act_own")
    act_n = [0]
    dve_own = sem("dve_own")
    dve_n = [0]
    pool_own = sem("pool_own")
    pool_n = [0]
    setup_act = sem("setup_act")
    setup_dve = sem("setup_dve")
    powers = sem("powers")
    g_ready = sem("g_ready")
    f_ready = sem("f_ready")
    mats_ps = sem("mats_ps")
    mats_out = sem("mats_out")
    kr_ready = sem("kr_ready")
    toep_zero = sem("toep_zero")
    toep_in = sem("toep_in")
    rot_ready = sem("rot_ready")
    ub_ready = sem("ub_ready")
    u_out = sem("u_out")
    ada_l1 = [sem(f"ada_l1_in{i}") for i in range(2)]
    sq_ready = sem("sq_ready")
    u_in = sem("u_in")
    ua_pad = sem("ua_pad")
    ua_ready = sem("ua_ready")
    pooled = sem("pooled")
    pool_ps = sem("pool_ps")
    pool_free = sem("pool_free")
    inj_ps = sem("inj_ps")
    states = sem("states")
    y_ps = sem("y_ps")
    y_copied = sem("y_copied")
    y_out_s = sem("y_out_s")
    y_in = sem("y_in")
    gelu_hi = sem("gelu_hi")
    gelu_lo = sem("gelu_lo")
    gate_act = sem("gate_act")
    cat_mid = sem("cat_mid")
    cat_hi = sem("cat_hi")
    cat_ready = sem("cat_ready")
    l1_consts = sem("l1_consts")
    idx_in = sem("idx_in")
    idx_ps = sem("idx_ps")
    idx_rel = sem("idx_rel")
    idx_acc = sem("idx_acc")
    dsel_ready = sem("dsel_ready")
    proj = sem("proj_copied")
    z_ps = sem("z_ps")
    z_copied = sem("z_copied")
    z_abs = sem("z_abs")
    z_soft = sem("z_soft")
    sp_diag = sem("sp_diag")
    sp_ready = sem("sp_ready")
    r_ps = sem("r_ps")
    r_used = sem("r_used")
    w_exp = sem("w_exp")
    w_ready = sem("w_ready")
    o_ps = sem("o_ps")
    o_free = sem("o_free")
    s_ps = sem("s_ps")
    s_used = sem("s_used")
    max_ready = sem("max_ready")
    p_exp = sem("p_exp")
    p_ready = sem("p_ready")
    t_ps = sem("t_ps")
    t_copied = sem("t_copied")
    oc_ps = sem("oc_ps")
    fin_t = sem("fin_t")
    fin_ps = sem("fin_ps")
    fin_copied = sem("fin_copied")
    out_done = sem("out_done")

    def w1_src(layer, q, i):
        return mlp_w1[layer].rearrange("(k p) n -> p k n", p=P)[
            :, :, bass.ds(q * (FF // QUARTERS) + i * SLOT, SLOT)]

    def w2_src(layer, q, i):
        v = mlp_w2[layer].rearrange("(k p) n -> p k n", p=P)
        return v[:, bass.ds(q * QT, QT), i * SLOT:(i + 1) * SLOT]

    ADA_STEPS = 8 * 4

    def ada_src(a, qt, k):
        return ada_w[a // 2, a % 2, k * P:(k + 1) * P, bass.ds(qt * ADA_Q, ADA_Q)]

    block = nc.Block()
    block.__enter__()

    @block.sync
    def _(sp):
        sp.dma_start(x_nat[:, :, :], x[0].rearrange("(t p) d -> p t d", p=P)).then_inc(x_in, 16)

        def load(n, src, q=None):
            if n >= 2:
                sp.wait_ge(lo_ready, n - 1 + (0 if q is None else 8 * q))
            dst = raw[n % 2][:, :, :]
            if n == GLU:
                dst = dst.rearrange("p a b -> p (a b)").rearrange("p (k n) -> p k n", k=4)
            sp.dma_start(dst, src).then_inc(raw_in[n % 2], 16)

        def load_ada0(e):
            if e >= ADA_RING:
                sp.wait_ge(ada_used, e - ADA_RING + 1)
            sp.dma_start(ada_ring[:, e % ADA_RING, :], ada_src(0, e // 8, e % 8))\
              .then_inc(ada_in[e % ADA_RING], 16)

        load(0, slots[0])
        load(1, slots[1])
        for e in range(ADA_STEPS):
            load_ada0(e)
        sp.wait_ge(kr_ready, 1)
        sp.wait_ge(toep_zero, 1)
        for m in range(RUN):
            sp.dma_start(toep[m * C:(m + 1) * C, :, (RUN - 1 - m) * C:],
                         kr[:, :, 0:(m + 1) * C]).then_inc(toep_in, 16)
        for n in range(2, GLU + 1):
            load(n, slots[n])
        sp.wait_ge(u_out, 16 * 4)
        sp.wait_ge(rot_ready, 1)
        for m in range(RUN):
            j = RUN - 1 - m
            sp.dma_start(u_run[m * C:(m + 1) * C, :, :],
                         u_dram.rearrange("(g c) t -> c g t", c=C)[:, :, j * NRUN:(j + 1) * NRUN])\
              .then_inc(u_in, 16)
        load(AB_OUT, slots[AB_OUT])
        for half in range(2):
            sp.wait_ge(y_copied, 2 * half + 2)
            g0 = half * G // 2
            for i in range(RUN):
                sp.dma_start(
                    y_dram.rearrange("(g c) t -> c g t", c=C)[:, g0:g0 + G // 2, i * NRUN:(i + 1) * NRUN],
                    y_run[i * C:(i + 1) * C, g0:g0 + G // 2, :]).then_inc(y_out_s, 16)
        sp.wait_ge(y_out_s, 16 * 2 * RUN)
        sp.wait_ge(y_ps, 4)
        for ct in range(4):
            sp.dma_start(y_t[:, ct, :], y_dram[ct * P:(ct + 1) * P, :]).then_inc(y_in, 16)
        for n in range(AB_OUT + 1, MLP[0]):
            load(n, slots[n])

        def quarter(layer, q):
            n0 = MLP[layer]
            for i in range(4):
                load(n0 + i, w1_src(layer, q, i), q)
            for i in range(4):
                load(n0 + 4 + i, w2_src(layer, q, i), q)

        with sp.Fori(0, QUARTERS) as q:
            quarter(0, q)
        for n in range(CD_IN, MLP[1]):
            if n == KI:
                sp.wait_ge(lo_ready, n - 1)
                for c0, src, w in ((0, CD["ki"], HD), (HD, CD["ki"], HD), (2 * HD, CD["wi"], 8)):
                    sp.dma_start(raw[n % 2][:, :, c0:c0 + w], cols(cd_w_in[0], src, w))\
                      .then_inc(raw_in[n % 2], 16)
            else:
                load(n, slots[n])
        with sp.Fori(0, QUARTERS) as q:
            quarter(1, q)
        for k in range(KC):
            sp.wait_ge(fin_copied, k + 1)
            sp.dma_start(out[0].rearrange("(t p) d -> p t d", p=P)[:, :, k * P:(k + 1) * P],
                         y_out[:, :, k * P:(k + 1) * P]).then_inc(out_done, 16)
        sp.wait_ge(out_done, 16 * KC)

    @block.gpsimd
    def _(pool):
        def own(ins):
            pool_n[0] += 1
            ins.then_inc(pool_own, 1)

        def settle():
            pool.wait_ge(pool_own, pool_n[0])

        own(pool.memset(ident[:, :], 0.0))
        own(pool.memset(ones[:, :], 1.0))
        settle()
        pool.affine_select(out=ident[:, :], in_=ident[:, :], compare_op=ALU.not_equal, fill=1.0,
                           base=0, pattern=[[-1, P]], channel_multiplier=1).then_inc(consts, 1)
        own(pool.iota(small[:, 0:PAD].bitcast(I32), pattern=[[1, PAD]], base=1, channel_multiplier=0))
        settle()
        pool.tensor_copy(recip[:, :], small[:, 0:PAD].bitcast(I32)).then_inc(consts, 1)
        pool.memset(toep[:, :, :], 0.0).then_inc(toep_zero, 1)

        squares = [0]

        def square_tile(k, wait):
            wait()
            if squares[0]:
                pool.wait_ge(sumsq_ready, squares[0])
            if k == 0:
                ins = pool.tensor_tensor(sumsq[:, :], xT[:, k, :], xT[:, k, :], ALU.mult)
            else:
                own(pool.tensor_tensor(work[3][:, 0:L], xT[:, k, :], xT[:, k, :], ALU.mult))
                settle()
                ins = pool.tensor_tensor(sumsq[:, :], sumsq[:, :], work[3][:, 0:L], ALU.add)
            ins.then_inc(sumsq_ready, 1)
            squares[0] += 1

        for k in range(KC):
            square_tile(k, lambda: pool.wait_ge(x_ready, k + 1))

        pool.wait_ge(powers, 1)

        def bc(c_t):
            return c_t[:, :, :].unsqueeze(2).to_broadcast([P, GT, RUN + 1, C])

        def bp(p_t):
            return p_t[:, :, :].unsqueeze(3).to_broadcast([P, GT, RUN + 1, C])

        def tt(o, a, b, op):
            own(pool.tensor_tensor(o, a, b, op))
            settle()

        tt(g_re[:, :, :, :], bc(cb[0]), bp(pw_re), ALU.mult)
        tt(g_tmp[:, :, :, :], bc(cb[1]), bp(pw_im), ALU.mult)
        tt(g_re[:, :, :, :], g_re[:, :, :, :], g_tmp[:, :, :, :], ALU.subtract)
        tt(g_ni[:, :, :, :], bc(cb[0]), bp(pw_im), ALU.mult)
        tt(g_tmp[:, :, :, :], bc(cb[1]), bp(pw_re), ALU.mult)
        tt(g_ni[:, :, :, :], g_ni[:, :, :, :], g_tmp[:, :, :, :], ALU.add)
        pool.tensor_scalar(g_ni[:, :, :, :], g_ni[:, :, :, :], -1.0, None, ALU.mult)\
            .then_inc(g_ready, 1)

        norms = [0]

        def normalise():
            norms[0] += 1
            pool.wait_ge(rstd_ready, norms[0])
            for k in range(KC):
                if k >= 2:
                    pool.wait_ge(h_ready, 8 * (norms[0] - 1) + k - 1)
                pool.tensor_tensor(work[k % 2][:, 0:L], xT[:, k, :], rstd[:, :], ALU.mult)\
                    .then_inc(xn_ready, 1)

        normalise()

        for w in (0, 1):
            pool.wait_ge(h_ready, 8)
            own(pool.memset(work[w][:, 0:PAD], 0.0))
        pool.wait_ge(ua_pad, 1)
        for ct in range(4):
            pool.wait_ge(act_drain, drains[first_tile[AB_IN + 2] + ct][1])
            if ct:
                pool.wait_ge(pooled, ct)
            u = ua[:, ct, :]
            src, step = u, 1
            for r in range(ct + 1):
                settle()
                dst = work[r % 2][:, :]
                own(pool.tensor_tensor(dst[:, PAD:], src[:, PAD:], src[:, PAD - step:PAD + L - step],
                                       ALU.add))
                src, step = dst, 2 * step
            win = WINDOWS[ct]
            settle()
            own(pool.tensor_tensor(src[:, PAD:PAD + win], src[:, PAD:PAD + win], recip[:, 0:win],
                                   ALU.mult))
            own(pool.tensor_scalar(src[:, PAD + win:], src[:, PAD + win:], 1.0 / win, None, ALU.mult))
            settle()
            pool.tensor_tensor(u[:, PAD:], src[:, PAD:], u[:, PAD:], ALU.subtract).then_inc(pooled, 1)

        def ada_dma(e, src, ring_value):
            pool.wait_ge(ada_used, ring_value)
            pool.dma_start(ada_ring[:, e % ADA_RING, :], src).then_inc(ada_in_1[e % ADA_RING], 16)

        for e in range(ADA_STEPS, 2 * ADA_STEPS):
            ada_dma(e, ada_src(1, (e // 8) % 4, e % 8), e - ADA_RING + 1)
        for k in range(KC):
            d = drains[first_tile[AB_OUT] + k]
            square_tile(k, lambda: pool.wait_ge(dve_drain, d[1]))
        normalise()

        def quarter(layer, q):
            t0 = first_tile[MLP[layer]]
            base_sq, base_own = squares[0], pool_n[0]
            for i in range(8):
                if layer == 0:
                    for r in range(2):
                        e = i * 2 + r
                        s, k = e // 8, e % 8
                        pool.wait_ge(ada_used, 2 * ADA_STEPS + e - 1 + 16 * q)
                        pool.dma_start(ada_ring[:, e % 2, :], ada_src(2 + s, q, k))\
                            .then_inc(ada_l1[e % 2], 16)
                if i >= 4:
                    for r in range(2):
                        k = (i - 4) * 2 + r
                        pool.wait_ge(dve_drain, drains[t0 + 8 + k][1] + 8 * q)
                        pool.wait_ge(sumsq_ready, base_sq + k + 8 * q)
                        if k == 0:
                            ins = pool.tensor_tensor(sumsq[:, :], xT[:, k, :], xT[:, k, :], ALU.mult)
                        else:
                            pool.tensor_tensor(work[3][:, 0:L], xT[:, k, :], xT[:, k, :], ALU.mult)\
                                .then_inc(pool_own, 1)
                            pool.wait_ge(pool_own, base_own + k + 7 * q)
                            ins = pool.tensor_tensor(sumsq[:, :], sumsq[:, :], work[3][:, 0:L], ALU.add)
                        ins.then_inc(sumsq_ready, 1)

        def mlp(layer):
            with pool.Fori(0, QUARTERS) as q:
                quarter(layer, q)
            squares[0] += 8 * QUARTERS
            pool_n[0] += 7 * QUARTERS

        mlp(0)
        pool.wait_ge(tile_done, first_tile[CD_IN])
        own(pool.memset(tri[:, :], 1.0))
        own(pool.iota(dist[:, :].bitcast(I32), pattern=[[-1, L]], base=L - P, channel_multiplier=1))
        settle()
        own(pool.affine_select(out=tri[:, :], in_=tri[:, :], compare_op=ALU.is_ge, fill=0.0,
                               base=0, pattern=[[-1, P]], channel_multiplier=1))
        settle()
        pool.tensor_copy(dist[:, :], dist[:, :].bitcast(I32)).then_inc(l1_consts, 1)
        normalise()

        def keep_causal(buf, signal):
            for j in range(NB):
                v = buf[:, z_at[j]:z_at[j] + P]
                ins = pool.affine_select(out=v, in_=v, compare_op=ALU.is_gt, fill=0.0, base=0,
                                         pattern=[[1, P]], channel_multiplier=-1)
                ins.then_inc(signal, 1)

        for step in range(H + 1):
            if step < H:
                pool.wait_ge(sp_diag, step + 1)
                keep_causal(sp_sb[step % 2], sp_ready)
            if step >= 1:
                pool.wait_ge(w_exp, step)
                keep_causal(z_sb[(step - 1) % 2], w_ready)

        for k in range(KC):
            d = drains[first_tile[CD_OUT] + k]
            square_tile(k, lambda: pool.wait_ge(dve_drain, d[1]))
        normalise()
        mlp(1)

    @block.scalar
    def _(act):
        def own(ins):
            act_n[0] += 1
            ins.then_inc(act_own, 1)

        def settle():
            act.wait_ge(act_own, act_n[0])

        def rows(v):
            return v.rearrange("(r c) -> r c", c=P)

        act.dma_start(raw_a[0:32, :], norm_g.rearrange("l s (r c) -> (l s r) c", c=P)).then_inc(small_in, 16)
        act.dma_start(raw_a[32:P, :], ada_b.rearrange("l s (r c) -> (l s r) c", c=P)).then_inc(small_in, 16)
        act.dma_start(raw_b[0:8, :], rows(c[0])).then_inc(small_in, 16)
        act.dma_start(raw_b[8:16, :], rows(final_g)).then_inc(small_in, 16)
        act.dma_start(raw_b[16:20, :], rows(pool_scale[0])).then_inc(small_in, 16)
        act.dma_start(raw_b[20:24, :], rows(glu_b[0])).then_inc(small_in, 16)
        act.dma_start(raw_b[24:40, :], ssm_lam_re[0].rearrange("(t g) p -> t (g p)", g=2)).then_inc(small_in, 16)
        act.dma_start(raw_b[40:56, :], ssm_lam_im[0].rearrange("(t g) p -> t (g p)", g=2)).then_inc(small_in, 16)
        act.dma_start(raw_dt2[:, :], ssm_log_dt[0].rearrange("(t g) -> t g", g=2)).then_inc(dt_in, 16)
        for ri, src in enumerate((ssm_c_re, ssm_c_im)):
            for half in range(2):
                for t in range(8):
                    g0 = (half * 8 + t) * 2
                    act.dma_start(
                        c_nat[t * C:(t + 1) * C, ri * 2 + half, :].rearrange("c (g p) -> c g p", g=2),
                        src[0, g0:g0 + 2].rearrange("g c p -> c g p")).then_inc(small_in, 16)
        for ri, src in enumerate((ssm_b_re, ssm_b_im)):
            act.dma_start(bb[ri][:, :, :], src[0].rearrange("(t g) p c -> (g p) t c", g=2)).then_inc(b_in, 16)
        act.dma_start(skip[:, :], ssm_d[0].rearrange("(g c) -> c g", c=C),
                      allow_slow_non_contiguous=True).then_inc(d_in, 16)
        act.dma_start(pool_w_t[:, :, :], pool_w[0].rearrange("g c d -> c g d")).then_inc(poolw_in, 16)

        def prep(n, q=None):
            m, over = n, 0
            if q is not None:
                over = q
            act.wait_ge(raw_in[n % 2], landed[n] + 64 * over)
            if n >= 2:
                act.wait_ge(tile_done, first_tile[n - 1] + 16 * over)
            w = 2 * HD + 8 if n == KI else SLOT
            act.activation(w_hi[n % 2][:, :, 0:w], raw[n % 2][:, :, 0:w], ACT.Copy).then_inc(hi_ready, 1)

        for k in range(KC):
            act.wait_ge(xT_ps, k + 1)
            act.activation(xT[:, k, :], bank[k % 4], ACT.Copy).then_inc(x_ready, 1)

        act.wait_ge(params, 1)
        act.activation(sm[:, 0, :], pb[:, 56:72], ACT.Exp).then_inc(setup_act, 1)
        act.wait_ge(setup_dve, 1)
        act.activation(sm[:, 4, :], sm[:, 1, :], ACT.Exp).then_inc(setup_act, 1)
        act.activation(sm[:, 5, :], sm[:, 1, :], ACT.Exp, scale=float(RUN)).then_inc(setup_act, 1)
        act.activation(sm[:, 6, :], sm[:, 3, :], ACT.Sin).then_inc(setup_act, 1)
        act.activation(sm[:, 7, :], sm[:, 3, :], ACT.Sin, scale=0.5).then_inc(setup_act, 1)

        prep(0)
        norms = [0]

        def norm_rstd():
            norms[0] += 1
            act.wait_ge(norm_sum, norms[0])
            own(act.activation(rstd[:, :], bank[6], ACT.Ln, scale=1.0 / D, bias=eps_t[:, 0:1]))
            settle()
            act.activation(rstd[:, :], rstd[:, :], ACT.Exp, scale=-0.5).then_inc(rstd_ready, 1)

        def modulate(a):
            act.wait_ge(mods_ready, a + 1)
            for k in range(KC):
                act.wait_ge(xn_ready, 8 * a + k + 1)
                act.activation(h_hi[:, k, :], work[k % 2][:, 0:L], ACT.Identity,
                               scale=mods[:, a, 8 + k:9 + k], bias=mods[:, a, k:k + 1]).then_inc(hh_ready, 1)

        for i in range(8):
            act.wait_ge(mats_ps, i + 1)
            dst = (e_re, e_im)[i // 4][:, (i % 4) * 4:(i % 4) * 4 + 4, :]
            act.activation(dst.rearrange("p t n -> p (t n)"), bank[4 + i % 2], ACT.Copy).then_inc(mats_out, 1)
        norm_rstd()
        for i in range(8, 16):
            act.wait_ge(mats_ps, i + 1)
            t = (i - 8) // 2 * 4
            dst = kr[:, :, :].rearrange("p (t g) n -> p g t n", g=2)[:, i % 2, t:t + 4, :]
            act.activation(dst, bank[4 + i % 2][0:C, :].rearrange("p (t n) -> p t n", n=P), ACT.Copy)\
               .then_inc(mats_out, 1)
        act.wait_ge(toep_in, 16 * RUN)
        modulate(0)

        def copy_tile(t, dst, src=None, **kw):
            act.wait_ge(tile_done, t + 1)
            act.activation(dst, bank[t % 4] if src is None else src, ACT.Copy, **kw).then_inc(act_drain, 1)

        for n in range(AB_IN, GLU):
            prep(n + 1)
            for r in range(2):
                t = first_tile[n] + r
                if n < AB_IN + 2:
                    ct = 2 * (n - AB_IN) + r
                    copy_tile(t, ub[:, ct, :, :], bank[t % 4].rearrange("p (k j) -> p j k", j=RUN))
                    act.wait_ge(act_drain, drains[t][1])
                    act.dma_start(u_dram[ct * P:(ct + 1) * P, :],
                                  ub[:, ct, :, :].rearrange("p j k -> p (j k)")).then_inc(u_out, 16)
                else:
                    copy_tile(t, ua[:, 2 * (n - AB_IN - 2) + r, PAD:])
        for b in range(4):
            act.wait_ge(y_ps, b + 1)
            dst = y_run[:, :, :].rearrange("p (t g) k -> p g t k", g=2)[:, b % 2, b // 2 * 8:b // 2 * 8 + 8, :]
            act.activation(dst, bank[b].rearrange("p (t k) -> p t k", k=NRUN), ACT.Copy)\
               .then_inc(y_copied, 1)
        for g in range(4):
            act.wait_ge(pool_ps, g + 1)
            act.activation(h_hi[:, g, :], bank[4 + g], ACT.Identity, scale=pb[:, 16 + g:17 + g])\
               .then_inc(cat_hi, 1)
        act.wait_ge(y_in, 16 * 4)
        for ct in range(4):
            own(act.activation(y_act[:, ct, :], y_t[:, ct, :], ACT.Gelu_apprx_tanh))
            settle()
            act.activation(yg_hi[:, ct, :], y_act[:, ct, :], ACT.Copy).then_inc(gelu_hi, 1)
        prep(AB_OUT)
        for m in range(4):
            t = first_tile[GLU] + m
            act.wait_ge(tile_done, t + 1)
            act.activation(gate_t[:, m, :], bank[t % 4], ACT.Sigmoid, bias=pb[:, 20 + m:21 + m])\
               .then_inc(act_drain, 1)
        for m in range(4):
            act.wait_ge(cat_mid, m + 1)
            act.activation(h_hi[:, 4 + m, :], cat_f[:, m, :], ACT.Copy).then_inc(cat_hi, 1)
        for n in range(AB_OUT, MLP[0]):
            prep(n + 1)
        norm_rstd()
        modulate(1)

        def quarter(layer, q, last=False):
            n0, t0 = MLP[layer], first_tile[MLP[layer]]
            a0 = 32 * layer
            for i in range(8):
                if not (last and i == 7):
                    prep(n0 + i + 1, q)
                if i < 4:
                    for r in range(2):
                        t = 2 * i + r
                        act.wait_ge(tile_done, t0 + t + 1 + 16 * q)
                        if t >= 2:
                            act.wait_ge(a_ready, a0 + t - 1 + 8 * q)
                        act.activation(work[t % 2][:, 0:L], bank[(t0 + t) % 4], ACT.Relu)\
                           .then_inc(act_drain, 1)
                        act.wait_ge(act_drain, drains[t0 + t][1] + 8 * q)
                        act.activation(a_hi[:, t, :], work[t % 2][:, 0:L], ACT.Square)\
                           .then_inc(square_done, 1)

        with act.Fori(0, QUARTERS) as q:
            quarter(0, q)

        norm_rstd()
        modulate(2)

        def index_relu():
            cnt = 0
            for i in range(1, NB):
                for h in range(8):
                    act.wait_ge(idx_ps, cnt + 1)
                    if cnt >= 2:
                        act.wait_ge(idx_acc, cnt - 1)
                    act.activation(work[cnt % 2][:, 0:(i + 1) * P], bank[4 + cnt % 4][:, 0:(i + 1) * P],
                                   ACT.Relu).then_inc(idx_rel, 1)
                    cnt += 1

        for j, (name, half) in enumerate(cd_slots):
            n = CD_IN + j
            prep(n + 1)
            t0 = first_tile[n]
            if name == "ki":
                copy_tile(t0, ki_t[:, :])
                copy_tile(t0 + 1, wi_t[:, :, :].rearrange("p b h -> p (b h)"),
                          bank[(t0 + 1) % 4][:, 0:NB * 8], scale=IDX_SCALE)
            elif name in ("vd", "vc"):
                for b in range(NB):
                    copy_tile(t0 + b, qk[name][:, b, half * SLOT:(half + 1) * SLOT],
                              bank[(t0 + b) % 4][:, 0:SLOT])
            else:
                dst = qi_t if name == "qi" else qk[name]
                for r in range(2):
                    copy_tile(t0 + r, dst[:, 2 * half + r, :], scale=HD ** -0.5 if name in ("qd", "qc") else 1.0)
            if j == cd_slots.index(("qd", 0)):
                index_relu()

        cats = [8]

        def out_hi(tile, b, waits, value):
            act.wait_ge(waits, value)
            act.activation(h_hi[:, tile, :], bank[b], ACT.Copy).then_inc(cat_hi, 1)

        act.wait_ge(tile_done, first_tile[CD_OUT])
        for step in range(H + 1):
            if step < H:
                z, s_ = z_sb[step % 2], sp_sb[step % 2]
                if step == 0:
                    act.wait_ge(dsel_ready, 1)
                if step >= 2:
                    act.wait_ge(o_ps, step - 1)
                for j in range(NB):
                    act.wait_ge(z_ps, NB * step + j + 1)
                    act.activation(z[:, z_at[j]:z_at[j] + (NB - j) * P], bank[j % 2][:, 0:(NB - j) * P],
                                   ACT.Copy).then_inc(z_copied, 1)
                for i in range(NB):
                    act.wait_ge(max_ready, NB * step + i + 1)
                    act.activation(work[i][:, 0:(i + 1) * P], work[i][:, 0:(i + 1) * P], ACT.Exp,
                                   bias=small[:, i:i + 1],
                                   accum_out=small[:, 8 + i:9 + i]).then_inc(p_exp, 1)
            if step >= 1:
                z = z_sb[(step - 1) % 2]
                act.wait_ge(r_used, NB * step)
                act.activation(z[:, :], z[:, :], ACT.Exp).then_inc(w_exp, 1)
            if step < H:
                s_ = sp_sb[step % 2]
                act.wait_ge(z_abs, step + 1)
                own(act.activation(s_[:, :], s_[:, :], ACT.Exp, scale=-1.0))
                settle()
                act.activation(s_[:, :], s_[:, :], ACT.Ln, bias=eps_t[:, 1:2]).then_inc(z_soft, 1)
                for i in range(NB):
                    act.wait_ge(t_ps, NB * step + i + 1)
                    if i == 0 and step >= 1:
                        act.wait_ge(oc_ps, step)
                    act.activation(pT[:, 0:i + 1, i * P:(i + 1) * P],
                                   bank[5][:, 0:(i + 1) * P].rearrange("p (j q) -> p j q", q=P),
                                   ACT.Copy).then_inc(t_copied, 1)
            if step >= 1 and (step - 1) % 2 == 1:
                out_hi(4 + (step - 1) // 2, 6, o_ps, step)
            if step < H and step % 2 == 1:
                out_hi(step // 2, 7, oc_ps, step + 1)
        for n in range(CD_OUT, MLP[1]):
            prep(n + 1)
        norm_rstd()
        modulate(3)
        with act.Fori(0, QUARTERS - 1) as q:
            quarter(1, q)
        quarter(1, QUARTERS - 1, last=True)
        norm_rstd()
        for k in range(KC):
            act.wait_ge(fin_ps, k + 1)
            act.activation(y_out[:, :, k * P:(k + 1) * P], bank[k % 4].rearrange("p (t n) -> p t n", n=P),
                           ACT.Copy).then_inc(fin_copied, 1)

    @block.vector
    def _(dve):
        def own(ins):
            dve_n[0] += 1
            ins.then_inc(dve_own, 1)

        def settle():
            dve.wait_ge(dve_own, dve_n[0])

        def tt(o, a, b, op):
            own(dve.tensor_tensor(o, a, b, op))
            settle()

        def ts(o, a, s1, s2, op0, op1=ALU.bypass):
            own(dve.tensor_scalar(o, a, s1, s2, op0, op1))
            settle()

        def stt(o, a, s1, b, op0, op1):
            own(dve.scalar_tensor_tensor(out=o, in0=a, scalar=s1, in1=b, op0=op0, op1=op1))
            settle()

        own(dve.memset(eps_t[:, 0:1], EPS))
        own(dve.memset(eps_t[:, 1:2], 1.0))
        dve.wait_ge(consts, 2)
        own(dve.reciprocal(recip[:, :], recip[:, :]))
        dve.wait_ge(dt_in, 16)
        dve.tensor_copy(raw_dt[:, :].rearrange("t (g p) -> t g p", g=2),
                        raw_dt2[:, :].unsqueeze(2).to_broadcast([GT, 2, S])).then_inc(dt_rows, 1)
        dve.wait_ge(params_ps, 1)
        own(dve.tensor_copy(pa[:, :], bank[4][:, 0:P]))
        own(dve.tensor_copy(cb[0][:, :, :].rearrange("p t c -> p (t c)"), bank[5][:, 0:256]))
        own(dve.tensor_copy(cb[1][:, :, :].rearrange("p t c -> p (t c)"), bank[5][:, 256:512]))
        own(dve.tensor_copy(pb[:, :], bank[4][:, P:P + 72]))
        settle()
        dve.sem_inc(params, 1)

        DT, LRDT, TH, RED, MAG, MAG8, SIN, SINH, COS, AR, AI, DEN, RD, X1, X2, ZR, ZI, K_, CU, SU, \
            RC, RS = (0, 1, 2, 3, 4, 5, 6, 7, 8, 9, 10, 11, 12, 13, 14, 15, 16, 17, 18, 19, 20, 21)

        def v(i):
            return sm[:, i, :]

        lr, li = pb[:, 24:40], pb[:, 40:56]
        M, A, SB = ALU.mult, ALU.add, ALU.subtract
        dve.wait_ge(setup_act, 1)
        tt(v(LRDT), lr, v(DT), M)
        tt(v(TH), li, v(DT), M)
        magic = 1.5 * 2.0 ** 23
        c1 = 6.28125
        c2 = 0.0019350051879882812
        c3 = 2 * math.pi - c1 - c2
        ts(v(K_), v(TH), 1.0 / (2 * math.pi), None, M)
        ts(v(K_), v(K_), magic, None, A)
        ts(v(K_), v(K_), -magic, None, A)
        stt(v(RED), v(K_), -c1, v(TH), M, A)
        stt(v(RED), v(K_), -c2, v(RED), M, A)
        stt(v(RED), v(K_), -c3, v(RED), M, A)
        dve.tensor_scalar(v(RED), v(RED), 3.1415925, -3.1415925, ALU.min, ALU.max).then_inc(setup_dve, 1)
        dve.wait_ge(setup_act, 5)
        tt(v(COS), v(SINH), v(SINH), M)
        ts(v(COS), v(COS), -2.0, 1.0, M, A)
        tt(v(AR), v(MAG), v(COS), M)
        tt(v(AI), v(MAG), v(SIN), M)
        tt(v(X1), lr, lr, M)
        tt(v(X2), li, li, M)
        tt(v(DEN), v(X1), v(X2), A)
        own(dve.reciprocal(v(RD), v(DEN)))
        ts(v(X1), v(AR), -1.0, None, A)
        tt(v(ZR), v(X1), lr, M)
        tt(v(X2), v(AI), li, M)
        tt(v(ZR), v(ZR), v(X2), A)
        tt(v(ZR), v(ZR), v(RD), M)
        tt(v(ZI), v(AI), lr, M)
        tt(v(X2), v(X1), li, M)
        tt(v(ZI), v(ZI), v(X2), SB)
        tt(v(ZI), v(ZI), v(RD), M)
        own(dve.memset(pw_re[:, :, 0:1], 1.0))
        own(dve.memset(pw_im[:, :, 0:1], 0.0))
        own(dve.tensor_copy(pw_re[:, :, 1:2], v(AR).unsqueeze(2)))
        own(dve.tensor_copy(pw_im[:, :, 1:2], v(AI).unsqueeze(2)))
        settle()
        t1 = work[2][:, 0:GT * 4].rearrange("p (t m) -> p t m", t=GT)
        t2 = work[2][:, GT * 4:GT * 8].rearrange("p (t m) -> p t m", t=GT)
        for m in (1, 2, 4):
            ar = pw_re[:, :, m:m + 1].to_broadcast([P, GT, m])
            ai = pw_im[:, :, m:m + 1].to_broadcast([P, GT, m])
            pr, pi = pw_re[:, :, 1:m + 1], pw_im[:, :, 1:m + 1]
            nr, ni = pw_re[:, :, m + 1:2 * m + 1], pw_im[:, :, m + 1:2 * m + 1]
            tt(t1[:, :, 0:m], pr, ar, M)
            tt(t2[:, :, 0:m], pi, ai, M)
            tt(nr, t1[:, :, 0:m], t2[:, :, 0:m], SB)
            tt(t1[:, :, 0:m], pr, ai, M)
            tt(t2[:, :, 0:m], pi, ar, M)
            tt(ni, t1[:, :, 0:m], t2[:, :, 0:m], A)
        dve.sem_inc(powers, 1)

        ada_e = [0]

        def ada_step():
            e = ada_e[0]
            ada_e[0] += 1
            k = e % 8
            e1 = e - ADA_STEPS
            if e1 < 0:
                dve.wait_ge(ada_in[e % ADA_RING], 16 * (e // ADA_RING + 1))
            else:
                dve.wait_ge(ada_in_1[e % ADA_RING], 16 * (e1 // ADA_RING + 1))
            src = ada_ring[:, e % ADA_RING, :]
            if k == 0:
                ins = dve.tensor_scalar(ada_acc[:, :], src, pb[:, 0:1], None, M)
            else:
                dve.wait_ge(ada_used, e)
                ins = dve.scalar_tensor_tensor(out=ada_acc[:, :], in0=src, scalar=pb[:, k:k + 1],
                                               in1=ada_acc[:, :], op0=M, op1=A)
            ins.then_inc(ada_used, 1)

        def ada_collect(u):
            a, qt = u // 4, u % 4
            dve.wait_ge(ada_sum, u + 1)
            dve.tensor_tensor(mods[:, a, qt * 6:qt * 6 + 6], bank[7][:, 0:6],
                              pa[:, 32 + a * 24 + qt * 6:32 + a * 24 + qt * 6 + 6], A)\
               .then_inc(mods_part, 1)

        def ada_finish(a, parts):
            dve.wait_ge(mods_part, parts)
            own(dve.scalar_tensor_tensor(out=mods[:, a, 8:16], in0=mods[:, a, 8:16], scalar=1.0,
                                         in1=pa[:, a * 8:a * 8 + 8], op0=A, op1=M))
            own(dve.tensor_scalar(mods[:, a, 16:24], mods[:, a, 16:24], 1.0, None, A))
            settle()
            dve.sem_inc(mods_ready, 1)

        for _ in range(8):
            ada_step()
        dve.wait_ge(b_in, 32)
        zr = v(ZR).unsqueeze(2).to_broadcast([P, GT, C])
        zi = v(ZI).unsqueeze(2).to_broadcast([P, GT, C])
        w3 = work[2][:, 0:GT * C].rearrange("p (t c) -> p t c", t=GT)
        tt(bz[0][:, :, :], bb[0][:, :, :], zr, M)
        tt(w3, bb[1][:, :, :], zi, M)
        tt(bz[0][:, :, :], bz[0][:, :, :], w3, SB)
        tt(bz[1][:, :, :], bb[1][:, :, :], zr, M)
        tt(w3, bb[0][:, :, :], zi, M)
        tt(bz[1][:, :, :], bz[1][:, :, :], w3, A)
        ada_collect(0)

        def fb(b):
            return b[:, :, :].unsqueeze(2).to_broadcast([P, GT, RUN, C])

        def fp(p):
            return p[:, :, 0:RUN].unsqueeze(3).to_broadcast([P, GT, RUN, C])

        ftmp = f_tmp[:, :, :, :]
        tt(f_re[:, :, :, :], fb(bz[0]), fp(pw_re), M)
        tt(ftmp, fb(bz[1]), fp(pw_im), M)
        tt(f_re[:, :, :, :], f_re[:, :, :, :], ftmp, SB)
        tt(f_im[:, :, :, :], fb(bz[1]), fp(pw_re), M)
        tt(ftmp, fb(bz[0]), fp(pw_im), M)
        dve.tensor_tensor(f_im[:, :, :, :], f_im[:, :, :, :], ftmp, A).then_inc(f_ready, 1)
        for u in range(1, 4):
            for _ in range(8):
                ada_step()
            ada_collect(u)
        ada_finish(0, 4)

        def prep(n, q=None):
            dve.wait_ge(hi_ready, n + 1 + (0 if q is None else 8 * q))
            w = 2 * HD + 8 if n == KI else SLOT
            dve.tensor_tensor(w_lo[n % 2][:, :, 0:w], raw[n % 2][:, :, 0:w],
                              w_hi[n % 2][:, :, 0:w].bitcast(F32), SB).then_inc(lo_ready, 1)

        prep(0)
        dve.wait_ge(mats_out, 16)
        dve.wait_ge(d_in, 16)
        tt(skip_d[:, :, :], skip[:, :].unsqueeze(2).to_broadcast([C, G, C]),
           ident[0:C, 0:C].unsqueeze(1).to_broadcast([C, G, C]), M)
        dve.tensor_tensor(kr[:, :, 0:C], kr[:, :, 0:C], skip_d[:, :, :], A).then_inc(kr_ready, 1)
        own(dve.memset(ua[:, :, 0:PAD], 0.0))
        settle()
        dve.sem_inc(ua_pad, 1)

        def modulate(a):
            for k in range(KC):
                dve.wait_ge(xn_ready, 8 * a + k + 1)
                own(dve.tensor_scalar(work[2 + k % 2][:, 0:L], work[k % 2][:, 0:L],
                                      mods[:, a, 8 + k:9 + k], mods[:, a, k:k + 1], M, A))
                settle()
                dve.wait_ge(hh_ready, 8 * a + k + 1)
                dve.tensor_tensor(h_lo[:, k, :], work[2 + k % 2][:, 0:L], h_hi[:, k, :].bitcast(F32), SB)\
                   .then_inc(h_ready, 1)

        modulate(0)
        prep(1)
        tt(v(X1), v(COS), v(COS), M)
        tt(v(X2), v(SIN), v(SIN), M)
        tt(v(CU), v(X1), v(X2), SB)
        tt(v(SU), v(COS), v(SIN), M)
        ts(v(SU), v(SU), 2.0, None, M)

        def double():
            tt(v(X1), v(CU), v(CU), M)
            tt(v(X2), v(SU), v(SU), M)
            tt(v(SU), v(CU), v(SU), M)
            ts(v(SU), v(SU), 2.0, None, M)
            tt(v(CU), v(X1), v(X2), SB)

        double()
        double()
        own(dve.tensor_copy(v(RC), v(MAG8)))
        keep = small
        dve.wait_ge(kr_ready, 1)
        own(dve.memset(rot_c[:, :, 0:1], 1.0))
        own(dve.memset(rot_s[:, :, 0:1], 0.0))
        own(dve.tensor_copy(keep[:, 16:32], v(MAG8)))
        settle()
        m = 1
        while m < NRUN:
            cu = v(CU).unsqueeze(2).to_broadcast([P, GT, m])
            su = v(SU).unsqueeze(2).to_broadcast([P, GT, m])
            x1 = work[2][:, 0:GT * m].rearrange("p (t m) -> p t m", t=GT)
            x2 = work[3][:, 0:GT * m].rearrange("p (t m) -> p t m", t=GT)
            tt(x1, rot_c[:, :, 0:m], cu, M)
            tt(x2, rot_s[:, :, 0:m], su, M)
            tt(rot_c[:, :, m:2 * m], x1, x2, SB)
            tt(x1, rot_c[:, :, 0:m], su, M)
            tt(x2, rot_s[:, :, 0:m], cu, M)
            tt(rot_s[:, :, m:2 * m], x1, x2, A)
            if 2 * m < NRUN:
                double()
            m *= 2
        dve.sem_inc(rot_ready, 1)
        prep(2)
        prep(3)
        prep(4)

        def flat(t):
            return t[:, :, :].rearrange("p t k -> p (t k)")

        xr, xi = psum[:, 4 * L:6 * L], psum[:, 6 * L:8 * L]
        dve.wait_ge(inj_ps, 1)
        tt(flat(s_re), xr, flat(rot_c), M)
        tt(flat(s_t1), xi, flat(rot_s), M)
        tt(flat(s_im), xi, flat(rot_c), M)
        tt(flat(s_t2), xr, flat(rot_s), M)
        tt(flat(s_re), flat(s_re), flat(s_t1), A)
        tt(flat(s_im), flat(s_im), flat(s_t2), SB)
        for s_ in (s_re, s_im):
            for t in range(GT):
                own(dve.tensor_tensor_scan(s_[:, t, :], keep[:, 16 + t:17 + t].to_broadcast([P, NRUN]),
                                           s_[:, t, :], 0.0, M, A))
        settle()
        dve.wait_ge(u_out, 64)
        own(dve.memset(b_re[:, :, 0:1], 0.0))
        own(dve.memset(b_im[:, :, 0:1], 0.0))
        tt(flat(s_t1), flat(s_re), flat(rot_c), M)
        tt(flat(s_t2), flat(s_im), flat(rot_s), M)
        tt(b_re[:, :, 1:], s_t1[:, :, 0:NRUN - 1], s_t2[:, :, 0:NRUN - 1], SB)
        tt(flat(s_t1), flat(s_re), flat(rot_s), M)
        tt(flat(s_t2), flat(s_im), flat(rot_c), M)
        dve.tensor_tensor(b_im[:, :, 1:], s_t1[:, :, 0:NRUN - 1], s_t2[:, :, 0:NRUN - 1], A)\
           .then_inc(states, 1)
        for g in range(4):
            dve.wait_ge(cat_hi, g + 1)
            dve.scalar_tensor_tensor(out=h_lo[:, g, :], in0=bank[4 + g], scalar=pb[:, 16 + g:17 + g],
                                     in1=h_hi[:, g, :].bitcast(F32), op0=M, op1=SB).then_inc(cat_ready, 1)
        for ct in range(4):
            dve.wait_ge(gelu_hi, ct + 1)
            dve.tensor_tensor(yg_lo[:, ct, :], y_act[:, ct, :], yg_hi[:, ct, :].bitcast(F32), SB)\
               .then_inc(gelu_lo, 1)
        prep(AB_OUT)
        for m in range(4):
            dve.wait_ge(act_drain, drains[first_tile[GLU] + m][1])
            dve.tensor_tensor(cat_f[:, m, :].rearrange("p (k j) -> p j k", j=RUN),
                              gate_t[:, m, :].rearrange("p (j k) -> p j k", j=RUN),
                              y_act[:, m, :].rearrange("p (j k) -> p j k", j=RUN), M).then_inc(cat_mid, 1)
        for m in range(4):
            dve.wait_ge(cat_hi, 4 + m + 1)
            dve.tensor_tensor(h_lo[:, 4 + m, :], cat_f[:, m, :], h_hi[:, 4 + m, :].bitcast(F32), SB)\
               .then_inc(cat_ready, 1)

        def residual(t, k, a, q=None):
            over = 0 if q is None else q
            dve.wait_ge(tile_done, t + 1 + 16 * over)
            dve.scalar_tensor_tensor(out=xT[:, k, :], in0=bank[t % 4], scalar=mods[:, a, 16 + k:17 + k],
                                     in1=xT[:, k, :], op0=M, op1=A).then_inc(dve_drain, 1)

        for i in range(4):
            n = AB_OUT + i
            prep(n + 1)
            for _ in range(8):
                ada_step()
            for r in range(2):
                residual(first_tile[n] + r, 2 * i + r, 0)
            ada_collect(4 + i)
        ada_finish(1, 8)
        modulate(1)

        def quarter(layer, q, last=False):
            n0, t0 = MLP[layer], first_tile[MLP[layer]]
            a0 = 32 * layer
            for i in range(8):
                if not (last and i == 7):
                    prep(n0 + i + 1, q)
                if layer == 0:
                    for r in range(2):
                        e = 2 * i + r
                        k = e % 8
                        dve.wait_ge(ada_l1[e % 2], 16 * (e // 2 + 1) + 128 * q)
                        src = ada_ring[:, e % 2, :]
                        if k == 0:
                            ins = dve.tensor_scalar(ada_acc[:, :], src, pb[:, 0:1], None, M)
                        else:
                            dve.wait_ge(ada_used, 2 * ADA_STEPS + e + 16 * q)
                            ins = dve.scalar_tensor_tensor(out=ada_acc[:, :], in0=src,
                                                           scalar=pb[:, k:k + 1], in1=ada_acc[:, :],
                                                           op0=M, op1=A)
                        ins.then_inc(ada_used, 1)
                for r in range(2):
                    t = 2 * i + r
                    if i < 4:
                        dve.wait_ge(act_drain, drains[t0 + t][1] + 8 * q)
                        if t >= 1:
                            dve.wait_ge(a_ready, a0 + t + 8 * q)
                        dve.tensor_tensor(work[2][:, 0:L], work[t % 2][:, 0:L], work[t % 2][:, 0:L], M)\
                           .then_inc(sq_ready, 1)
                        dve.wait_ge(sq_ready, a0 + t + 1 + 8 * q)
                        dve.wait_ge(square_done, a0 + t + 1 + 8 * q)
                        dve.tensor_tensor(a_lo[:, t, :], work[2][:, 0:L], a_hi[:, t, :].bitcast(F32), SB)\
                           .then_inc(a_ready, 1)
                    else:
                        if t == 8:
                            dve.wait_ge(sumsq_ready, (2 * KC if layer == 0 else 3 * KC + 8 * QUARTERS) + 8 * q)
                        residual(t0 + t, t - 8, 2 * layer + 1, q)
                if layer == 0 and i % 4 == 3:
                    s = i // 4
                    dve.wait_ge(ada_sum, 8 + s + 1 + 2 * q)
                    dve.tensor_tensor(mods[:, 2 + s, bass.ds(q * 6, 6)], bank[7][:, 0:6],
                                      pa[:, bass.ds(q * 6 + 32 + (2 + s) * 24, 6)], A).then_inc(mods_part, 1)

        with dve.Fori(0, QUARTERS) as q:
            quarter(0, q)
        ada_finish(2, 16)
        ada_finish(3, 16)
        modulate(2)

        top8 = small[:, 32:40]

        def block_score(i):
            return score[:, sc_at[i]:sc_at[i] + (i + 1) * P]

        def index_scores():
            cnt = 0
            for i in range(1, NB):
                for h in range(8):
                    dve.wait_ge(idx_rel, cnt + 1)
                    rel, w = work[cnt % 2][:, 0:(i + 1) * P], wi_t[:, i, h:h + 1]
                    if h == 0:
                        ins = dve.tensor_scalar(block_score(i), rel, w, None, M)
                    else:
                        dve.wait_ge(idx_acc, cnt)
                        ins = dve.scalar_tensor_tensor(out=block_score(i), in0=rel, scalar=w,
                                                       in1=block_score(i), op0=M, op1=A)
                    ins.then_inc(idx_acc, 1)
                    cnt += 1
                dve.wait_ge(idx_acc, cnt)
                own(dve.memset(block_score(i)[0:CHUNK, i * P + CHUNK:(i + 1) * P], UNSEEN))
            settle()

        rounds = [(i, r) for i in range(1, NB) for r in range(TOPK // 8)]

        def take_round(i):
            own(dve.max(out=top8, in_=block_score(i)))
            settle()
            own(dve.match_replace(out=block_score(i), in_to_replace=top8, in_values=block_score(i),
                                  imm_value=TAKEN))
            settle()

        def selected_distances():
            dve.wait_ge(l1_consts, 1)
            own(dve.scalar_tensor_tensor(out=dist[:, :], in0=dist[:, :], scalar=-1.0, in1=dist[:, :],
                                         op0=M, op1=ALU.max))
            settle()
            own(dve.tensor_copy(dsel[:, 0:P], dist[:, L - P:L]))
            settle()
            own(dve.memset(dsel[0:CHUNK, CHUNK:P], FAR))
            for i in range(1, NB):
                w = (i + 1) * P
                ts(block_score(i), block_score(i), TAKEN / 2, FAR, ALU.is_gt, M)
                off = L - P - i * P
                tt(dsel[:, sel_at[i]:sel_at[i] + w], block_score(i), dist[:, off:off + w], A)
            dve.sem_inc(dsel_ready, 1)

        for j, (name, half) in enumerate(cd_slots):
            n = CD_IN + j
            prep(n + 1)
            if j == cd_slots.index(("qd", 0)):
                index_scores()
            elif j > cd_slots.index(("qd", 0)):
                for _ in range(5):
                    if rounds:
                        take_round(rounds.pop(0)[0])
        assert not rounds
        selected_distances()

        def out_lo(tile, b, value):
            dve.wait_ge(cat_hi, value)
            dve.tensor_tensor(h_lo[:, tile, :], bank[b], h_hi[:, tile, :].bitcast(F32), SB)\
               .then_inc(cat_ready, 1)

        cats = [8]
        for step in range(H + 1):
            if step < H:
                for i in range(NB):
                    w = (i + 1) * P
                    dve.wait_ge(s_ps, NB * step + i + 1)
                    if step >= 1:
                        dve.wait_ge(t_ps, NB * (step - 1) + i + 1)
                    dve.scalar_tensor_tensor(out=work[i][:, 0:w], in0=dsel[:, sel_at[i]:sel_at[i] + w],
                                             scalar=-SLOPES[step], in1=bank[4][:, 0:w],
                                             op0=M, op1=A).then_inc(s_used, 1)
                    dve.wait_ge(s_used, NB * step + i + 1)
                    dve.reduce_max(small[:, i:i + 1], work[i][:, 0:w], AX_X, negate=True)\
                       .then_inc(max_ready, 1)
            if step >= 1:
                z = z_sb[(step - 1) % 2]
                for c_, j in enumerate(reversed(range(NB))):
                    dve.wait_ge(r_ps, NB * (step - 1) + c_ + 1)
                    v_ = z[:, z_at[j]:z_at[j] + (NB - j) * P]
                    dve.tensor_tensor(v_, v_, bank[2 + c_ % 2][:, 0:(NB - j) * P], SB).then_inc(r_used, 1)
            if step < H:
                z, s_ = z_sb[step % 2], sp_sb[step % 2]
                dve.wait_ge(z_copied, NB * (step + 1))
                dve.scalar_tensor_tensor(out=s_[:, :], in0=z[:, :], scalar=-1.0, in1=z[:, :],
                                         op0=M, op1=ALU.max).then_inc(z_abs, 1)
                for i in range(NB):
                    w = (i + 1) * P
                    dve.wait_ge(p_exp, NB * step + i + 1)
                    own(dve.reciprocal(small[:, 12 + i:13 + i], small[:, 8 + i:9 + i]))
                    settle()
                    dve.tensor_scalar(work[i][:, 0:w], work[i][:, 0:w], small[:, 12 + i:13 + i], None, M)\
                       .then_inc(p_ready, 1)
                dve.wait_ge(z_soft, step + 1)
                dve.scalar_tensor_tensor(out=s_[:, :], in0=z[:, :], scalar=0.0, in1=s_[:, :],
                                         op0=ALU.max, op1=A).then_inc(sp_diag, 1)
            if step >= 1 and (step - 1) % 2 == 1:
                cats[0] += 1
                out_lo(4 + (step - 1) // 2, 6, cats[0])
            if step < H and step % 2 == 1:
                cats[0] += 1
                out_lo(step // 2, 7, cats[0])

        for i in range(4):
            n = CD_OUT + i
            prep(n + 1)
            for r in range(2):
                residual(first_tile[n] + r, 2 * i + r, 2)
        modulate(3)
        with dve.Fori(0, QUARTERS - 1) as q:
            quarter(1, q)
        quarter(1, QUARTERS - 1, last=True)
        dve.wait_ge(rstd_ready, 5)
        for k in range(KC):
            if k >= 4:
                dve.wait_ge(fin_ps, k - 3)
            dve.scalar_tensor_tensor(out=work[k % 4][:, 0:L], in0=xT[:, k, :], scalar=pb[:, 8 + k:9 + k],
                                     in1=rstd[:, :], op0=M, op1=M).then_inc(fin_t, 1)

    @block.tensor
    def _(pe):
        def mm(o, lhsT, rhs, start, stop, **kw):
            return nc.tensor.matmul(o, lhsT, rhs, start=start, stop=stop, **kw)

        def transpose(o, in_):
            n = in_.shape[0]
            return nc.tensor.transpose(o, in_, ident[0:n, 0:n])

        def product(o, w, x_, first, last):
            (w_h, w_l), (x_h, x_l) = w, x_
            mm(o, w_h, x_h, first, False)
            mm(o, w_h, x_l, False, False)
            return mm(o, w_l, x_h, False, last)

        pe.wait_ge(small_in, 16 * (8 + 32))
        pe.wait_ge(consts, 2)
        transpose(bank[4][:, 0:P], raw_a[:, :])
        transpose(bank[4][:, P:P + 56], raw_b[:, :])
        pe.wait_ge(dt_rows, 1)
        transpose(bank[4][:, P + 56:P + 72], raw_dt[:, :])
        for i in range(4):
            last = transpose(bank[5][:, i * P:(i + 1) * P], c_nat[:, i, :])
        last.then_inc(params_ps, 1)
        pe.wait_ge(x_in, 16)
        for k in range(KC):
            if k >= 4:
                pe.wait_ge(x_ready, k - 3)
            for b in range(NB):
                last = transpose(bank[k % 4][:, b * P:(b + 1) * P], x_nat[:, b, k * P:(k + 1) * P])
            last.then_inc(xT_ps, 1)

        def ada_sums(value, unit, q=None):
            if q is not None or unit > 0:
                pe.wait_ge(mods_part, unit)
            pe.wait_ge(ada_used, value)
            for j in range(6):
                last = mm(bank[7][:, j:j + 1], ada_acc[:, j * P:(j + 1) * P], ones[:, 0:1], True, True)
            last.then_inc(ada_sum, 1)

        norms = [0]

        def norm(value):
            pe.wait_ge(sumsq_ready, value)
            if norms[0]:
                pe.wait_ge(rstd_ready, norms[0])
            mm(bank[6], ones[:, :], sumsq[:, :], True, True).then_inc(norm_sum, 1)
            norms[0] += 1

        ada_sums(8, 0)
        norm(KC)
        pe.wait_ge(f_ready, 1)
        for i in range(8):
            if i >= 2:
                pe.wait_ge(mats_out, i - 1)
            f = (f_re, f_im)[i // 4]
            for r in range(4):
                t = (i % 4) * 4 + r
                last = transpose(bank[4 + i % 2][:, r * P:(r + 1) * P],
                                 f[:, t, :, :].rearrange("p m c -> p (m c)"))
            last.then_inc(mats_ps, 1)
        for u in range(1, 4):
            ada_sums(8 * (u + 1), u)
        pe.wait_ge(g_ready, 1)
        for i in range(8, 16):
            pe.wait_ge(mats_out, i - 1)
            p0 = S * (i % 2)
            for r in range(4):
                t = (i - 8) // 2 * 4 + r
                o = bank[4 + i % 2][0:C, r * P:(r + 1) * P]
                for n_, (b_, g_) in enumerate(((bz[0], g_re), (bz[1], g_ni))):
                    last = mm(o, b_[p0:p0 + S, t, :],
                              g_[p0:p0 + S, t, 0:RUN, :].rearrange("p m c -> p (m c)"), n_ == 0, n_ == 1)
            last.then_inc(mats_ps, 1)

        def slot_ready(n, q=None):
            pe.wait_ge(lo_ready, n + 1 + (0 if q is None else 8 * q))

        def tile_free(t, q=None):
            if t >= 4:
                by_dve, count = drains[t - 4]
                pe.wait_ge(dve_drain if by_dve else act_drain, count + (0 if q is None else 8 * q))

        def weight(n, k, c0, w=P):
            return w_hi[n % 2][:, k, c0:c0 + w], w_lo[n % 2][:, k, c0:c0 + w]

        def h(k, c0=0, w=L):
            return h_hi[:, k, c0:c0 + w], h_lo[:, k, c0:c0 + w]

        def tile(n, t, r, ready, base, q=None, moving=h, first=False):
            tile_free(t, q)
            for k in range(8):
                if first:
                    pe.wait_ge(ready, base + k + 1)
                last = product(bank[t % 4], weight(n, k, r * P), moving(k), k == 0, k == 7)
            last.then_inc(tile_done, 1)

        def plain_slots(n0, count, ready, base):
            for n in range(n0, n0 + count):
                slot_ready(n)
                for r in range(2):
                    tile(n, first_tile[n] + r, r, ready, base, first=n == n0 and r == 0)

        plain_slots(AB_IN, 4, h_ready, 0)

        pe.wait_ge(u_in, 16 * RUN)
        pe.wait_ge(mods_part, 4)
        for g in range(G):
            t, p0 = g // 2, S * (g % 2)
            for e_, b0 in ((e_re, 4), (e_im, 6)):
                o = bank[b0 + t // 8][p0:p0 + S, (t % 8) * NRUN:(t % 8 + 1) * NRUN]
                last = mm(o, e_[:, t, p0:p0 + S], u_run[:, g, :], True, True)
        last.then_inc(inj_ps, 1)
        pe.wait_ge(toep_in, 16 * RUN)
        pe.wait_ge(act_drain, drains[first_tile[GLU] - 1][1])

        def y_at(g):
            t = g // 2
            return bank[g % 2 + t // 8 * 2][:, (t % 8) * NRUN:(t % 8 + 1) * NRUN]

        for g in range(G):
            mm(y_at(g), toep[:, g, :], u_run[:, g, :], g % 16 < 2, False, skip_group_check=True)
        pe.wait_ge(states, 1)
        for g in range(G):
            t, p0 = g // 2, S * (g % 2)
            for g_, b_ in ((g_re, b_re), (g_ni, b_im)):
                last = mm(y_at(g), g_[p0:p0 + S, t, 1:, :].rearrange("p m c -> p (m c)"),
                          b_[p0:p0 + S, t, :], False, g_ is g_ni and g % 16 >= 14, skip_group_check=True)
            if g % 16 >= 14:
                last.then_inc(y_ps, 1)
        pe.wait_ge(poolw_in, 16)
        for g in range(4):
            pe.wait_ge(pooled, g + 1)
            mm(bank[4 + g], pool_w_t[:, g, :], ua[:, g, PAD:], True, True).then_inc(pool_ps, 1)
        slot_ready(GLU)
        pe.wait_ge(y_copied, 4)
        glu_h = w_hi[GLU % 2][:, :, :].rearrange("p a b -> p (a b)").rearrange("p (k n) -> p k n", k=4)
        glu_l = w_lo[GLU % 2][:, :, :].rearrange("p a b -> p (a b)").rearrange("p (k n) -> p k n", k=4)
        for m in range(4):
            t = first_tile[GLU] + m
            tile_free(t)
            for k in range(4):
                pe.wait_ge(gelu_lo, k + 1)
                last = product(bank[t % 4], (glu_h[:, k, m * P:(m + 1) * P], glu_l[:, k, m * P:(m + 1) * P]),
                               (yg_hi[:, k, :], yg_lo[:, k, :]), k == 0, k == 3)
            last.then_inc(tile_done, 1)
        pe.wait_ge(cat_ready, 4)
        for i in range(4):
            n = AB_OUT + i
            slot_ready(n)
            for r in range(2):
                tile(n, first_tile[n] + r, r, cat_ready, 0, first=i == 0 and r == 0)
            ada_sums(8 * (4 + i + 1), 4 + i)
        norm(2 * KC)

        def a(k):
            return a_hi[:, k, :], a_lo[:, k, :]

        def quarter(layer, q):
            n0, t0 = MLP[layer], first_tile[MLP[layer]]
            a0 = 32 * layer
            for i in range(8):
                slot_ready(n0 + i, q)
                for r in range(2):
                    t = 2 * i + r
                    tile_free(t0 + t, q)
                    for k in range(8):
                        if t == 0:
                            pe.wait_ge(h_ready, 8 * (2 * layer + 1) + k + 1)
                        if t == 8:
                            pe.wait_ge(a_ready, a0 + k + 1 + 8 * q)
                        last = product(bank[(t0 + t) % 4], weight(n0 + i, k, r * P),
                                       h(k) if i < 4 else a(k), k == 0, k == 7)
                    last.then_inc(tile_done, 1)
                if layer == 0 and i % 4 == 3:
                    ada_sums(2 * ADA_STEPS + 8 * (i // 4 + 1) + 16 * q, 8 + i // 4 + 2 * q, q)

        with pe.Fori(0, QUARTERS) as q:
            quarter(0, q)
        norm(2 * KC + 8 * QUARTERS)

        def index_products():
            pe.wait_ge(act_drain, drains[first_tile[KI] + 1][1])
            cnt = 0
            for i in range(1, NB):
                for hh in range(8):
                    if cnt >= 4:
                        pe.wait_ge(idx_rel, cnt - 3)
                    p0 = HD * (hh % 2)
                    mm(bank[4 + cnt % 4][:, 0:(i + 1) * P], qi_t[p0:p0 + HD, hh // 2, i * P:(i + 1) * P],
                       ki_t[p0:p0 + HD, 0:(i + 1) * P], True, True).then_inc(idx_ps, 1)
                    cnt += 1
            pe.wait_ge(idx_rel, cnt)

        for j, (name, half) in enumerate(cd_slots):
            n = CD_IN + j
            slot_ready(n)
            t0 = first_tile[n]
            if name == "ki":
                tile(n, t0, 0, h_ready, 16)
                tile_free(t0 + 1)
                for b in range(NB):
                    for k in range(8):
                        last = product(bank[(t0 + 1) % 4][:, b * 8:(b + 1) * 8], h(k, b * P, P),
                                       weight(n, k, P, 8), k == 0, k == 7)
                last.then_inc(tile_done, 1)
            elif name in ("vd", "vc"):
                for b in range(NB):
                    tile_free(t0 + b)
                    for k in range(8):
                        last = product(bank[(t0 + b) % 4][:, 0:SLOT], h(k, b * P, P),
                                       weight(n, k, 0, SLOT), k == 0, k == 7)
                    last.then_inc(tile_done, 1)
            else:
                for r in range(2):
                    tile(n, t0 + r, r, h_ready, 16, first=j == 0 and r == 0)
            if name == "qd" and half == 0:
                index_products()

        def stick_cat(pair):
            return 8 + 2 * pair + 2

        def dsa_cat(pair):
            return 8 + 2 * pair + 1

        qd, kd, vd, qc, kc, vc = (qk[x_] for x_ in ("qd", "kd", "vd", "qc", "kc", "vc"))
        pe.wait_ge(act_drain, drains[first_tile[CD_OUT] - 1][1])
        for step in range(H + 1):
            hh = step
            p0 = HD * (step % 2)
            if step < H:
                for i in range(NB):
                    if step or i:
                        pe.wait_ge(s_used, NB * step + i)
                    mm(bank[4][:, 0:(i + 1) * P], qc[p0:p0 + HD, hh // 2, i * P:(i + 1) * P],
                       kc[p0:p0 + HD, hh // 2, 0:(i + 1) * P], True, True).then_inc(s_ps, 1)
                for j in range(NB):
                    if step or j >= 2:
                        pe.wait_ge(z_copied, NB * step + j - 1)
                    mm(bank[j % 2][:, 0:(NB - j) * P], kd[p0:p0 + HD, hh // 2, j * P:(j + 1) * P],
                       qd[p0:p0 + HD, hh // 2, j * P:], True, True).then_inc(z_ps, 1)
            if step >= 1:
                pr = step - 1
                s_, z = sp_sb[pr % 2], z_sb[pr % 2]
                pe.wait_ge(sp_ready, NB * step)
                for c_, j in enumerate(reversed(range(NB))):
                    if pr or c_ >= 2:
                        pe.wait_ge(r_used, NB * pr + c_ - 1)
                    o = bank[2 + c_ % 2]
                    w = (NB - j) * P
                    last = mm(o[:, 0:w], tri[:, :], s_[:, z_at[j]:z_at[j] + w], True, j == NB - 1)
                    for j2 in range(j + 1, NB):
                        w2 = (NB - j2) * P
                        last = mm(o[:, w - w2:w], ones[:, :], s_[:, z_at[j2]:z_at[j2] + w2], False,
                                  j2 == NB - 1)
                    last.then_inc(r_ps, 1)
            if step < H:
                for i in range(NB):
                    pe.wait_ge(p_ready, NB * step + i + 1)
                    if step or i:
                        pe.wait_ge(t_copied, NB * step + i)
                    for j in range(i + 1):
                        last = transpose(bank[5][:, j * P:(j + 1) * P], work[i][:, j * P:(j + 1) * P])
                    last.then_inc(t_ps, 1)
            if step >= 1:
                pr = step - 1
                po = HD * (pr % 2)
                if pr >= 2 and pr % 2 == 0:
                    pe.wait_ge(cat_ready, stick_cat(pr // 2 - 1))
                pe.wait_ge(w_ready, NB * step)
                for j in range(NB):
                    last = mm(bank[6][po:po + HD, j * P:], vd[:, j, pr * HD:(pr + 1) * HD],
                              z_sb[pr % 2][:, z_at[j]:z_at[j] + (NB - j) * P], j == 0, j == NB - 1)
                last.then_inc(o_ps, 1)
            if step < H:
                if step >= 2 and step % 2 == 0:
                    pe.wait_ge(cat_ready, dsa_cat(step // 2 - 1))
                pe.wait_ge(t_copied, NB * (step + 1))
                for j in range(NB):
                    last = mm(bank[7][p0:p0 + HD, j * P:], vc[:, j, hh * HD:(hh + 1) * HD],
                              pT[:, j, j * P:], j == 0, j == NB - 1)
                last.then_inc(oc_ps, 1)
        pe.wait_ge(cat_ready, 16)
        plain_slots(CD_OUT, 4, cat_ready, 8)
        norm(3 * KC + 8 * QUARTERS)
        with pe.Fori(0, QUARTERS) as q:
            quarter(1, q)
        norm(3 * KC + 16 * QUARTERS)
        for k in range(KC):
            pe.wait_ge(fin_t, k + 1)
            if k >= 4:
                pe.wait_ge(fin_copied, k - 3)
            for b in range(NB):
                last = transpose(bank[k % 4][:, b * P:(b + 1) * P], work[k % 4][:, b * P:(b + 1) * P])
            last.then_inc(fin_ps, 1)

    block.__exit__(None, None, None)


INPUTS = ["x", "c", "norm_g", "ada_w", "ada_b", "mlp_w1", "mlp_w2", "ab_w_in", "ab_w_out", "pool_w",
          "pool_scale", "ssm_lam_re", "ssm_lam_im", "ssm_log_dt", "ssm_b_re", "ssm_b_im", "ssm_c_re",
          "ssm_c_im", "ssm_d", "glu_w", "glu_b", "cd_w_in", "cd_w_out", "final_g"]


def kernel(**inputs):
    import numpy as np
    import concourse.bacc as bacc
    from concourse.bass_utils import run_bass_kernel_spmd

    nc = bacc.Bacc("TRN2", target_bir_lowering=False, num_devices=1)
    arrays, args = {}, []
    for name in INPUTS:
        a = np.ascontiguousarray(inputs[name])
        arrays[f"in_{name}"] = a
        args.append(nc.dram_tensor(f"in_{name}", a.shape, mybir.dt.from_np(a.dtype),
                                   kind="ExternalInput").ap())
    out = nc.dram_tensor("out", (1, L, D), F32, kind="ExternalOutput")
    trunk(nc, *args, out.ap())
    r = run_bass_kernel_spmd(nc, [arrays], core_ids=[0])
    return r.results[0]["out"]
```

```python
import math

import concourse.bass as bass
from concourse import mybir

ALU = mybir.AluOpType
ACT = mybir.ActivationFunctionType
F32 = mybir.dt.float32
F32R = mybir.dt.float32r
I32 = mybir.dt.int32
AX_X = mybir.AxisListType.X

P = 128
D = 1024
L = 512
KC = D // P
NB = L // P
FF = 4 * D
SLOT = 256
QUARTERS = 4
QT = FF // QUARTERS // P
EPS = 1e-6
CHUNK = 64
HALF = D // 2

G, S, C = 32, 64, 16
RUN = P // C
NRUN = L // RUN
GT = G // 2
WINDOWS = (2, 4, 8, 16)
PAD = 16

H, HD = 8, 64
TOPK = 128
IDX_SCALE = (8 ** -0.5) * (64 ** -0.5)
SLOPES = [2.0 ** (-8.0 * (h + 1) / H) for h in range(H)]
UNSEEN = -1.0e30
TAKEN = -3.0e38
FAR = 1.0e30
ADA_Q = 3 * D // 4
ADA_RING = 3
ADA_FIRST = 10


def trunk(nc, x, c, norm_g, ada_w, ada_b, mlp_w1, mlp_w2, ab_w_in, ab_w_out, pool_w, pool_scale,
          ssm_lam_re, ssm_lam_im, ssm_log_dt, ssm_b_re, ssm_b_im, ssm_c_re, ssm_c_im, ssm_d,
          glu_w, glu_b, cd_w_in, cd_w_out, final_g, out):

    cursor = [(nc.sbuf_base + 63) // 64 * 64]

    def place(name, shape, dt=F32, offset=None):
        size = 4 * math.prod(shape[1:])
        if offset is None:
            offset = cursor[0]
            cursor[0] += (size + 31) // 32 * 32
        return nc.alloc_sbuf_tensor_at(name, shape, dt, offset=offset)

    xT = place("xT", [P, KC, L])
    h_at = cursor[0]
    h_hi = place("h_hi", [P, KC, L], F32R)
    h_lo = place("h_lo", [P, KC, L], F32R)
    raw = [place(f"w_raw{i}", [P, 8, SLOT]) for i in range(2)]
    w_at = cursor[0]
    w_hi = [place(f"w_hi{i}", [P, 8, SLOT], F32R) for i in range(2)]
    w_lo = [place(f"w_lo{i}", [P, 8, SLOT], F32R) for i in range(2)]
    ada_ring_at = cursor[0]
    ada_ring = place("ada_ring", [P, ADA_RING, ADA_Q])
    ada_acc = place("ada_acc", [P, ADA_Q])
    ident = place("ident", [P, P])
    ones = place("ones", [P, P])
    pa = place("pa", [P, P])
    pb = place("pb", [P, 72])
    mods = place("mods", [P, 4, 24])
    eps_t = place("eps_t", [P, 8])
    recip = place("recip", [P, PAD])
    small = place("small", [P, 64])
    wi_t = place("wi_t", [P, NB, 8])
    work = [place(f"work{i}", [P, L + PAD]) for i in range(4)]
    sumsq = place("sumsq", [P, L])
    rstd = place("rstd", [P, L])
    pool_w_t = place("pool_w_t", [P, 4, P])
    arena = cursor[0]

    def lay(at, name, shape, dt=F32):
        t = place(name, shape, dt, offset=at[0])
        at[0] += (4 * math.prod(shape[1:]) + 31) // 32 * 32
        return t

    ada_first = place("ada_first", [P, ADA_FIRST, ADA_Q], F32, offset=w_at)
    at = [h_at]
    x_nat = lay(at, "x_nat", [P, NB, D])
    kr = place("kr", [C, G, P], F32, offset=h_at)
    g_tmp = lay(at, "g_tmp", [P, GT, RUN + 1, C])
    raw_a = lay(at, "raw_a", [P, P])
    raw_c = lay(at, "raw_c", [KC, P])
    raw_b = lay(at, "raw_b", [48, P])
    raw_dt2 = lay(at, "raw_dt2", [GT, 2])
    raw_dt = lay(at, "raw_dt", [GT, P])
    c_nat = [lay(at, f"c_nat{i}", [P, 4, 2, S]) for i in range(2)]
    assert at[0] <= h_at + 2 * 4 * KC * L
    at = [arena]
    f_at = arena
    f_re = lay(at, "f_re", [P, GT, RUN, C])
    f_im = lay(at, "f_im", [P, GT, RUN, C])
    at[0] += 512
    g_re = lay(at, "g_re", [P, GT, RUN + 1, C])
    g_ni = lay(at, "g_ni", [P, GT, RUN + 1, C])
    toep = lay(at, "toep", [P, G, P])
    e_at = at[0]
    e_re = lay(at, "e_re", [P, GT, P])
    e_im = lay(at, "e_im", [P, GT, P])
    u_at = at[0]
    u_run = lay(at, "u_run", [P, G, NRUN])
    rot_c = lay(at, "rot_c", [P, GT, NRUN])
    rot_s = lay(at, "rot_s", [P, GT, NRUN])
    assert at[0] <= nc.sbuf_usable_end, (at[0], nc.sbuf_usable_end)
    at = [f_at]
    ub = lay(at, "ub", [P, 4, RUN, NRUN])
    ua = lay(at, "ua", [P, 4, L + PAD])
    at = [f_at]
    b_re = lay(at, "b_re", [P, GT, NRUN])
    b_im = lay(at, "b_im", [P, GT, NRUN])
    y_act = place("y_act", [P, 4, L], F32, offset=f_at)
    at = [e_at]
    s_re = lay(at, "s_re", [P, GT, NRUN])
    s_im = lay(at, "s_im", [P, GT, NRUN])
    s_t1 = lay(at, "s_t1", [P, GT, NRUN])
    s_t2 = lay(at, "s_t2", [P, GT, NRUN])
    sq_x = place("sq_x", [P, 4, L], F32, offset=e_at + 8192)
    f_tmp = place("f_tmp", [P, GT, RUN, C], F32, offset=e_at)
    y_run = place("y_run", [P, G, NRUN], F32, offset=e_at)
    at = [e_at]
    yg_hi = lay(at, "yg_hi", [P, 4, L], F32R)
    yg_lo = lay(at, "yg_lo", [P, 4, L], F32R)
    y_t = place("y_t", [P, 4, L], F32, offset=u_at)
    gate_t = place("gate_t", [P, 4, L], F32, offset=u_at)
    cat_f = place("cat_f", [P, 4, L], F32, offset=u_at + 8192)
    at = [u_at]
    sm = lay(at, "sm", [P, 32, GT])
    pw_re = lay(at, "pw_re", [P, GT, RUN + 1])
    pw_im = lay(at, "pw_im", [P, GT, RUN + 1])
    cb = [lay(at, f"cb{i}", [P, GT, C]) for i in range(2)]
    bb = [lay(at, f"bb{i}", [P, GT, C]) for i in range(2)]
    bz = [place(f"bz{i}", [P, GT, C], F32, offset=u_at + 8192 + i * 1024) for i in range(2)]
    skip = place("skip", [C, G], F32, offset=u_at + 8192 + 2048)
    skip_d = place("skip_d", [C, G, C], F32, offset=u_at + 8192 + 2048 + 128)
    assert at[0] <= u_at + 8192
    at = [arena]
    a_hi = lay(at, "a_hi", [P, QT, L], F32R)
    a_lo = lay(at, "a_lo", [P, QT, L], F32R)
    ada_l1_ring = lay(at, "ada_l1_ring", [P, 16, ADA_Q])
    assert at[0] <= nc.sbuf_usable_end, (at[0], nc.sbuf_usable_end)
    at = [arena]
    qk = {}
    for name in ("qd", "kd", "vd", "qc", "kc", "vc"):
        qk[name] = lay(at, name, [P, 4, L])
    sel_at = [0, P, P + 2 * P, P + 2 * P + 3 * P]
    dsel = lay(at, "dsel", [P, sum((i + 1) * P for i in range(NB))])
    tri = lay(at, "tri", [P, P])
    idx_at = at[0]
    qi_t = lay(at, "qi_t", [P, 4, L])
    ki_t = lay(at, "ki_t", [P, L])
    dist = lay(at, "dist", [P, L])
    sc_at = [0, 0, 2 * P, 5 * P]
    score = lay(at, "score", [P, 9 * P])
    at = [idx_at]
    W1 = sum((NB - j) * P for j in range(NB))
    z_at = [0, 4 * P, 7 * P, 9 * P]
    z_sb = [lay(at, f"z_sb{i}", [P, W1]) for i in range(2)]
    sp_sb = [lay(at, f"sp_sb{i}", [P, W1]) for i in range(2)]
    pT = lay(at, "pT", [P, NB, L])
    assert at[0] <= nc.sbuf_usable_end, (at[0], nc.sbuf_usable_end)
    p_at = [0, P, 3 * P, 6 * P]
    probs_b = place("probs_b", [P, 10 * P], F32, offset=ada_ring_at)

    def probs(step, i):
        if step % 2:
            return probs_b[:, p_at[i]:p_at[i] + (i + 1) * P]
        return work[i][:, 0:(i + 1) * P]

    y_out = place("y_out", [P, NB, D], F32, offset=arena)

    psum = nc.alloc_psum_tensor("psum", [P, 8 * L], F32)
    bank = [psum[:, i * L:(i + 1) * L] for i in range(8)]

    u_dram = nc.dram_tensor("u_scratch", (HALF, L), F32, kind="Internal").ap()
    y_dram = nc.dram_tensor("y_scratch", (HALF, L), F32, kind="Internal").ap()

    def sem(name):
        return nc.alloc_semaphore(name)

    def cols(w, c0, n=SLOT):
        return w.rearrange("(k p) n -> p k n", p=P)[:, :, c0:c0 + n]

    slots = []
    AB_IN = len(slots)
    slots += [cols(ab_w_in[0], c0) for c0 in (HALF, HALF + SLOT, 0, SLOT)]
    GLU = len(slots)
    slots += [glu_w[0].rearrange("(k p) n -> p k n", p=P)]
    AB_OUT = len(slots)
    slots += [cols(ab_w_out[0], c0) for c0 in range(0, D, SLOT)]
    MLP = [len(slots)]
    slots += [None] * (8 * QUARTERS)
    CD_IN = len(slots)
    CD = dict(qc=0, kc=512, vc=1024, qi=1536, ki=2048, wi=2112, qd=2120, kd=2632, vd=3144)
    cd_order = ["qi", "ki", "qd", "kd", "vd", "qc", "kc", "vc"]
    cd_slots = []
    for name in cd_order:
        for half in range(1 if name == "ki" else 2):
            cd_slots.append((name, half))
            slots.append(None if name == "ki" else cols(cd_w_in[0], CD[name] + half * SLOT))
    KI = CD_IN + cd_slots.index(("ki", 0))
    CD_OUT = len(slots)
    slots += [cols(cd_w_out[0], c0) for c0 in range(0, D, SLOT)]
    MLP.append(len(slots))
    slots += [None] * (8 * QUARTERS)
    NSLOT = len(slots)

    landed = []
    total = [0, 0]
    for n in range(NSLOT):
        total[n % 2] += 48 if n == KI else 16
        landed.append(total[n % 2])

    tiles_of = {n: 2 for n in range(NSLOT)}
    tiles_of[GLU] = 4
    for i, (name, _) in enumerate(cd_slots):
        if name in ("vd", "vc"):
            tiles_of[CD_IN + i] = NB
    first_tile, drains = [], []
    drained = {False: 0, True: 0}
    for n in range(NSLOT):
        first_tile.append(len(drains))
        for _ in range(tiles_of[n]):
            by_dve = AB_OUT <= n < AB_OUT + 4 or CD_OUT <= n < CD_OUT + 4 or \
                any(m <= n < m + 32 and (n - m) % 8 >= 4 for m in MLP)
            drained[by_dve] += 1
            drains.append((by_dve, drained[by_dve]))

    raw_in = [sem("raw_in0"), sem("raw_in1")]
    hi_ready = sem("w_hi_ready")
    lo_ready = sem("w_lo_ready")
    tile_done = sem("tile_done")
    act_drain = sem("act_drained")
    dve_drain = sem("dve_drained")
    square_done = sem("square_done")
    a_ready = sem("a_ready")
    sumsq_ready = sem("sumsq_ready")
    norm_part = sem("norm_part")
    norm_sum = sem("norm_sum")
    rstd_ready = sem("rstd_ready")
    xn_ready = sem("xn_ready")
    hh_ready = sem("h_hi_ready")
    h_ready = sem("h_ready")
    ada_in = [sem(f"ada_in{i}") for i in range(ADA_RING)]
    ada_in0 = [sem(f"ada_first_in{i}") for i in range(ADA_FIRST)]
    ada_used = sem("ada_used")
    ada_sum = sem("ada_sum")
    mods_part = sem("mods_part")
    mods_ready = sem("mods_ready")
    small_in = sem("small_in")
    b_in = sem("b_in")
    d_in = sem("d_in")
    dt_in = sem("dt_in")
    dt_rows = sem("dt_rows")
    poolw_in = sem("poolw_in")
    x_in = sem("x_in")
    consts = sem("consts")
    params_ps = sem("params_ps")
    params = sem("params")
    xT_ps = sem("xT_ps")
    act_own = sem("act_own")
    act_n = [0]
    dve_own = sem("dve_own")
    dve_n = [0]
    pool_own = sem("pool_own")
    pool_n = [0]
    setup_act = sem("setup_act")
    setup_dve = sem("setup_dve")
    powers = sem("powers")
    g_ready = sem("g_ready")
    f_ready = sem("f_ready")
    mats_ps = sem("mats_ps")
    mats_out = sem("mats_out")
    kr_ready = sem("kr_ready")
    toep_zero = sem("toep_zero")
    toep_in = sem("toep_in")
    rot_ready = sem("rot_ready")
    ub_ready = sem("ub_ready")
    u_out = sem("u_out")
    ada_l1 = [sem(f"ada_l1_in{i}") for i in range(8)]
    c_in = sem("c_in")
    c_ps = sem("c_ps")
    cn_in = sem("cn_in")
    x_squared = sem("x_squared")
    sq_ready = sem("sq_ready")
    u_in = sem("u_in")
    ua_pad = sem("ua_pad")
    ua_ready = sem("ua_ready")
    pooled = sem("pooled")
    pool_ps = sem("pool_ps")
    pool_free = sem("pool_free")
    inj_ps = sem("inj_ps")
    states = sem("states")
    y_ps = sem("y_ps")
    y_copied = sem("y_copied")
    y_out_s = sem("y_out_s")
    y_in = sem("y_in")
    gelu_hi = sem("gelu_hi")
    gelu_lo = sem("gelu_lo")
    gate_act = sem("gate_act")
    cat_mid = sem("cat_mid")
    cat_hi = sem("cat_hi")
    cat_ready = sem("cat_ready")
    l1_consts = sem("l1_consts")
    idx_in = sem("idx_in")
    idx_ps = sem("idx_ps")
    idx_rel = sem("idx_rel")
    idx_acc = sem("idx_acc")
    dsel_ready = sem("dsel_ready")
    proj = sem("proj_copied")
    z_ps = sem("z_ps")
    z_copied = sem("z_copied")
    z_abs = sem("z_abs")
    z_soft = sem("z_soft")
    sp_diag = sem("sp_diag")
    sp_ready = sem("sp_ready")
    r_ps = sem("r_ps")
    r_used = sem("r_used")
    w_exp = sem("w_exp")
    w_ready = sem("w_ready")
    o_ps = sem("o_ps")
    o_free = sem("o_free")
    s_ps = sem("s_ps")
    s_used = sem("s_used")
    max_ready = sem("max_ready")
    p_exp = sem("p_exp")
    p_ready = sem("p_ready")
    t_ps = sem("t_ps")
    t_copied = sem("t_copied")
    oc_ps = sem("oc_ps")
    fin_t = sem("fin_t")
    fin_ps = sem("fin_ps")
    fin_copied = sem("fin_copied")
    out_done = sem("out_done")

    def w1_src(layer, q, i):
        return mlp_w1[layer].rearrange("(k p) n -> p k n", p=P)[
            :, :, bass.ds(q * (FF // QUARTERS) + i * SLOT, SLOT)]

    def w2_src(layer, q, i):
        v = mlp_w2[layer].rearrange("(k p) n -> p k n", p=P)
        return v[:, bass.ds(q * QT, QT), i * SLOT:(i + 1) * SLOT]

    ADA_STEPS = 8 * 4
    ADA_EARLY = 8 * 3

    def ada_src(a, qt, k):
        return ada_w[a // 2, a % 2, k * P:(k + 1) * P, bass.ds(qt * ADA_Q, ADA_Q)]

    block = nc.Block()
    block.__enter__()

    @block.sync
    def _(sp):
        sp.dma_start(x_nat[:, :, :], x[0].rearrange("(t p) d -> p t d", p=P)).then_inc(x_in, 16)

        def load(n, src, q=None):
            if n >= 2:
                sp.wait_ge(lo_ready, n - 1 + (0 if q is None else 8 * q))
            dst = raw[n % 2][:, :, :]
            if n == GLU:
                dst = dst.rearrange("p a b -> p (a b)").rearrange("p (k n) -> p k n", k=4)
            sp.dma_start(dst, src).then_inc(raw_in[n % 2], 16)

        def load_ada(e):
            u = e // 8
            if e < ADA_EARLY:
                r, buf, signal = ADA_FIRST, ada_first, ada_in0
            else:
                r, buf, signal = ADA_RING, ada_ring, ada_in
            at_ = e if e < ADA_EARLY else e - ADA_EARLY
            if at_ >= r:
                sp.wait_ge(ada_used, e - r + 1)
            sp.dma_start(buf[:, at_ % r, :], ada_src(u // 4, u % 4, e % 8)).then_inc(signal[at_ % r], 16)

        ada_next = [0]

        def more_ada(count):
            for _ in range(count):
                load_ada(ada_next[0])
                ada_next[0] += 1

        more_ada(8)
        load(0, slots[0])
        more_ada(ADA_EARLY - 8)
        load(1, slots[1])
        load(2, slots[2])
        more_ada(4)
        load(3, slots[3])
        more_ada(4)
        load(GLU, slots[GLU])
        sp.wait_ge(u_out, 16 * 4)
        sp.wait_ge(rot_ready, 1)
        for m in range(RUN):
            j = RUN - 1 - m
            sp.dma_start(u_run[m * C:(m + 1) * C, :, :],
                         u_dram.rearrange("(g c) t -> c g t", c=C)[:, :, j * NRUN:(j + 1) * NRUN])\
              .then_inc(u_in, 16)
        more_ada(8)
        load(AB_OUT, slots[AB_OUT])
        more_ada(8 + ADA_RING)
        for half in range(2):
            sp.wait_ge(y_copied, 2 * half + 2)
            g0 = half * G // 2
            for i in range(RUN):
                sp.dma_start(
                    y_dram.rearrange("(g c) t -> c g t", c=C)[:, g0:g0 + G // 2, i * NRUN:(i + 1) * NRUN],
                    y_run[i * C:(i + 1) * C, g0:g0 + G // 2, :]).then_inc(y_out_s, 16)
        sp.wait_ge(y_out_s, 16 * 2 * RUN)
        sp.wait_ge(y_ps, 4)
        for ct in range(4):
            sp.dma_start(y_t[:, ct, :], y_dram[ct * P:(ct + 1) * P, :]).then_inc(y_in, 16)
        more_ada(8 - ADA_RING)
        load(AB_OUT + 1, slots[AB_OUT + 1])
        more_ada(4)
        load(AB_OUT + 2, slots[AB_OUT + 2])
        more_ada(4)
        load(AB_OUT + 3, slots[AB_OUT + 3])
        assert ada_next[0] == 2 * ADA_STEPS
        sp.wait_ge(cat_ready, 8)

        def quarter(layer, q):
            n0 = MLP[layer]
            for i in range(8):
                load(n0 + i, w1_src(layer, q, i) if i < 4 else w2_src(layer, q, i - 4), q)
                if layer == 0:
                    for e in (2 * i, 2 * i + 1):
                        sp.wait_ge(ada_used, 2 * ADA_STEPS - 16 + e + 1 + 16 * q)
                        sp.dma_start(ada_l1_ring[:, e, :], ada_src(2 + e // 8, q, e % 8))\
                          .then_inc(ada_l1[i], 16)

        with sp.Fori(0, QUARTERS) as q:
            quarter(0, q)
        for n in range(CD_IN, MLP[1]):
            if n == KI:
                sp.wait_ge(lo_ready, n - 1)
                for c0, src, w in ((0, CD["ki"], HD), (HD, CD["ki"], HD), (2 * HD, CD["wi"], 8)):
                    sp.dma_start(raw[n % 2][:, :, c0:c0 + w], cols(cd_w_in[0], src, w))\
                      .then_inc(raw_in[n % 2], 16)
            else:
                load(n, slots[n])
        with sp.Fori(0, QUARTERS) as q:
            quarter(1, q)
        for k in range(KC):
            sp.wait_ge(fin_copied, k + 1)
            sp.dma_start(out[0].rearrange("(t p) d -> p t d", p=P)[:, :, k * P:(k + 1) * P],
                         y_out[:, :, k * P:(k + 1) * P]).then_inc(out_done, 16)
        sp.wait_ge(out_done, 16 * KC)

    @block.gpsimd
    def _(pool):
        def own(ins):
            pool_n[0] += 1
            ins.then_inc(pool_own, 1)

        def settle():
            pool.wait_ge(pool_own, pool_n[0])

        own(pool.memset(ident[:, :], 0.0))
        own(pool.memset(ones[:, :], 1.0))
        settle()
        pool.affine_select(out=ident[:, :], in_=ident[:, :], compare_op=ALU.not_equal, fill=1.0,
                           base=0, pattern=[[-1, P]], channel_multiplier=1).then_inc(consts, 1)
        own(pool.iota(small[:, 0:PAD].bitcast(I32), pattern=[[1, PAD]], base=1, channel_multiplier=0))
        settle()
        pool.tensor_copy(recip[:, :], small[:, 0:PAD].bitcast(I32)).then_inc(consts, 1)
        pool.memset(toep[:, :, :], 0.0).then_inc(toep_zero, 1)

        squares = [0]

        def square_tile(k, wait):
            wait()
            if squares[0]:
                pool.wait_ge(sumsq_ready, squares[0])
            if k == 0:
                ins = pool.tensor_tensor(sumsq[:, :], xT[:, k, :], xT[:, k, :], ALU.mult)
            else:
                own(pool.tensor_tensor(work[3][:, 0:L], xT[:, k, :], xT[:, k, :], ALU.mult))
                settle()
                ins = pool.tensor_tensor(sumsq[:, :], sumsq[:, :], work[3][:, 0:L], ALU.add)
            ins.then_inc(sumsq_ready, 1)
            squares[0] += 1

        pool.wait_ge(powers, 1)

        def bc(c_t):
            return c_t[:, :, :].unsqueeze(2).to_broadcast([P, GT, RUN + 1, C])

        def bp(p_t):
            return p_t[:, :, :].unsqueeze(3).to_broadcast([P, GT, RUN + 1, C])

        def tt(o, a, b, op):
            own(pool.tensor_tensor(o, a, b, op))
            settle()

        tt(g_re[:, :, :, :], bc(cb[0]), bp(pw_re), ALU.mult)
        tt(g_tmp[:, :, :, :], bc(cb[1]), bp(pw_im), ALU.mult)
        tt(g_re[:, :, :, :], g_re[:, :, :, :], g_tmp[:, :, :, :], ALU.subtract)
        tt(g_ni[:, :, :, :], bc(cb[0]), bp(pw_im), ALU.mult)
        tt(g_tmp[:, :, :, :], bc(cb[1]), bp(pw_re), ALU.mult)
        tt(g_ni[:, :, :, :], g_ni[:, :, :, :], g_tmp[:, :, :, :], ALU.add)
        pool.tensor_scalar(g_ni[:, :, :, :], g_ni[:, :, :, :], -1.0, None, ALU.mult)\
            .then_inc(g_ready, 1)

        norms = [0]

        def normalise():
            norms[0] += 1
            pool.wait_ge(rstd_ready, norms[0])
            for k in range(KC):
                if k >= 2:
                    pool.wait_ge(h_ready, 8 * (norms[0] - 1) + k - 1)
                pool.tensor_tensor(work[k % 2][:, 0:L], xT[:, k, :], rstd[:, :], ALU.mult)\
                    .then_inc(xn_ready, 1)

        normalise()

        for w in (0, 1):
            pool.wait_ge(h_ready, 8)
            own(pool.memset(work[w][:, 0:PAD], 0.0))
        pool.wait_ge(ua_pad, 1)
        for ct in range(4):
            pool.wait_ge(act_drain, drains[first_tile[AB_IN + 2] + ct][1])
            if ct:
                pool.wait_ge(pooled, ct)
            u = ua[:, ct, :]
            src, step = u, 1
            for r in range(ct + 1):
                settle()
                dst = work[r % 2][:, :]
                own(pool.tensor_tensor(dst[:, PAD:], src[:, PAD:], src[:, PAD - step:PAD + L - step],
                                       ALU.add))
                src, step = dst, 2 * step
            win = WINDOWS[ct]
            settle()
            own(pool.tensor_tensor(src[:, PAD:PAD + win], src[:, PAD:PAD + win], recip[:, 0:win],
                                   ALU.mult))
            own(pool.tensor_scalar(src[:, PAD + win:], src[:, PAD + win:], 1.0 / win, None, ALU.mult))
            settle()
            pool.tensor_tensor(u[:, PAD:], src[:, PAD:], u[:, PAD:], ALU.subtract).then_inc(pooled, 1)

        for k in range(KC):
            d = drains[first_tile[AB_OUT] + k]
            square_tile(k, lambda: pool.wait_ge(dve_drain, d[1]))
        normalise()

        def quarter(layer, q):
            t0 = first_tile[MLP[layer]]
            base_sq, base_own = squares[0], pool_n[0]
            for i in range(8):
                if i >= 4:
                    for r in range(2):
                        k = (i - 4) * 2 + r
                        pool.wait_ge(dve_drain, drains[t0 + 8 + k][1] + 8 * q)
                        pool.wait_ge(sumsq_ready, base_sq + k + 8 * q)
                        if k == 0:
                            ins = pool.tensor_tensor(sumsq[:, :], xT[:, k, :], xT[:, k, :], ALU.mult)
                        else:
                            pool.tensor_tensor(work[3][:, 0:L], xT[:, k, :], xT[:, k, :], ALU.mult)\
                                .then_inc(pool_own, 1)
                            pool.wait_ge(pool_own, base_own + k + 7 * q)
                            ins = pool.tensor_tensor(sumsq[:, :], sumsq[:, :], work[3][:, 0:L], ALU.add)
                        ins.then_inc(sumsq_ready, 1)

        def mlp(layer):
            with pool.Fori(0, QUARTERS) as q:
                quarter(layer, q)
            squares[0] += 8 * QUARTERS
            pool_n[0] += 7 * QUARTERS

        mlp(0)
        pool.wait_ge(tile_done, first_tile[CD_IN])
        own(pool.memset(tri[:, :], 1.0))
        own(pool.iota(dist[:, :].bitcast(I32), pattern=[[-1, L]], base=L - P, channel_multiplier=1))
        settle()
        own(pool.affine_select(out=tri[:, :], in_=tri[:, :], compare_op=ALU.is_ge, fill=0.0,
                               base=0, pattern=[[-1, P]], channel_multiplier=1))
        settle()
        pool.tensor_copy(dist[:, :], dist[:, :].bitcast(I32)).then_inc(l1_consts, 1)
        normalise()

        def keep_causal(buf, j, signal):
            v = buf[:, z_at[j]:z_at[j] + P]
            ins = pool.affine_select(out=v, in_=v, compare_op=ALU.is_gt, fill=0.0, base=0,
                                     pattern=[[1, P]], channel_multiplier=-1)
            ins.then_inc(signal, 1)

        for step in range(H + 1):
            if step >= 1:
                for j in range(NB):
                    pool.wait_ge(w_exp, NB * (step - 1) + j + 1)
                    keep_causal(z_sb[(step - 1) % 2], j, w_ready)
            if step < H:
                pool.wait_ge(sp_diag, step + 1)
                for j in range(NB):
                    keep_causal(sp_sb[step % 2], j, sp_ready)

        for k in range(KC):
            d = drains[first_tile[CD_OUT] + k]
            square_tile(k, lambda: pool.wait_ge(dve_drain, d[1]))
        normalise()
        mlp(1)

    @block.scalar
    def _(act):
        def own(ins):
            act_n[0] += 1
            ins.then_inc(act_own, 1)

        def settle():
            act.wait_ge(act_own, act_n[0])

        def rows(v):
            return v.rearrange("(r c) -> r c", c=P)

        act.dma_start(raw_c[:, :], rows(c[0])).then_inc(c_in, 16)
        act.dma_start(raw_a[0:32, :], norm_g.rearrange("l s (r c) -> (l s r) c", c=P)).then_inc(small_in, 16)
        act.dma_start(raw_a[32:P, :], ada_b.rearrange("l s (r c) -> (l s r) c", c=P)).then_inc(small_in, 16)
        act.dma_start(raw_b[0:8, :], rows(final_g)).then_inc(small_in, 16)
        act.dma_start(raw_b[8:12, :], rows(pool_scale[0])).then_inc(small_in, 16)
        act.dma_start(raw_b[12:16, :], rows(glu_b[0])).then_inc(small_in, 16)
        act.dma_start(raw_b[16:32, :], ssm_lam_re[0].rearrange("(t g) p -> t (g p)", g=2)).then_inc(small_in, 16)
        act.dma_start(raw_b[32:48, :], ssm_lam_im[0].rearrange("(t g) p -> t (g p)", g=2)).then_inc(small_in, 16)
        act.dma_start(raw_dt2[:, :], ssm_log_dt[0].rearrange("(t g) -> t g", g=2)).then_inc(dt_in, 16)
        for ri, src in enumerate((ssm_c_re, ssm_c_im)):
            for twice in range(2):
                act.dma_start(c_nat[ri][:, :, twice, :],
                              src[0].rearrange("(b g) c p -> (g c) b p", b=4)).then_inc(cn_in, 16)
        for ri, src in enumerate((ssm_b_re, ssm_b_im)):
            act.dma_start(bb[ri][:, :, :], src[0].rearrange("(t g) p c -> (g p) t c", g=2)).then_inc(b_in, 16)
        act.dma_start(skip[:, :], ssm_d[0].rearrange("(g c) -> c g", c=C),
                      allow_slow_non_contiguous=True).then_inc(d_in, 16)
        act.dma_start(pool_w_t[:, :, :], pool_w[0].rearrange("g c d -> c g d")).then_inc(poolw_in, 16)

        def prep(n, q=None):
            m, over = n, 0
            if q is not None:
                over = q
            act.wait_ge(raw_in[n % 2], landed[n] + 64 * over)
            if n >= 2:
                act.wait_ge(tile_done, first_tile[n - 1] + 16 * over)
            w = 2 * HD + 8 if n == KI else SLOT
            act.activation(w_hi[n % 2][:, :, 0:w], raw[n % 2][:, :, 0:w], ACT.Copy).then_inc(hi_ready, 1)

        for k in range(KC):
            act.wait_ge(xT_ps, k + 1)
            own(act.activation(xT[:, k, :], bank[k % 4], ACT.Copy))
            if k >= 4:
                act.wait_ge(norm_part, k - 3)
            act.activation(sq_x[:, k % 4, :], bank[k % 4], ACT.Square).then_inc(x_squared, 1)

        act.wait_ge(params, 1)
        act.activation(sm[:, 0, :], pb[:, 56:72], ACT.Exp).then_inc(setup_act, 1)
        act.wait_ge(setup_dve, 1)
        act.activation(sm[:, 4, :], sm[:, 1, :], ACT.Exp).then_inc(setup_act, 1)
        act.activation(sm[:, 5, :], sm[:, 1, :], ACT.Exp, scale=float(RUN)).then_inc(setup_act, 1)
        act.activation(sm[:, 6, :], sm[:, 3, :], ACT.Sin).then_inc(setup_act, 1)
        act.activation(sm[:, 7, :], sm[:, 3, :], ACT.Sin, scale=0.5).then_inc(setup_act, 1)

        norms = [0]

        def norm_rstd():
            norms[0] += 1
            act.wait_ge(norm_sum, norms[0])
            own(act.activation(rstd[:, :], bank[6], ACT.Ln, scale=1.0 / D, bias=eps_t[:, 0:1]))
            settle()
            act.activation(rstd[:, :], rstd[:, :], ACT.Exp, scale=-0.5).then_inc(rstd_ready, 1)

        def modulate(a):
            act.wait_ge(mods_ready, a + 1)
            for k in range(KC):
                act.wait_ge(xn_ready, 8 * a + k + 1)
                act.activation(h_hi[:, k, :], work[k % 2][:, 0:L], ACT.Identity,
                               scale=mods[:, a, 8 + k:9 + k], bias=mods[:, a, k:k + 1]).then_inc(hh_ready, 1)

        for i in range(8):
            act.wait_ge(mats_ps, i + 1)
            dst = (e_re, e_im)[i // 4][:, (i % 4) * 4:(i % 4) * 4 + 4, :]
            act.activation(dst.rearrange("p t n -> p (t n)"), bank[4 + i % 2], ACT.Copy).then_inc(mats_out, 1)
        norm_rstd()
        for i in range(8, 16):
            act.wait_ge(mats_ps, i + 1)
            t = (i - 8) // 2 * 4
            dst = kr[:, :, :].rearrange("p (t g) n -> p g t n", g=2)[:, i % 2, t:t + 4, :]
            act.activation(dst, bank[4 + i % 2][0:C, :].rearrange("p (t n) -> p t n", n=P), ACT.Copy)\
               .then_inc(mats_out, 1)
        act.wait_ge(ada_used, ADA_EARLY)
        prep(0)
        act.wait_ge(kr_ready, 1)
        act.wait_ge(toep_zero, 1)
        for m in range(RUN):
            act.dma_start(toep[m * C:(m + 1) * C, :, (RUN - 1 - m) * C:],
                          kr[:, :, 0:(m + 1) * C]).then_inc(toep_in, 16)
        act.wait_ge(toep_in, 16 * RUN)
        modulate(0)

        def copy_tile(t, dst, src=None, **kw):
            act.wait_ge(tile_done, t + 1)
            act.activation(dst, bank[t % 4] if src is None else src, ACT.Copy, **kw).then_inc(act_drain, 1)

        for n in range(AB_IN, GLU):
            prep(n + 1)
            for r in range(2):
                t = first_tile[n] + r
                if n < AB_IN + 2:
                    ct = 2 * (n - AB_IN) + r
                    copy_tile(t, ub[:, ct, :, :], bank[t % 4].rearrange("p (k j) -> p j k", j=RUN))
                    act.wait_ge(act_drain, drains[t][1])
                    act.dma_start(u_dram[ct * P:(ct + 1) * P, :],
                                  ub[:, ct, :, :].rearrange("p j k -> p (j k)")).then_inc(u_out, 16)
                else:
                    copy_tile(t, ua[:, 2 * (n - AB_IN - 2) + r, PAD:])
        for b in range(4):
            act.wait_ge(y_ps, b + 1)
            dst = y_run[:, :, :].rearrange("p (t g) k -> p g t k", g=2)[:, b % 2, b // 2 * 8:b // 2 * 8 + 8, :]
            act.activation(dst, bank[b].rearrange("p (t k) -> p t k", k=NRUN), ACT.Copy)\
               .then_inc(y_copied, 1)
        for g in range(4):
            act.wait_ge(pool_ps, g + 1)
            act.activation(h_hi[:, g, :], bank[4 + g], ACT.Identity, scale=pb[:, 16 + g:17 + g])\
               .then_inc(cat_hi, 1)
        act.wait_ge(y_in, 16 * 4)
        for ct in range(4):
            own(act.activation(y_act[:, ct, :], y_t[:, ct, :], ACT.Gelu_apprx_tanh))
            settle()
            act.activation(yg_hi[:, ct, :], y_act[:, ct, :], ACT.Copy).then_inc(gelu_hi, 1)
        prep(AB_OUT)
        for m in range(4):
            t = first_tile[GLU] + m
            act.wait_ge(tile_done, t + 1)
            act.activation(gate_t[:, m, :], bank[t % 4], ACT.Sigmoid, bias=pb[:, 20 + m:21 + m])\
               .then_inc(act_drain, 1)
        for m in range(4):
            act.wait_ge(cat_mid, m + 1)
            act.activation(h_hi[:, 4 + m, :], cat_f[:, m, :], ACT.Copy).then_inc(cat_hi, 1)
        for n in range(AB_OUT, MLP[0]):
            prep(n + 1)
        norm_rstd()
        modulate(1)

        def quarter(layer, q, last=False):
            n0, t0 = MLP[layer], first_tile[MLP[layer]]
            a0 = 32 * layer
            for i in range(8):
                if not (last and i == 7):
                    prep(n0 + i + 1, q)
                if i < 4:
                    for r in range(2):
                        t = 2 * i + r
                        act.wait_ge(tile_done, t0 + t + 1 + 16 * q)
                        if t >= 2:
                            act.wait_ge(a_ready, a0 + t - 1 + 8 * q)
                        act.activation(work[t % 2][:, 0:L], bank[(t0 + t) % 4], ACT.Relu)\
                           .then_inc(act_drain, 1)
                        act.wait_ge(act_drain, drains[t0 + t][1] + 8 * q)
                        act.activation(a_hi[:, t, :], work[t % 2][:, 0:L], ACT.Square)\
                           .then_inc(square_done, 1)

        with act.Fori(0, QUARTERS) as q:
            quarter(0, q)

        norm_rstd()
        modulate(2)

        def index_relu():
            cnt = 0
            for i in range(1, NB):
                for h in range(8):
                    act.wait_ge(idx_ps, cnt + 1)
                    if cnt >= 2:
                        act.wait_ge(idx_acc, cnt - 1)
                    act.activation(work[cnt % 2][:, 0:(i + 1) * P], bank[4 + cnt % 4][:, 0:(i + 1) * P],
                                   ACT.Relu).then_inc(idx_rel, 1)
                    cnt += 1

        for j, (name, half) in enumerate(cd_slots):
            n = CD_IN + j
            prep(n + 1)
            t0 = first_tile[n]
            if name == "ki":
                copy_tile(t0, ki_t[:, :])
                copy_tile(t0 + 1, wi_t[:, :, :].rearrange("p b h -> p (b h)"),
                          bank[(t0 + 1) % 4][:, 0:NB * 8], scale=IDX_SCALE)
            elif name in ("vd", "vc"):
                for b in range(NB):
                    copy_tile(t0 + b, qk[name][:, b, half * SLOT:(half + 1) * SLOT],
                              bank[(t0 + b) % 4][:, 0:SLOT])
            else:
                dst = qi_t if name == "qi" else qk[name]
                for r in range(2):
                    copy_tile(t0 + r, dst[:, 2 * half + r, :], scale=HD ** -0.5 if name in ("qd", "qc") else 1.0)
            if j == cd_slots.index(("qd", 0)):
                index_relu()

        def out_hi(pair):
            for tile, b, signal in ((pair, 7, oc_ps), (4 + pair, 6, o_ps)):
                act.wait_ge(signal, 2 * pair + 2)
                act.activation(h_hi[:, tile, :], bank[b], ACT.Copy).then_inc(cat_hi, 1)

        act.wait_ge(tile_done, first_tile[CD_OUT])
        for step in range(H + 1):
            if step < H:
                z, s_ = z_sb[step % 2], sp_sb[step % 2]
                if step == 0:
                    act.wait_ge(dsel_ready, 1)
                if step >= 2:
                    act.wait_ge(o_ps, step - 1)
                for j in range(NB):
                    act.wait_ge(z_ps, NB * step + j + 1)
                    act.activation(z[:, z_at[j]:z_at[j] + (NB - j) * P], bank[j % 2][:, 0:(NB - j) * P],
                                   ACT.Copy).then_inc(z_copied, 1)
            if step >= 1:
                for i in range(NB):
                    act.wait_ge(t_ps, NB * (step - 1) + i + 1)
                    if i == 0 and step >= 2:
                        act.wait_ge(oc_ps, step - 1)
                    act.activation(pT[:, 0:i + 1, i * P:(i + 1) * P],
                                   bank[4 + i % 2][:, 0:(i + 1) * P].rearrange("p (j q) -> p j q", q=P),
                                   ACT.Copy).then_inc(t_copied, 1)
            if step >= 3 and step % 2 == 1:
                out_hi((step - 3) // 2)
            for i in range(NB):
                if step < H:
                    act.wait_ge(max_ready, NB * step + i + 1)
                    act.activation(probs(step, i), probs(step, i), ACT.Exp, bias=small[:, i:i + 1],
                                   accum_out=small[:, 8 + i:9 + i]).then_inc(p_exp, 1)
            if step >= 1:
                z = z_sb[(step - 1) % 2]
                for j in range(NB):
                    act.wait_ge(r_used, NB * (step - 1) + j + 1)
                    v_ = z[:, z_at[j]:z_at[j] + (NB - j) * P]
                    act.activation(v_, v_, ACT.Exp).then_inc(w_exp, 1)
            if step < H:
                act.wait_ge(z_abs, step + 1)
                own(act.activation(s_[:, :], s_[:, :], ACT.Exp, scale=-1.0))
                settle()
                act.activation(s_[:, :], s_[:, :], ACT.Ln, bias=eps_t[:, 1:2]).then_inc(z_soft, 1)
        out_hi(H // 2 - 1)
        for n in range(CD_OUT, MLP[1]):
            prep(n + 1)
        norm_rstd()
        modulate(3)
        with act.Fori(0, QUARTERS - 1) as q:
            quarter(1, q)
        quarter(1, QUARTERS - 1, last=True)
        norm_rstd()
        for k in range(KC):
            act.wait_ge(fin_ps, k + 1)
            act.activation(y_out[:, :, k * P:(k + 1) * P], bank[k % 4].rearrange("p (t n) -> p t n", n=P),
                           ACT.Copy).then_inc(fin_copied, 1)

    @block.vector
    def _(dve):
        def own(ins):
            dve_n[0] += 1
            ins.then_inc(dve_own, 1)

        def settle():
            dve.wait_ge(dve_own, dve_n[0])

        def tt(o, a, b, op):
            own(dve.tensor_tensor(o, a, b, op))
            settle()

        def ts(o, a, s1, s2, op0, op1=ALU.bypass):
            own(dve.tensor_scalar(o, a, s1, s2, op0, op1))
            settle()

        def stt(o, a, s1, b, op0, op1):
            own(dve.scalar_tensor_tensor(out=o, in0=a, scalar=s1, in1=b, op0=op0, op1=op1))
            settle()

        ada_e = [0]

        def ada_step():
            e = ada_e[0]
            ada_e[0] += 1
            k = e % 8
            if e < ADA_EARLY:
                r, buf, signal, at_ = ADA_FIRST, ada_first, ada_in0, e
            else:
                r, buf, signal, at_ = ADA_RING, ada_ring, ada_in, e - ADA_EARLY
            dve.wait_ge(signal[at_ % r], 16 * (at_ // r + 1))
            src = buf[:, at_ % r, :]
            if k == 0:
                ins = dve.tensor_scalar(ada_acc[:, :], src, pb[:, 0:1], None, ALU.mult)
            else:
                dve.wait_ge(ada_used, e)
                ins = dve.scalar_tensor_tensor(out=ada_acc[:, :], in0=src, scalar=pb[:, k:k + 1],
                                               in1=ada_acc[:, :], op0=ALU.mult, op1=ALU.add)
            ins.then_inc(ada_used, 1)

        def ada_steps(count):
            for _ in range(count):
                ada_step()

        own(dve.memset(eps_t[:, 0:1], EPS))
        own(dve.memset(eps_t[:, 1:2], 1.0))
        dve.wait_ge(c_ps, 1)
        own(dve.tensor_copy(pb[:, 0:8], bank[7][:, 0:8]))
        settle()
        dve.wait_ge(dt_in, 16)
        dve.tensor_copy(raw_dt[:, :].rearrange("t (g p) -> t g p", g=2),
                        raw_dt2[:, :].unsqueeze(2).to_broadcast([GT, 2, S])).then_inc(dt_rows, 1)
        ada_steps(4)
        dve.wait_ge(consts, 2)
        own(dve.reciprocal(recip[:, :], recip[:, :]))
        dve.wait_ge(params_ps, 1)
        own(dve.tensor_copy(pa[:, :], bank[4][:, 0:P]))
        for ri in range(2):
            for g2 in range(2):
                part = slice(S * g2, S * g2 + S)
                own(dve.tensor_copy(cb[ri][part, :, :],
                                    bank[5 + ri].rearrange("p (t g c) -> p g t c", g=2, c=C)[part, g2]))
        own(dve.tensor_copy(pb[:, 8:72], bank[4][:, P:P + 64]))
        settle()
        dve.sem_inc(params, 1)

        DT, LRDT, TH, RED, MAG, MAG8, SIN, SINH, COS, AR, AI, DEN, RD, X1, X2, ZR, ZI, K_, CU, SU, \
            RC, RS = (0, 1, 2, 3, 4, 5, 6, 7, 8, 9, 10, 11, 12, 13, 14, 15, 16, 17, 18, 19, 20, 21)

        def v(i):
            return sm[:, i, :]

        lr, li = pb[:, 24:40], pb[:, 40:56]
        M, A, SB = ALU.mult, ALU.add, ALU.subtract
        dve.wait_ge(setup_act, 1)
        tt(v(LRDT), lr, v(DT), M)
        tt(v(TH), li, v(DT), M)
        magic = 1.5 * 2.0 ** 23
        c1 = 6.28125
        c2 = 0.0019350051879882812
        c3 = 2 * math.pi - c1 - c2
        ts(v(K_), v(TH), 1.0 / (2 * math.pi), None, M)
        ts(v(K_), v(K_), magic, None, A)
        ts(v(K_), v(K_), -magic, None, A)
        stt(v(RED), v(K_), -c1, v(TH), M, A)
        stt(v(RED), v(K_), -c2, v(RED), M, A)
        stt(v(RED), v(K_), -c3, v(RED), M, A)
        dve.tensor_scalar(v(RED), v(RED), 3.1415925, -3.1415925, ALU.min, ALU.max).then_inc(setup_dve, 1)
        dve.wait_ge(setup_act, 5)
        tt(v(COS), v(SINH), v(SINH), M)
        ts(v(COS), v(COS), -2.0, 1.0, M, A)
        tt(v(AR), v(MAG), v(COS), M)
        tt(v(AI), v(MAG), v(SIN), M)
        tt(v(X1), lr, lr, M)
        tt(v(X2), li, li, M)
        tt(v(DEN), v(X1), v(X2), A)
        own(dve.reciprocal(v(RD), v(DEN)))
        ts(v(X1), v(AR), -1.0, None, A)
        tt(v(ZR), v(X1), lr, M)
        tt(v(X2), v(AI), li, M)
        tt(v(ZR), v(ZR), v(X2), A)
        tt(v(ZR), v(ZR), v(RD), M)
        tt(v(ZI), v(AI), lr, M)
        tt(v(X2), v(X1), li, M)
        tt(v(ZI), v(ZI), v(X2), SB)
        tt(v(ZI), v(ZI), v(RD), M)
        own(dve.memset(pw_re[:, :, 0:1], 1.0))
        own(dve.memset(pw_im[:, :, 0:1], 0.0))
        own(dve.tensor_copy(pw_re[:, :, 1:2], v(AR).unsqueeze(2)))
        own(dve.tensor_copy(pw_im[:, :, 1:2], v(AI).unsqueeze(2)))
        settle()
        t1 = work[2][:, 0:GT * 4].rearrange("p (t m) -> p t m", t=GT)
        t2 = work[2][:, GT * 4:GT * 8].rearrange("p (t m) -> p t m", t=GT)
        for m in (1, 2, 4):
            ar = pw_re[:, :, m:m + 1].to_broadcast([P, GT, m])
            ai = pw_im[:, :, m:m + 1].to_broadcast([P, GT, m])
            pr, pi = pw_re[:, :, 1:m + 1], pw_im[:, :, 1:m + 1]
            nr, ni = pw_re[:, :, m + 1:2 * m + 1], pw_im[:, :, m + 1:2 * m + 1]
            tt(t1[:, :, 0:m], pr, ar, M)
            tt(t2[:, :, 0:m], pi, ai, M)
            tt(nr, t1[:, :, 0:m], t2[:, :, 0:m], SB)
            tt(t1[:, :, 0:m], pr, ai, M)
            tt(t2[:, :, 0:m], pi, ar, M)
            tt(ni, t1[:, :, 0:m], t2[:, :, 0:m], A)
        dve.sem_inc(powers, 1)

        def ada_collect(u):
            a, qt = u // 4, u % 4
            dve.wait_ge(ada_sum, u + 1)
            dve.tensor_tensor(mods[:, a, qt * 6:qt * 6 + 6], bank[7][:, 0:6],
                              pa[:, 32 + a * 24 + qt * 6:32 + a * 24 + qt * 6 + 6], A)\
               .then_inc(mods_part, 1)

        def ada_scale(a, parts):
            dve.wait_ge(mods_part, parts)
            dve.scalar_tensor_tensor(out=mods[:, a, 8:16], in0=mods[:, a, 8:16], scalar=1.0,
                                     in1=pa[:, a * 8:a * 8 + 8], op0=A, op1=M).then_inc(mods_ready, 1)
            dve.wait_ge(mods_ready, a + 1)

        def ada_gate(a, parts):
            dve.wait_ge(mods_part, parts)
            own(dve.tensor_scalar(mods[:, a, 16:24], mods[:, a, 16:24], 1.0, None, A))
            settle()

        ada_steps(4)
        dve.wait_ge(b_in, 32)
        zr = v(ZR).unsqueeze(2).to_broadcast([P, GT, C])
        zi = v(ZI).unsqueeze(2).to_broadcast([P, GT, C])
        w3 = work[2][:, 0:GT * C].rearrange("p (t c) -> p t c", t=GT)
        tt(bz[0][:, :, :], bb[0][:, :, :], zr, M)
        tt(w3, bb[1][:, :, :], zi, M)
        tt(bz[0][:, :, :], bz[0][:, :, :], w3, SB)
        tt(bz[1][:, :, :], bb[1][:, :, :], zr, M)
        tt(w3, bb[0][:, :, :], zi, M)
        tt(bz[1][:, :, :], bz[1][:, :, :], w3, A)
        ada_collect(0)

        def fb(b):
            return b[:, :, :].unsqueeze(2).to_broadcast([P, GT, RUN, C])

        def fp(p):
            return p[:, :, 0:RUN].unsqueeze(3).to_broadcast([P, GT, RUN, C])

        ftmp = f_tmp[:, :, :, :]
        tt(f_re[:, :, :, :], fb(bz[0]), fp(pw_re), M)
        tt(ftmp, fb(bz[1]), fp(pw_im), M)
        tt(f_re[:, :, :, :], f_re[:, :, :, :], ftmp, SB)
        tt(f_im[:, :, :, :], fb(bz[1]), fp(pw_re), M)
        tt(ftmp, fb(bz[0]), fp(pw_im), M)
        dve.tensor_tensor(f_im[:, :, :, :], f_im[:, :, :, :], ftmp, A).then_inc(f_ready, 1)
        for u in range(1, 3):
            ada_steps(8)
            ada_collect(u)
        ada_scale(0, 3)

        def prep(n, q=None):
            dve.wait_ge(hi_ready, n + 1 + (0 if q is None else 8 * q))
            w = 2 * HD + 8 if n == KI else SLOT
            dve.tensor_tensor(w_lo[n % 2][:, :, 0:w], raw[n % 2][:, :, 0:w],
                              w_hi[n % 2][:, :, 0:w].bitcast(F32), SB).then_inc(lo_ready, 1)

        prep(0)
        dve.wait_ge(mats_out, 16)
        dve.wait_ge(d_in, 16)
        tt(skip_d[:, :, :], skip[:, :].unsqueeze(2).to_broadcast([C, G, C]),
           ident[0:C, 0:C].unsqueeze(1).to_broadcast([C, G, C]), M)
        dve.tensor_tensor(kr[:, :, 0:C], kr[:, :, 0:C], skip_d[:, :, :], A).then_inc(kr_ready, 1)
        own(dve.memset(ua[:, :, 0:PAD], 0.0))
        settle()
        dve.sem_inc(ua_pad, 1)

        def modulate(a):
            for k in range(KC):
                dve.wait_ge(xn_ready, 8 * a + k + 1)
                own(dve.tensor_scalar(work[2 + k % 2][:, 0:L], work[k % 2][:, 0:L],
                                      mods[:, a, 8 + k:9 + k], mods[:, a, k:k + 1], M, A))
                settle()
                dve.wait_ge(hh_ready, 8 * a + k + 1)
                dve.tensor_tensor(h_lo[:, k, :], work[2 + k % 2][:, 0:L], h_hi[:, k, :].bitcast(F32), SB)\
                   .then_inc(h_ready, 1)

        modulate(0)
        prep(1)
        ada_steps(4)
        tt(v(X1), v(COS), v(COS), M)
        tt(v(X2), v(SIN), v(SIN), M)
        tt(v(CU), v(X1), v(X2), SB)
        tt(v(SU), v(COS), v(SIN), M)
        ts(v(SU), v(SU), 2.0, None, M)

        def double():
            tt(v(X1), v(CU), v(CU), M)
            tt(v(X2), v(SU), v(SU), M)
            tt(v(SU), v(CU), v(SU), M)
            ts(v(SU), v(SU), 2.0, None, M)
            tt(v(CU), v(X1), v(X2), SB)

        double()
        double()
        own(dve.tensor_copy(v(RC), v(MAG8)))
        keep = small
        dve.wait_ge(kr_ready, 1)
        own(dve.memset(rot_c[:, :, 0:1], 1.0))
        own(dve.memset(rot_s[:, :, 0:1], 0.0))
        own(dve.tensor_copy(keep[:, 16:32], v(MAG8)))
        settle()
        m = 1
        while m < NRUN:
            cu = v(CU).unsqueeze(2).to_broadcast([P, GT, m])
            su = v(SU).unsqueeze(2).to_broadcast([P, GT, m])
            x1 = work[2][:, 0:GT * m].rearrange("p (t m) -> p t m", t=GT)
            x2 = work[3][:, 0:GT * m].rearrange("p (t m) -> p t m", t=GT)
            tt(x1, rot_c[:, :, 0:m], cu, M)
            tt(x2, rot_s[:, :, 0:m], su, M)
            tt(rot_c[:, :, m:2 * m], x1, x2, SB)
            tt(x1, rot_c[:, :, 0:m], su, M)
            tt(x2, rot_s[:, :, 0:m], cu, M)
            tt(rot_s[:, :, m:2 * m], x1, x2, A)
            if 2 * m < NRUN:
                double()
            m *= 2
        dve.sem_inc(rot_ready, 1)
        prep(2)
        ada_steps(4)
        prep(3)
        ada_collect(3)
        ada_gate(0, 4)
        ada_steps(4)
        prep(4)
        ada_steps(4)
        ada_collect(4)
        ada_steps(8)

        def flat(t):
            return t[:, :, :].rearrange("p t k -> p (t k)")

        xr, xi = psum[:, 4 * L:6 * L], psum[:, 6 * L:8 * L]
        dve.wait_ge(inj_ps, 1)
        tt(flat(s_re), xr, flat(rot_c), M)
        tt(flat(s_t1), xi, flat(rot_s), M)
        tt(flat(s_im), xi, flat(rot_c), M)
        tt(flat(s_t2), xr, flat(rot_s), M)
        tt(flat(s_re), flat(s_re), flat(s_t1), A)
        tt(flat(s_im), flat(s_im), flat(s_t2), SB)
        for s_ in (s_re, s_im):
            for t in range(GT):
                own(dve.tensor_tensor_scan(s_[:, t, :], keep[:, 16 + t:17 + t].to_broadcast([P, NRUN]),
                                           s_[:, t, :], 0.0, M, A))
        settle()
        dve.wait_ge(u_out, 64)
        own(dve.memset(b_re[:, :, 0:1], 0.0))
        own(dve.memset(b_im[:, :, 0:1], 0.0))
        tt(flat(s_t1), flat(s_re), flat(rot_c), M)
        tt(flat(s_t2), flat(s_im), flat(rot_s), M)
        tt(b_re[:, :, 1:], s_t1[:, :, 0:NRUN - 1], s_t2[:, :, 0:NRUN - 1], SB)
        tt(flat(s_t1), flat(s_re), flat(rot_s), M)
        tt(flat(s_t2), flat(s_im), flat(rot_c), M)
        dve.tensor_tensor(b_im[:, :, 1:], s_t1[:, :, 0:NRUN - 1], s_t2[:, :, 0:NRUN - 1], A)\
           .then_inc(states, 1)
        for g in range(4):
            dve.wait_ge(cat_hi, g + 1)
            dve.scalar_tensor_tensor(out=h_lo[:, g, :], in0=bank[4 + g], scalar=pb[:, 16 + g:17 + g],
                                     in1=h_hi[:, g, :].bitcast(F32), op0=M, op1=SB).then_inc(cat_ready, 1)
        ada_collect(5)
        ada_steps(8)
        for ct in range(4):
            dve.wait_ge(gelu_hi, ct + 1)
            dve.tensor_tensor(yg_lo[:, ct, :], y_act[:, ct, :], yg_hi[:, ct, :].bitcast(F32), SB)\
               .then_inc(gelu_lo, 1)
        prep(AB_OUT)
        for m in range(4):
            dve.wait_ge(act_drain, drains[first_tile[GLU] + m][1])
            dve.tensor_tensor(cat_f[:, m, :].rearrange("p (k j) -> p j k", j=RUN),
                              gate_t[:, m, :].rearrange("p (j k) -> p j k", j=RUN),
                              y_act[:, m, :].rearrange("p (j k) -> p j k", j=RUN), M).then_inc(cat_mid, 1)
        for m in range(4):
            dve.wait_ge(cat_hi, 4 + m + 1)
            dve.tensor_tensor(h_lo[:, 4 + m, :], cat_f[:, m, :], h_hi[:, 4 + m, :].bitcast(F32), SB)\
               .then_inc(cat_ready, 1)

        def residual(t, k, a, q=None):
            over = 0 if q is None else q
            dve.wait_ge(tile_done, t + 1 + 16 * over)
            dve.scalar_tensor_tensor(out=xT[:, k, :], in0=bank[t % 4], scalar=mods[:, a, 16 + k:17 + k],
                                     in1=xT[:, k, :], op0=M, op1=A).then_inc(dve_drain, 1)

        for i in range(4):
            n = AB_OUT + i
            prep(n + 1)
            if i == 0:
                ada_collect(6)
                ada_scale(1, 7)
            if i < 2:
                ada_steps(4)
            if i == 2:
                ada_collect(7)
                ada_gate(1, 8)
            for r in range(2):
                residual(first_tile[n] + r, 2 * i + r, 0)
        modulate(1)

        def quarter(layer, q, last=False):
            n0, t0 = MLP[layer], first_tile[MLP[layer]]
            a0 = 32 * layer
            for i in range(8):
                if not (last and i == 7):
                    prep(n0 + i + 1, q)
                if layer == 0:
                    for r in range(2):
                        e = 2 * i + r
                        k = e % 8
                        dve.wait_ge(ada_l1[i], 32 * q + 32)
                        src = ada_l1_ring[:, e, :]
                        if k == 0:
                            ins = dve.tensor_scalar(ada_acc[:, :], src, pb[:, 0:1], None, M)
                        else:
                            dve.wait_ge(ada_used, 2 * ADA_STEPS + e + 16 * q)
                            ins = dve.scalar_tensor_tensor(out=ada_acc[:, :], in0=src,
                                                           scalar=pb[:, k:k + 1], in1=ada_acc[:, :],
                                                           op0=M, op1=A)
                        ins.then_inc(ada_used, 1)
                for r in range(2):
                    t = 2 * i + r
                    if i < 4:
                        dve.wait_ge(act_drain, drains[t0 + t][1] + 8 * q)
                        if t >= 1:
                            dve.wait_ge(a_ready, a0 + t + 8 * q)
                        dve.tensor_tensor(work[2][:, 0:L], work[t % 2][:, 0:L], work[t % 2][:, 0:L], M)\
                           .then_inc(sq_ready, 1)
                        dve.wait_ge(sq_ready, a0 + t + 1 + 8 * q)
                        dve.wait_ge(square_done, a0 + t + 1 + 8 * q)
                        dve.tensor_tensor(a_lo[:, t, :], work[2][:, 0:L], a_hi[:, t, :].bitcast(F32), SB)\
                           .then_inc(a_ready, 1)
                    else:
                        if t == 8:
                            dve.wait_ge(sumsq_ready, (KC if layer == 0 else 2 * KC + 8 * QUARTERS) + 8 * q)
                        residual(t0 + t, t - 8, 2 * layer + 1, q)
                if layer == 0 and i % 4 == 3:
                    s = i // 4
                    dve.wait_ge(ada_sum, 8 + s + 1 + 2 * q)
                    dve.tensor_tensor(mods[:, 2 + s, bass.ds(q * 6, 6)], bank[7][:, 0:6],
                                      pa[:, bass.ds(q * 6 + 32 + (2 + s) * 24, 6)], A).then_inc(mods_part, 1)

        with dve.Fori(0, QUARTERS) as q:
            quarter(0, q)
        for a in (2, 3):
            ada_scale(a, 16)
            ada_gate(a, 16)
        modulate(2)

        top8 = small[:, 32:40]

        def block_score(i):
            return score[:, sc_at[i]:sc_at[i] + (i + 1) * P]

        def index_scores():
            cnt = 0
            for i in range(1, NB):
                for h in range(8):
                    dve.wait_ge(idx_rel, cnt + 1)
                    rel, w = work[cnt % 2][:, 0:(i + 1) * P], wi_t[:, i, h:h + 1]
                    if h == 0:
                        ins = dve.tensor_scalar(block_score(i), rel, w, None, M)
                    else:
                        dve.wait_ge(idx_acc, cnt)
                        ins = dve.scalar_tensor_tensor(out=block_score(i), in0=rel, scalar=w,
                                                       in1=block_score(i), op0=M, op1=A)
                    ins.then_inc(idx_acc, 1)
                    cnt += 1
                dve.wait_ge(idx_acc, cnt)
                own(dve.memset(block_score(i)[0:CHUNK, i * P + CHUNK:(i + 1) * P], UNSEEN))
            settle()

        rounds = [(i, r) for i in range(1, NB) for r in range(TOPK // 8)]

        def take_round(i):
            own(dve.max(out=top8, in_=block_score(i)))
            settle()
            own(dve.match_replace(out=block_score(i), in_to_replace=top8, in_values=block_score(i),
                                  imm_value=TAKEN))
            settle()

        def selected_distances():
            dve.wait_ge(l1_consts, 1)
            own(dve.scalar_tensor_tensor(out=dist[:, :], in0=dist[:, :], scalar=-1.0, in1=dist[:, :],
                                         op0=M, op1=ALU.max))
            settle()
            own(dve.tensor_copy(dsel[:, 0:P], dist[:, L - P:L]))
            settle()
            own(dve.memset(dsel[0:CHUNK, CHUNK:P], FAR))
            for i in range(1, NB):
                w = (i + 1) * P
                ts(block_score(i), block_score(i), TAKEN / 2, FAR, ALU.is_gt, M)
                off = L - P - i * P
                tt(dsel[:, sel_at[i]:sel_at[i] + w], block_score(i), dist[:, off:off + w], A)
            dve.sem_inc(dsel_ready, 1)

        for j, (name, half) in enumerate(cd_slots):
            n = CD_IN + j
            prep(n + 1)
            if j == cd_slots.index(("qd", 0)):
                index_scores()
            elif j > cd_slots.index(("qd", 0)):
                for _ in range(5):
                    if rounds:
                        take_round(rounds.pop(0)[0])
        assert not rounds
        selected_distances()

        def out_lo(pair):
            for r, (tile, b) in enumerate(((pair, 7), (4 + pair, 6))):
                dve.wait_ge(cat_hi, 8 + 2 * pair + r + 1)
                dve.tensor_tensor(h_lo[:, tile, :], bank[b], h_hi[:, tile, :].bitcast(F32), SB)\
                   .then_inc(cat_ready, 1)

        def softplus_sum(head):
            dve.wait_ge(z_soft, head + 1)
            dve.scalar_tensor_tensor(out=sp_sb[head % 2][:, :], in0=z_sb[head % 2][:, :], scalar=0.0,
                                     in1=sp_sb[head % 2][:, :], op0=ALU.max, op1=A).then_inc(sp_diag, 1)

        for step in range(H + 1):
            if step == H:
                softplus_sum(step - 1)
            if step < H:
                for i in range(NB):
                    w = (i + 1) * P
                    dve.wait_ge(s_ps, NB * step + i + 1)
                    if step >= 2:
                        dve.wait_ge(t_ps, NB * (step - 2) + i + 1)
                    dve.scalar_tensor_tensor(out=probs(step, i), in0=dsel[:, sel_at[i]:sel_at[i] + w],
                                             scalar=-SLOPES[step], in1=bank[4 + i % 2][:, 0:w],
                                             op0=M, op1=A).then_inc(s_used, 1)
                    dve.wait_ge(s_used, NB * step + i + 1)
                    dve.reduce_max(small[:, i:i + 1], probs(step, i), AX_X, negate=True)\
                       .then_inc(max_ready, 1)
                    if i == 1 and step >= 1:
                        softplus_sum(step - 1)
                z, s_ = z_sb[step % 2], sp_sb[step % 2]
                dve.wait_ge(z_copied, NB * (step + 1))
                dve.scalar_tensor_tensor(out=s_[:, :], in0=z[:, :], scalar=-1.0, in1=z[:, :],
                                         op0=M, op1=ALU.max).then_inc(z_abs, 1)
            if step >= 3 and step % 2 == 1:
                out_lo((step - 3) // 2)
            if step >= 1:
                zp = z_sb[(step - 1) % 2]
                for j in range(NB):
                    dve.wait_ge(r_ps, NB * (step - 1) + j + 1)
                    v_ = zp[:, z_at[j]:z_at[j] + (NB - j) * P]
                    dve.tensor_tensor(v_, v_, bank[2 + j % 2][:, 0:(NB - j) * P], SB).then_inc(r_used, 1)
            if step < H:
                for i in range(NB):
                    dve.wait_ge(p_exp, NB * step + i + 1)
                    own(dve.reciprocal(small[:, 12 + i:13 + i], small[:, 8 + i:9 + i]))
                    settle()
                    dve.tensor_scalar(probs(step, i), probs(step, i), small[:, 12 + i:13 + i], None, M)\
                       .then_inc(p_ready, 1)
        out_lo(H // 2 - 1)

        for i in range(4):
            n = CD_OUT + i
            prep(n + 1)
            for r in range(2):
                residual(first_tile[n] + r, 2 * i + r, 2)
        modulate(3)
        with dve.Fori(0, QUARTERS - 1) as q:
            quarter(1, q)
        quarter(1, QUARTERS - 1, last=True)
        dve.wait_ge(rstd_ready, 5)
        for k in range(KC):
            if k >= 4:
                dve.wait_ge(fin_ps, k - 3)
            dve.scalar_tensor_tensor(out=work[k % 4][:, 0:L], in0=xT[:, k, :], scalar=pb[:, 8 + k:9 + k],
                                     in1=rstd[:, :], op0=M, op1=M).then_inc(fin_t, 1)

    @block.tensor
    def _(pe):
        def mm(o, lhsT, rhs, start, stop, **kw):
            return nc.tensor.matmul(o, lhsT, rhs, start=start, stop=stop, **kw)

        def transpose(o, in_):
            n = in_.shape[0]
            return nc.tensor.transpose(o, in_, ident[0:n, 0:n])

        def product(o, w, x_, first, last):
            (w_h, w_l), (x_h, x_l) = w, x_
            mm(o, w_h, x_h, first, False)
            mm(o, w_h, x_l, False, False)
            return mm(o, w_l, x_h, False, last)

        pe.wait_ge(consts, 2)
        pe.wait_ge(c_in, 16)
        transpose(bank[7][:, 0:KC], raw_c[:, :]).then_inc(c_ps, 1)
        pe.wait_ge(small_in, 16 * 7)
        transpose(bank[4][:, 0:P], raw_a[:, :])
        transpose(bank[4][:, P:P + 48], raw_b[:, :])
        pe.wait_ge(dt_rows, 1)
        transpose(bank[4][:, P + 48:P + 64], raw_dt[:, :])
        pe.wait_ge(cn_in, 16 * 4)
        for ri in range(2):
            for b in range(4):
                last = transpose(bank[5 + ri][:, b * P:(b + 1) * P],
                                 c_nat[ri][:, b, :, :].rearrange("p w s -> p (w s)"))
        last.then_inc(params_ps, 1)
        pe.wait_ge(x_in, 16)

        def x_squares(k):
            if k == 0:
                pe.wait_ge(params, 1)
            pe.wait_ge(x_squared, k + 1)
            mm(bank[6], ones[:, :], sq_x[:, k % 4, :], k == 0, k == KC - 1)\
                .then_inc(norm_sum if k == KC - 1 else norm_part, 1)

        for k in range(KC):
            if k >= 4:
                pe.wait_ge(x_squared, k - 3)
                x_squares(k - 4)
            for b in range(NB):
                last = transpose(bank[k % 4][:, b * P:(b + 1) * P], x_nat[:, b, k * P:(k + 1) * P])
            last.then_inc(xT_ps, 1)
        for k in range(KC - 4, KC):
            x_squares(k)

        def ada_sums(value, unit, q=None):
            if q is not None or unit > 0:
                pe.wait_ge(mods_part, unit)
            pe.wait_ge(ada_used, value)
            for j in range(6):
                last = mm(bank[7][:, j:j + 1], ada_acc[:, j * P:(j + 1) * P], ones[:, 0:1], True, True)
            last.then_inc(ada_sum, 1)

        norms = [1]

        def norm(value):
            pe.wait_ge(sumsq_ready, value)
            pe.wait_ge(rstd_ready, norms[0])
            mm(bank[6], ones[:, :], sumsq[:, :], True, True).then_inc(norm_sum, 1)
            norms[0] += 1

        ada_sums(8, 0)
        pe.wait_ge(f_ready, 1)
        for i in range(8):
            if i >= 2:
                pe.wait_ge(mats_out, i - 1)
            f = (f_re, f_im)[i // 4]
            for r in range(4):
                t = (i % 4) * 4 + r
                last = transpose(bank[4 + i % 2][:, r * P:(r + 1) * P],
                                 f[:, t, :, :].rearrange("p m c -> p (m c)"))
            last.then_inc(mats_ps, 1)
        for u in range(1, 3):
            ada_sums(8 * (u + 1), u)
        pe.wait_ge(g_ready, 1)
        for i in range(8, 16):
            pe.wait_ge(mats_out, i - 1)
            p0 = S * (i % 2)
            for r in range(4):
                t = (i - 8) // 2 * 4 + r
                o = bank[4 + i % 2][0:C, r * P:(r + 1) * P]
                for n_, (b_, g_) in enumerate(((bz[0], g_re), (bz[1], g_ni))):
                    last = mm(o, b_[p0:p0 + S, t, :],
                              g_[p0:p0 + S, t, 0:RUN, :].rearrange("p m c -> p (m c)"), n_ == 0, n_ == 1)
            last.then_inc(mats_ps, 1)

        def slot_ready(n, q=None):
            pe.wait_ge(lo_ready, n + 1 + (0 if q is None else 8 * q))

        def tile_free(t, q=None):
            if t >= 4:
                by_dve, count = drains[t - 4]
                pe.wait_ge(dve_drain if by_dve else act_drain, count + (0 if q is None else 8 * q))

        def weight(n, k, c0, w=P):
            return w_hi[n % 2][:, k, c0:c0 + w], w_lo[n % 2][:, k, c0:c0 + w]

        def h(k, c0=0, w=L):
            return h_hi[:, k, c0:c0 + w], h_lo[:, k, c0:c0 + w]

        def tile(n, t, r, ready, base, q=None, moving=h, first=False):
            tile_free(t, q)
            for k in range(8):
                if first:
                    pe.wait_ge(ready, base + k + 1)
                last = product(bank[t % 4], weight(n, k, r * P), moving(k), k == 0, k == 7)
            last.then_inc(tile_done, 1)

        def plain_slots(n0, count, ready, base):
            for n in range(n0, n0 + count):
                slot_ready(n)
                for r in range(2):
                    tile(n, first_tile[n] + r, r, ready, base, first=n == n0 and r == 0)

        for n in range(AB_IN, GLU):
            plain_slots(n, 1, h_ready, 0)
            if n % 2 == 1:
                ada_sums(8 * (4 + n // 2), 3 + n // 2)

        pe.wait_ge(u_in, 16 * RUN)
        pe.wait_ge(mods_part, 5)
        for g in range(G):
            t, p0 = g // 2, S * (g % 2)
            for e_, b0 in ((e_re, 4), (e_im, 6)):
                o = bank[b0 + t // 8][p0:p0 + S, (t % 8) * NRUN:(t % 8 + 1) * NRUN]
                last = mm(o, e_[:, t, p0:p0 + S], u_run[:, g, :], True, True)
        last.then_inc(inj_ps, 1)
        pe.wait_ge(toep_in, 16 * RUN)
        pe.wait_ge(act_drain, drains[first_tile[GLU] - 1][1])

        def y_at(g):
            t = g // 2
            return bank[g % 2 + t // 8 * 2][:, (t % 8) * NRUN:(t % 8 + 1) * NRUN]

        for g in range(G):
            mm(y_at(g), toep[:, g, :], u_run[:, g, :], g % 16 < 2, False, skip_group_check=True)
        pe.wait_ge(states, 1)
        for g in range(G):
            t, p0 = g // 2, S * (g % 2)
            for g_, b_ in ((g_re, b_re), (g_ni, b_im)):
                last = mm(y_at(g), g_[p0:p0 + S, t, 1:, :].rearrange("p m c -> p (m c)"),
                          b_[p0:p0 + S, t, :], False, g_ is g_ni and g % 16 >= 14, skip_group_check=True)
            if g % 16 >= 14:
                last.then_inc(y_ps, 1)
        pe.wait_ge(poolw_in, 16)
        for g in range(4):
            pe.wait_ge(pooled, g + 1)
            mm(bank[4 + g], pool_w_t[:, g, :], ua[:, g, PAD:], True, True).then_inc(pool_ps, 1)
        pe.wait_ge(cat_ready, 4)
        ada_sums(8 * 6, 5)
        slot_ready(GLU)
        pe.wait_ge(y_copied, 4)
        glu_h = w_hi[GLU % 2][:, :, :].rearrange("p a b -> p (a b)").rearrange("p (k n) -> p k n", k=4)
        glu_l = w_lo[GLU % 2][:, :, :].rearrange("p a b -> p (a b)").rearrange("p (k n) -> p k n", k=4)
        for m in range(4):
            t = first_tile[GLU] + m
            tile_free(t)
            for k in range(4):
                pe.wait_ge(gelu_lo, k + 1)
                last = product(bank[t % 4], (glu_h[:, k, m * P:(m + 1) * P], glu_l[:, k, m * P:(m + 1) * P]),
                               (yg_hi[:, k, :], yg_lo[:, k, :]), k == 0, k == 3)
            last.then_inc(tile_done, 1)
        for i in range(4):
            n = AB_OUT + i
            slot_ready(n)
            for r in range(2):
                tile(n, first_tile[n] + r, r, cat_ready, 0, first=i == 0 and r == 0)
            if i < 2:
                ada_sums(8 * (7 + i), 6 + i)
        norm(KC)

        def a(k):
            return a_hi[:, k, :], a_lo[:, k, :]

        def quarter(layer, q):
            n0, t0 = MLP[layer], first_tile[MLP[layer]]
            a0 = 32 * layer
            for i in range(8):
                slot_ready(n0 + i, q)
                for r in range(2):
                    t = 2 * i + r
                    tile_free(t0 + t, q)
                    for k in range(8):
                        if t == 0:
                            pe.wait_ge(h_ready, 8 * (2 * layer + 1) + k + 1)
                        if t == 8:
                            pe.wait_ge(a_ready, a0 + k + 1 + 8 * q)
                        last = product(bank[(t0 + t) % 4], weight(n0 + i, k, r * P),
                                       h(k) if i < 4 else a(k), k == 0, k == 7)
                    last.then_inc(tile_done, 1)
                if layer == 0 and i % 4 == 3:
                    ada_sums(2 * ADA_STEPS + 8 * (i // 4 + 1) + 16 * q, 8 + i // 4 + 2 * q, q)

        with pe.Fori(0, QUARTERS) as q:
            quarter(0, q)
        norm(KC + 8 * QUARTERS)

        def index_products():
            pe.wait_ge(act_drain, drains[first_tile[KI] + 1][1])
            cnt = 0
            for i in range(1, NB):
                for hh in range(8):
                    if cnt >= 4:
                        pe.wait_ge(idx_rel, cnt - 3)
                    p0 = HD * (hh % 2)
                    mm(bank[4 + cnt % 4][:, 0:(i + 1) * P], qi_t[p0:p0 + HD, hh // 2, i * P:(i + 1) * P],
                       ki_t[p0:p0 + HD, 0:(i + 1) * P], True, True).then_inc(idx_ps, 1)
                    cnt += 1
            pe.wait_ge(idx_rel, cnt)

        for j, (name, half) in enumerate(cd_slots):
            n = CD_IN + j
            slot_ready(n)
            t0 = first_tile[n]
            if name == "ki":
                tile(n, t0, 0, h_ready, 16)
                tile_free(t0 + 1)
                for b in range(NB):
                    for k in range(8):
                        last = product(bank[(t0 + 1) % 4][:, b * 8:(b + 1) * 8], h(k, b * P, P),
                                       weight(n, k, P, 8), k == 0, k == 7)
                last.then_inc(tile_done, 1)
            elif name in ("vd", "vc"):
                for b in range(NB):
                    tile_free(t0 + b)
                    for k in range(8):
                        last = product(bank[(t0 + b) % 4][:, 0:SLOT], h(k, b * P, P),
                                       weight(n, k, 0, SLOT), k == 0, k == 7)
                    last.then_inc(tile_done, 1)
            else:
                for r in range(2):
                    tile(n, t0 + r, r, h_ready, 16, first=j == 0 and r == 0)
            if name == "qd" and half == 0:
                index_products()

        def dsa_cat(pair):
            return 8 + 2 * pair + 1

        def stick_cat(pair):
            return 8 + 2 * pair + 2

        qd, kd, vd, qc, kc, vc = (qk[x_] for x_ in ("qd", "kd", "vd", "qc", "kc", "vc"))
        pe.wait_ge(act_drain, drains[first_tile[CD_OUT] - 1][1])
        for step in range(H + 1):
            p0 = HD * (step % 2)
            pr = step - 1
            po = HD * (pr % 2)
            if step < H:
                for i in range(NB):
                    if step >= 2 and i < 2:
                        pe.wait_ge(t_copied, NB * (step - 2) + i + 3)
                    elif step or i >= 2:
                        pe.wait_ge(s_used, NB * step + i - 1)
                    mm(bank[4 + i % 2][:, 0:(i + 1) * P], qc[p0:p0 + HD, step // 2, i * P:(i + 1) * P],
                       kc[p0:p0 + HD, step // 2, 0:(i + 1) * P], True, True).then_inc(s_ps, 1)
                for j in range(NB):
                    if step or j >= 2:
                        pe.wait_ge(z_copied, NB * step + j - 1)
                    mm(bank[j % 2][:, 0:(NB - j) * P], kd[p0:p0 + HD, step // 2, j * P:(j + 1) * P],
                       qd[p0:p0 + HD, step // 2, j * P:], True, True).then_inc(z_ps, 1)
            if step >= 1:
                for i in range(NB):
                    pe.wait_ge(p_ready, NB * pr + i + 1)
                    if step < H and i < 2:
                        pe.wait_ge(s_used, NB * step + i + 3)
                    else:
                        pe.wait_ge(t_copied, NB * pr + i - 1)
                    for j in range(i + 1):
                        last = transpose(bank[4 + i % 2][:, j * P:(j + 1) * P], probs(pr, i)[:, j * P:(j + 1) * P])
                    last.then_inc(t_ps, 1)
                s_, z = sp_sb[pr % 2], z_sb[pr % 2]
                pe.wait_ge(sp_ready, NB * step)
                for j in range(NB):
                    if pr or j >= 2:
                        pe.wait_ge(r_used, NB * pr + j - 1)
                    o = bank[2 + j % 2]
                    w = (NB - j) * P
                    last = mm(o[:, 0:w], tri[:, :], s_[:, z_at[j]:z_at[j] + w], True, j == NB - 1)
                    for j2 in range(j + 1, NB):
                        w2 = (NB - j2) * P
                        last = mm(o[:, w - w2:w], ones[:, :], s_[:, z_at[j2]:z_at[j2] + w2], False,
                                  j2 == NB - 1)
                    last.then_inc(r_ps, 1)
                if pr >= 2 and pr % 2 == 0:
                    pe.wait_ge(cat_ready, dsa_cat(pr // 2 - 1))
                pe.wait_ge(t_copied, NB * (pr + 1))
                for j in range(NB):
                    last = mm(bank[7][po:po + HD, j * P:], vc[:, j, pr * HD:(pr + 1) * HD],
                              pT[:, j, j * P:], j == 0, j == NB - 1)
                last.then_inc(oc_ps, 1)
                if pr >= 2 and pr % 2 == 0:
                    pe.wait_ge(cat_ready, stick_cat(pr // 2 - 1))
                for j in range(NB):
                    pe.wait_ge(w_ready, NB * pr + j + 1)
                    last = mm(bank[6][po:po + HD, j * P:], vd[:, j, pr * HD:(pr + 1) * HD],
                              z[:, z_at[j]:z_at[j] + (NB - j) * P], j == 0, j == NB - 1)
                last.then_inc(o_ps, 1)
        pe.wait_ge(cat_ready, 16)
        plain_slots(CD_OUT, 4, cat_ready, 8)
        norm(2 * KC + 8 * QUARTERS)
        with pe.Fori(0, QUARTERS) as q:
            quarter(1, q)
        norm(2 * KC + 16 * QUARTERS)
        for k in range(KC):
            pe.wait_ge(fin_t, k + 1)
            if k >= 4:
                pe.wait_ge(fin_copied, k - 3)
            for b in range(NB):
                last = transpose(bank[k % 4][:, b * P:(b + 1) * P], work[k % 4][:, b * P:(b + 1) * P])
            last.then_inc(fin_ps, 1)

    block.__exit__(None, None, None)


INPUTS = ["x", "c", "norm_g", "ada_w", "ada_b", "mlp_w1", "mlp_w2", "ab_w_in", "ab_w_out", "pool_w",
          "pool_scale", "ssm_lam_re", "ssm_lam_im", "ssm_log_dt", "ssm_b_re", "ssm_b_im", "ssm_c_re",
          "ssm_c_im", "ssm_d", "glu_w", "glu_b", "cd_w_in", "cd_w_out", "final_g"]


def kernel(**inputs):
    import numpy as np
    import concourse.bacc as bacc
    from concourse.bass_utils import run_bass_kernel_spmd

    nc = bacc.Bacc("TRN2", target_bir_lowering=False, num_devices=1)
    arrays, args = {}, []
    for name in INPUTS:
        a = np.ascontiguousarray(inputs[name])
        arrays[f"in_{name}"] = a
        args.append(nc.dram_tensor(f"in_{name}", a.shape, mybir.dt.from_np(a.dtype),
                                   kind="ExternalInput").ap())
    out = nc.dram_tensor("out", (1, L, D), F32, kind="ExternalOutput")
    trunk(nc, *args, out.ap())
    r = run_bass_kernel_spmd(nc, [arrays], core_ids=[0])
    return r.results[0]["out"]
```

```python
import math

import concourse.bass as bass
from concourse import mybir

ALU = mybir.AluOpType
ACT = mybir.ActivationFunctionType
F32 = mybir.dt.float32
F32R = mybir.dt.float32r
I32 = mybir.dt.int32
AX_X = mybir.AxisListType.X

P = 128
D = 1024
L = 512
KC = D // P
NB = L // P
FF = 4 * D
SQ = KC - 1
SLOT = 256
QUARTERS = 4
QT = FF // QUARTERS // P
EPS = 1e-6
CHUNK = 64
HALF = D // 2

G, S, C = 32, 64, 16
RUN = P // C
NRUN = L // RUN
GT = G // 2
WINDOWS = (2, 4, 8, 16)
PAD = 16

H, HD = 8, 64
TOPK = 128
IDX_SCALE = (8 ** -0.5) * (64 ** -0.5)
SLOPES = [2.0 ** (-8.0 * (h + 1) / H) for h in range(H)]
UNSEEN = -1.0e30
TAKEN = -3.0e38
FAR = 1.0e30
ADA_Q = 3 * D // 4
ADA_RING = 3
ADA_FIRST = 10


def trunk(nc, x, c, norm_g, ada_w, ada_b, mlp_w1, mlp_w2, ab_w_in, ab_w_out, pool_w, pool_scale,
          ssm_lam_re, ssm_lam_im, ssm_log_dt, ssm_b_re, ssm_b_im, ssm_c_re, ssm_c_im, ssm_d,
          glu_w, glu_b, cd_w_in, cd_w_out, final_g, out):

    cursor = [(nc.sbuf_base + 63) // 64 * 64]

    def place(name, shape, dt=F32, offset=None):
        size = 4 * math.prod(shape[1:])
        if offset is None:
            offset = cursor[0]
            cursor[0] += (size + 31) // 32 * 32
        return nc.alloc_sbuf_tensor_at(name, shape, dt, offset=offset)

    xT = place("xT", [P, KC, L])
    h_at = cursor[0]
    h_hi = place("h_hi", [P, KC, L], F32R)
    h_lo = place("h_lo", [P, KC, L], F32R)
    raw = [place(f"w_raw{i}", [P, 8, SLOT]) for i in range(2)]
    w_at = cursor[0]
    w_hi = [place(f"w_hi{i}", [P, 8, SLOT], F32R) for i in range(2)]
    w_lo = [place(f"w_lo{i}", [P, 8, SLOT], F32R) for i in range(2)]
    ada_ring_at = cursor[0]
    ada_ring = place("ada_ring", [P, ADA_RING, ADA_Q])
    ada_acc = place("ada_acc", [P, ADA_Q])
    ident = place("ident", [P, P])
    ones = place("ones", [P, P])
    pa = place("pa", [P, P])
    pb = place("pb", [P, 72])
    mods = place("mods", [P, 4, 24])
    eps_t = place("eps_t", [P, 8])
    recip = place("recip", [P, PAD])
    small = place("small", [P, 64])
    wi_t = place("wi_t", [P, NB, 8])
    work = [place(f"work{i}", [P, L + PAD]) for i in range(2)]
    work_b_at = cursor[0]
    work += [place(f"work{i}", [P, L + PAD]) for i in (2, 3)]
    ada_acc_b = place("ada_acc_b", [P, ADA_Q], F32, offset=work_b_at)
    sumsq = place("sumsq", [P, L])
    sm = place("sm", [P, 32, GT], F32, offset=cursor[0] - 4 * L)
    rstd = place("rstd", [P, L])
    pool_w_t = place("pool_w_t", [P, 4, P])
    arena = cursor[0]

    def lay(at, name, shape, dt=F32):
        t = place(name, shape, dt, offset=at[0])
        at[0] += (4 * math.prod(shape[1:]) + 31) // 32 * 32
        return t

    ada_first = place("ada_first", [P, ADA_FIRST, ADA_Q], F32, offset=w_at)
    at = [h_at]
    x_nat = lay(at, "x_nat", [P, NB, D])
    g_tmp = lay(at, "g_tmp", [P, GT, RUN + 1, C])
    raw_a = lay(at, "raw_a", [P, P])
    raw_c = lay(at, "raw_c", [KC, P])
    raw_b = lay(at, "raw_b", [48, P])
    raw_dt2 = lay(at, "raw_dt2", [GT, 2])
    raw_dt = lay(at, "raw_dt", [GT, P])
    c_nat = [lay(at, f"c_nat{i}", [P, 4, 2, S]) for i in range(2)]
    assert at[0] <= h_at + 2 * 4 * KC * L
    at = [arena]
    f_at = arena
    f_re = lay(at, "f_re", [P, GT, RUN, C])
    f_im = lay(at, "f_im", [P, GT, RUN, C])
    at[0] += 512
    g_re = lay(at, "g_re", [P, GT, RUN + 1, C])
    g_ni = lay(at, "g_ni", [P, GT, RUN + 1, C])
    toep = lay(at, "toep", [P, G, P])
    e_at = at[0]
    e_re = lay(at, "e_re", [P, GT, P])
    e_im = lay(at, "e_im", [P, GT, P])
    u_at = at[0]
    u_run = lay(at, "u_run", [P, G, NRUN])
    rot_c = lay(at, "rot_c", [P, GT, NRUN])
    rot_s = lay(at, "rot_s", [P, GT, NRUN])
    assert at[0] <= nc.sbuf_usable_end, (at[0], nc.sbuf_usable_end)
    at = [f_at]
    ub = lay(at, "ub", [P, 4, RUN, NRUN])
    kr = place("kr", [2 * C, GT, P], F32, offset=at[0])
    ua = lay(at, "ua", [P, 4, L + PAD])
    at = [f_at]
    b_re = lay(at, "b_re", [P, GT, 2, NRUN])
    b_im = place("b_im", [P, GT, 2, NRUN], F32, offset=h_at + 4 * KC * L + 2 * KC * L)
    y_act = place("y_act", [P, 4, L], F32, offset=f_at)
    at = [e_at]
    s_re = lay(at, "s_re", [P, GT, NRUN])
    s_im = lay(at, "s_im", [P, GT, NRUN])
    s_t1 = lay(at, "s_t1", [P, GT, NRUN])
    s_t2 = lay(at, "s_t2", [P, GT, NRUN])
    sq_x = place("sq_x", [P, 4, L], F32, offset=e_at + 8192)
    f_tmp = place("f_tmp", [P, GT, RUN, C], F32, offset=e_at)
    y_run = place("y_run", [P, G, NRUN], F32, offset=e_at)
    at = [e_at]
    yg_hi = lay(at, "yg_hi", [P, 4, L], F32R)
    yg_lo = lay(at, "yg_lo", [P, 4, L], F32R)
    y_t = place("y_t", [P, 4, L], F32, offset=u_at)
    gate_t = place("gate_t", [P, 4, L], F32, offset=u_at)
    cat_f = place("cat_f", [P, 4, L], F32, offset=u_at + 8192)
    at = [u_at]
    pw_re = lay(at, "pw_re", [P, GT, RUN + 1])
    pw_im = lay(at, "pw_im", [P, GT, RUN + 1])
    pw_ni = lay(at, "pw_ni", [P, GT, RUN + 1])
    cb = [lay(at, f"cb{i}", [P, GT, C]) for i in range(2)]
    bb = [lay(at, f"bb{i}", [P, GT, C]) for i in range(2)]
    assert at[0] <= u_at + 8192
    at = [u_at + 8192]
    bz = [lay(at, f"bz{i}", [P, GT, C]) for i in range(2)]
    bd = [lay(at, f"bd{i}", [P, GT, 2 * C]) for i in range(2)]
    skip = lay(at, "skip", [2 * C, GT])
    fold = lay(at, "fold", [2 * C, C])
    skip_d = lay(at, "skip_d", [2 * C, GT, C])
    assert at[0] <= u_at + 16384
    at = [arena]
    a_hi = lay(at, "a_hi", [P, QT, L], F32R)
    a_lo = lay(at, "a_lo", [P, QT, L], F32R)
    ada_l1_ring = lay(at, "ada_l1_ring", [P, 16, ADA_Q])
    assert at[0] <= nc.sbuf_usable_end, (at[0], nc.sbuf_usable_end)
    at = [arena]
    qk = {}
    for name in ("qd", "kd", "vd", "qc", "kc", "vc"):
        qk[name] = lay(at, name, [P, 4, L])
    sel_at = [0, P, P + 2 * P, P + 2 * P + 3 * P]
    dsel = lay(at, "dsel", [P, sum((i + 1) * P for i in range(NB))])
    tri = lay(at, "tri", [P, P])
    idx_at = at[0]
    qi_t = lay(at, "qi_t", [P, 4, L])
    ki_t = lay(at, "ki_t", [P, L])
    dist = lay(at, "dist", [P, L])
    sc_at = [0, 0, 2 * P, 5 * P]
    score = lay(at, "score", [P, 9 * P])
    at = [idx_at]
    W1 = sum((NB - j) * P for j in range(NB))
    z_at = [0, 4 * P, 7 * P, 9 * P]
    z_sb = [lay(at, f"z_sb{i}", [P, W1]) for i in range(2)]
    sp_sb = [lay(at, f"sp_sb{i}", [P, W1]) for i in range(2)]
    pT = lay(at, "pT", [P, NB, L])
    assert at[0] <= nc.sbuf_usable_end, (at[0], nc.sbuf_usable_end)
    p_at = [0, P, 3 * P, 6 * P]
    wi_row = place("wi_row", [8, L], F32, offset=ada_ring_at)
    probs_b = place("probs_b", [P, 10 * P], F32, offset=ada_ring_at)

    def probs(step, i):
        if step % 2:
            return probs_b[:, p_at[i]:p_at[i] + (i + 1) * P]
        return work[i][:, 0:(i + 1) * P]

    y_out = place("y_out", [P, NB, D], F32, offset=arena)

    psum = nc.alloc_psum_tensor("psum", [P, 8 * L], F32)
    bank = [psum[:, i * L:(i + 1) * L] for i in range(8)]

    u_dram = nc.dram_tensor("u_scratch", (HALF, L), F32, kind="Internal").ap()
    y_dram = nc.dram_tensor("y_scratch", (HALF, L), F32, kind="Internal").ap()

    def sem(name):
        return nc.alloc_semaphore(name)

    def cols(w, c0, n=SLOT):
        return w.rearrange("(k p) n -> p k n", p=P)[:, :, c0:c0 + n]

    slots = []
    AB_IN = len(slots)
    slots += [cols(ab_w_in[0], c0) for c0 in (HALF, HALF + SLOT, 0, SLOT)]
    GLU = len(slots)
    slots += [glu_w[0].rearrange("(k p) n -> p k n", p=P)]
    AB_OUT = len(slots)
    slots += [cols(ab_w_out[0], c0) for c0 in range(0, D, SLOT)]
    MLP = [len(slots)]
    slots += [None] * (8 * QUARTERS)
    CD_IN = len(slots)
    CD = dict(qc=0, kc=512, vc=1024, qi=1536, ki=2048, wi=2112, qd=2120, kd=2632, vd=3144)
    cd_order = ["qi", "ki", "qd", "kd", "vd", "qc", "kc", "vc"]
    cd_slots = []
    for name in cd_order:
        for half in range(1 if name == "ki" else 2):
            cd_slots.append((name, half))
            slots.append(None if name == "ki" else cols(cd_w_in[0], CD[name] + half * SLOT))
    KI = CD_IN + cd_slots.index(("ki", 0))
    CD_OUT = len(slots)
    slots += [cols(cd_w_out[0], c0) for c0 in range(0, D, SLOT)]
    MLP.append(len(slots))
    slots += [None] * (8 * QUARTERS)
    NSLOT = len(slots)

    INDEX = [(i, h) for i in range(1, NB) for h in range(8)]
    INDEX_GROUP = 4
    index_first = CD_IN + cd_slots.index(("qd", 0))

    def index_group(n, r):
        at_ = 2 * (n - index_first) + r
        if at_ < 0:
            return range(0)
        return range(min(at_ * INDEX_GROUP, len(INDEX)), min((at_ + 1) * INDEX_GROUP, len(INDEX)))

    landed = []
    total = [0, 0]
    for n in range(NSLOT):
        total[n % 2] += 48 if n == KI else 16
        landed.append(total[n % 2])

    tiles_of = {n: 2 for n in range(NSLOT)}
    tiles_of[GLU] = 4
    for i, (name, _) in enumerate(cd_slots):
        if name in ("vd", "vc"):
            tiles_of[CD_IN + i] = NB
    first_tile, drains = [], []
    drained = {False: 0, True: 0}
    for n in range(NSLOT):
        first_tile.append(len(drains))
        for _ in range(tiles_of[n]):
            by_dve = AB_OUT <= n < AB_OUT + 4 or CD_OUT <= n < CD_OUT + 4 or \
                any(m <= n < m + 32 and (n - m) % 8 >= 4 for m in MLP)
            drained[by_dve] += 1
            drains.append((by_dve, drained[by_dve]))

    raw_in = [sem("raw_in0"), sem("raw_in1")]
    hi_ready = sem("w_hi_ready")
    lo_ready = sem("w_lo_ready")
    tile_done = sem("tile_done")
    act_drain = sem("act_drained")
    dve_drain = sem("dve_drained")
    square_done = sem("square_done")
    a_ready = sem("a_ready")
    sumsq_ready = sem("sumsq_ready")
    last_square = sem("last_square")
    norm_part = sem("norm_part")
    norm_sum = sem("norm_sum")
    rstd_ready = sem("rstd_ready")
    xn_ready = sem("xn_ready")
    hh_ready = sem("h_hi_ready")
    h_ready = sem("h_ready")
    ada_in = [sem(f"ada_in{i}") for i in range(ADA_RING)]
    ada_in0 = [sem(f"ada_first_in{i}") for i in range(ADA_FIRST)]
    ada_used = sem("ada_used")
    ada_used_pe = sem("ada_used_pe")
    ada_sum = sem("ada_sum")
    mods_part = sem("mods_part")
    mods_ready = sem("mods_ready")
    small_in = sem("small_in")
    b_in = sem("b_in")
    d_in = sem("d_in")
    dt_in = sem("dt_in")
    dt_rows = sem("dt_rows")
    poolw_in = sem("poolw_in")
    x_in = sem("x_in")
    consts = sem("consts")
    params_ps = sem("params_ps")
    params = sem("params")
    xT_ps = sem("xT_ps")
    act_own = sem("act_own")
    act_n = [0]
    dve_own = sem("dve_own")
    dve_n = [0]
    pool_own = sem("pool_own")
    pool_n = [0]
    setup_act = sem("setup_act")
    setup_dve = sem("setup_dve")
    powers = sem("powers")
    c_ready = sem("c_ready")
    bd_ready = sem("bd_ready")
    g_ready = sem("g_ready")
    f_ready = sem("f_ready")
    mats_ps = sem("mats_ps")
    mats_out = sem("mats_out")
    kr_ready = sem("kr_ready")
    toep_zero = sem("toep_zero")
    toep_in = sem("toep_in")
    u_out = sem("u_out")
    ada_l1 = [sem(f"ada_l1_in{i}") for i in range(8)]
    c_in = sem("c_in")
    c_ps = sem("c_ps")
    cn_in = sem("cn_in")
    x_squared = sem("x_squared")
    sq_ready = sem("sq_ready")
    u_in = sem("u_in")
    ua_pad = sem("ua_pad")
    pooled = sem("pooled")
    pool_ps = sem("pool_ps")
    inj_ps = sem("inj_ps")
    inj_read = sem("inj_read")
    states = sem("states")
    y_ps = sem("y_ps")
    y_copied = sem("y_copied")
    y_out_s = [sem(f"y_out{i}") for i in range(2)]
    y_in = [sem(f"y_in{i}") for i in range(2)]
    gelu_hi = sem("gelu_hi")
    gelu_lo = sem("gelu_lo")
    cat_mid = sem("cat_mid")
    cat_hi = sem("cat_hi")
    cat_ready = sem("cat_ready")
    l1_consts = sem("l1_consts")
    wi_ps = sem("wi_ps")
    wi_ready = sem("wi_ready")
    idx_ps = sem("idx_ps")
    idx_rel = sem("idx_rel")
    idx_acc = sem("idx_acc")
    dsel_ready = sem("dsel_ready")
    z_ps = sem("z_ps")
    z_copied = sem("z_copied")
    z_abs = sem("z_abs")
    z_soft = sem("z_soft")
    sp_diag = sem("sp_diag")
    sp_ready = sem("sp_ready")
    r_ps = sem("r_ps")
    r_used = sem("r_used")
    w_exp = sem("w_exp")
    w_ready = sem("w_ready")
    o_ps = sem("o_ps")
    s_ps = sem("s_ps")
    s_used = sem("s_used")
    max_ready = sem("max_ready")
    p_exp = sem("p_exp")
    p_ready = sem("p_ready")
    t_ps = sem("t_ps")
    t_copied = sem("t_copied")
    oc_ps = sem("oc_ps")
    fin_t = sem("fin_t")
    fin_ps = sem("fin_ps")
    fin_copied = sem("fin_copied")
    out_done = sem("out_done")

    def w1_src(layer, q, i):
        return mlp_w1[layer].rearrange("(k p) n -> p k n", p=P)[
            :, :, bass.ds(q * (FF // QUARTERS) + i * SLOT, SLOT)]

    def w2_src(layer, q, i):
        v = mlp_w2[layer].rearrange("(k p) n -> p k n", p=P)
        return v[:, bass.ds(q * QT, QT), i * SLOT:(i + 1) * SLOT]

    ADA_STEPS = 8 * 4
    ADA_EARLY = 8 * 3
    ADA_PE = 8

    def ada_src(a, qt, k):
        return ada_w[a // 2, a % 2, k * P:(k + 1) * P, bass.ds(qt * ADA_Q, ADA_Q)]

    block = nc.Block()
    block.__enter__()

    @block.sync
    def _(sp):
        def rows(v):
            return v.rearrange("(r c) -> r c", c=P)

        sp.dma_start(raw_b[16:32, :], ssm_lam_re[0].rearrange("(t g) p -> t (g p)", g=2)).then_inc(small_in, 16)
        sp.dma_start(raw_b[32:48, :], ssm_lam_im[0].rearrange("(t g) p -> t (g p)", g=2)).then_inc(small_in, 16)
        sp.dma_start(raw_b[0:8, :], rows(final_g)).then_inc(small_in, 16)
        sp.dma_start(raw_b[8:12, :], rows(pool_scale[0])).then_inc(small_in, 16)
        sp.dma_start(raw_b[12:16, :], rows(glu_b[0])).then_inc(small_in, 16)

        def load(n, src, q=None):
            if n >= 2:
                sp.wait_ge(lo_ready, n - 1 + (0 if q is None else 8 * q))
            dst = raw[n % 2][:, :, :]
            if n == GLU:
                dst = dst.rearrange("p a b -> p (a b)").rearrange("p (k n) -> p k n", k=4)
            sp.dma_start(dst, src).then_inc(raw_in[n % 2], 16)

        def load_ada(e):
            u = e // 8
            if e < ADA_EARLY:
                r, buf, signal = ADA_FIRST, ada_first, ada_in0
            else:
                r, buf, signal = ADA_RING, ada_ring, ada_in
            at_ = e if e < ADA_EARLY else e - ADA_EARLY
            if at_ >= r:
                if e - r < ADA_PE:
                    sp.wait_ge(ada_used_pe, e - r + 1)
                else:
                    sp.wait_ge(ada_used, e - r + 1 - ADA_PE)
            sp.dma_start(buf[:, at_ % r, :], ada_src(u // 4, u % 4, e % 8)).then_inc(signal[at_ % r], 16)

        ada_next = [0]

        def more_ada(count):
            for _ in range(count):
                load_ada(ada_next[0])
                ada_next[0] += 1

        more_ada(2)
        sp.dma_start(x_nat[:, :, :], x[0].rearrange("(t p) d -> p t d", p=P)).then_inc(x_in, 16)
        more_ada(12)
        load(0, slots[0])
        more_ada(ADA_EARLY - 14)
        load(1, slots[1])
        load(2, slots[2])
        sp.wait_ge(kr_ready, 1)
        sp.wait_ge(toep_zero, 1)
        for m in range(RUN):
            for g2 in range(2):
                sp.dma_start(
                    toep[m * C:(m + 1) * C, :, :].rearrange("c (t g) n -> c g t n", g=2)[
                        :, g2, :, (RUN - 1 - m) * C:],
                    kr[g2 * C:(g2 + 1) * C, :, 0:(m + 1) * C]).then_inc(toep_in, 16)
        load(3, slots[3])
        more_ada(ADA_RING)
        more_ada(8 - ADA_RING)
        load(GLU, slots[GLU])
        load(AB_OUT, slots[AB_OUT])
        more_ada(16)
        load(AB_OUT + 1, slots[AB_OUT + 1])
        more_ada(4)
        load(AB_OUT + 2, slots[AB_OUT + 2])
        more_ada(8)
        load(AB_OUT + 3, slots[AB_OUT + 3])
        more_ada(4)
        assert ada_next[0] == 2 * ADA_STEPS
        sp.wait_ge(cat_ready, 8)

        def quarter(layer, q):
            n0 = MLP[layer]
            for i in range(8):
                load(n0 + i, w1_src(layer, q, i) if i < 4 else w2_src(layer, q, i - 4), q)
                if layer == 0:
                    for e in (2 * i, 2 * i + 1):
                        sp.wait_ge(ada_used, 2 * ADA_STEPS - ADA_PE - 16 + e + 1 + 16 * q)
                        sp.dma_start(ada_l1_ring[:, e, :], ada_src(2 + e // 8, q, e % 8))\
                          .then_inc(ada_l1[i], 16)

        with sp.Fori(0, QUARTERS) as q:
            quarter(0, q)
        for n in range(CD_IN, MLP[1]):
            if n == KI:
                sp.wait_ge(lo_ready, n - 1)
                for c0, src, w in ((0, CD["ki"], HD), (HD, CD["ki"], HD), (2 * HD, CD["wi"], 8)):
                    sp.dma_start(raw[n % 2][:, :, c0:c0 + w], cols(cd_w_in[0], src, w))\
                      .then_inc(raw_in[n % 2], 16)
            else:
                load(n, slots[n])
        with sp.Fori(0, QUARTERS) as q:
            quarter(1, q)
        for k in range(KC):
            sp.wait_ge(fin_copied, k + 1)
            sp.dma_start(out[0].rearrange("(t p) d -> p t d", p=P)[:, :, k * P:(k + 1) * P],
                         y_out[:, :, k * P:(k + 1) * P]).then_inc(out_done, 16)
        sp.wait_ge(out_done, 16 * KC)

    @block.gpsimd
    def _(pool):
        def own(ins):
            pool_n[0] += 1
            ins.then_inc(pool_own, 1)

        def settle():
            pool.wait_ge(pool_own, pool_n[0])

        own(pool.memset(ident[:, :], 0.0))
        own(pool.memset(ones[:, :], 1.0))
        settle()
        pool.affine_select(out=ident[:, :], in_=ident[:, :], compare_op=ALU.not_equal, fill=1.0,
                           base=0, pattern=[[-1, P]], channel_multiplier=1).then_inc(consts, 1)
        own(pool.iota(small[:, 0:PAD].bitcast(I32), pattern=[[1, PAD]], base=1, channel_multiplier=0))
        settle()
        pool.tensor_copy(recip[:, :], small[:, 0:PAD].bitcast(I32)).then_inc(consts, 1)
        pool.memset(toep[:, :, :], 0.0).then_inc(toep_zero, 1)

        squares = [0]

        def square_tile(k, wait):
            wait()
            if squares[0]:
                pool.wait_ge(sumsq_ready, squares[0])
            if k == 0:
                ins = pool.tensor_tensor(sumsq[:, :], xT[:, k, :], xT[:, k, :], ALU.mult)
            else:
                own(pool.tensor_tensor(work[3][:, 0:L], xT[:, k, :], xT[:, k, :], ALU.mult))
                settle()
                ins = pool.tensor_tensor(sumsq[:, :], sumsq[:, :], work[3][:, 0:L], ALU.add)
            ins.then_inc(sumsq_ready, 1)
            squares[0] += 1

        pool.wait_ge(powers, 1)
        pool.wait_ge(c_ready, 1)

        def bc(c_t):
            return c_t[:, :, :].unsqueeze(2).to_broadcast([P, GT, RUN + 1, C])

        def bp(p_t):
            return p_t[:, :, :].unsqueeze(3).to_broadcast([P, GT, RUN + 1, C])

        def tt(o, a, b, op):
            own(pool.tensor_tensor(o, a, b, op))
            settle()

        tt(g_re[:, :, :, :], bc(cb[0]), bp(pw_re), ALU.mult)
        tt(g_tmp[:, :, :, :], bc(cb[1]), bp(pw_ni), ALU.mult)
        tt(g_re[:, :, :, :], g_re[:, :, :, :], g_tmp[:, :, :, :], ALU.add)
        tt(g_ni[:, :, :, :], bc(cb[0]), bp(pw_ni), ALU.mult)
        tt(g_tmp[:, :, :, :], bc(cb[1]), bp(pw_re), ALU.mult)
        pool.tensor_tensor(g_ni[:, :, :, :], g_ni[:, :, :, :], g_tmp[:, :, :, :], ALU.subtract)\
            .then_inc(g_ready, 1)

        norms = [0]

        def normalise():
            norms[0] += 1
            pool.wait_ge(rstd_ready, norms[0])
            for k in range(KC):
                if k >= 2:
                    pool.wait_ge(h_ready, 8 * (norms[0] - 1) + k - 1)
                pool.tensor_tensor(work[k % 2][:, 0:L], xT[:, k, :], rstd[:, :], ALU.mult)\
                    .then_inc(xn_ready, 1)

        normalise()

        for w in (0, 1):
            pool.wait_ge(h_ready, 8)
            own(pool.memset(work[w][:, 0:PAD], 0.0))
        pool.wait_ge(ua_pad, 1)
        for ct in range(4):
            pool.wait_ge(act_drain, drains[first_tile[AB_IN + 2] + ct][1])
            if ct:
                pool.wait_ge(pooled, ct)
            u = ua[:, ct, :]
            src, step = u, 1
            for r in range(ct + 1):
                settle()
                dst = work[r % 2][:, :]
                own(pool.tensor_tensor(dst[:, PAD:], src[:, PAD:], src[:, PAD - step:PAD + L - step],
                                       ALU.add))
                src, step = dst, 2 * step
            win = WINDOWS[ct]
            settle()
            own(pool.tensor_tensor(src[:, PAD:PAD + win], src[:, PAD:PAD + win], recip[:, 0:win],
                                   ALU.mult))
            own(pool.tensor_scalar(src[:, PAD + win:], src[:, PAD + win:], 1.0 / win, None, ALU.mult))
            settle()
            pool.tensor_tensor(u[:, PAD:], src[:, PAD:], u[:, PAD:], ALU.subtract).then_inc(pooled, 1)

        for k in range(SQ):
            d = drains[first_tile[AB_OUT] + k]
            square_tile(k, lambda: pool.wait_ge(dve_drain, d[1]))
        normalise()

        def quarter(layer, q):
            t0 = first_tile[MLP[layer]]
            base_sq, base_own = squares[0], pool_n[0]
            for i in range(8):
                if i >= 4:
                    for r in range(2):
                        k = (i - 4) * 2 + r
                        if k == SQ:
                            continue
                        pool.wait_ge(dve_drain, drains[t0 + 8 + k][1] + 8 * q)
                        pool.wait_ge(sumsq_ready, base_sq + k + SQ * q)
                        if k == 0:
                            ins = pool.tensor_tensor(sumsq[:, :], xT[:, k, :], xT[:, k, :], ALU.mult)
                        else:
                            pool.tensor_tensor(work[3][:, 0:L], xT[:, k, :], xT[:, k, :], ALU.mult)\
                                .then_inc(pool_own, 1)
                            pool.wait_ge(pool_own, base_own + k + (SQ - 1) * q)
                            ins = pool.tensor_tensor(sumsq[:, :], sumsq[:, :], work[3][:, 0:L], ALU.add)
                        ins.then_inc(sumsq_ready, 1)

        def mlp(layer):
            with pool.Fori(0, QUARTERS) as q:
                quarter(layer, q)
            squares[0] += SQ * QUARTERS
            pool_n[0] += (SQ - 1) * QUARTERS

        mlp(0)
        pool.wait_ge(tile_done, first_tile[CD_IN])
        own(pool.memset(tri[:, :], 1.0))
        own(pool.iota(dist[:, :].bitcast(I32), pattern=[[-1, L]], base=L - P, channel_multiplier=1))
        settle()
        own(pool.affine_select(out=tri[:, :], in_=tri[:, :], compare_op=ALU.is_ge, fill=0.0,
                               base=0, pattern=[[-1, P]], channel_multiplier=1))
        settle()
        pool.tensor_copy(dist[:, :], dist[:, :].bitcast(I32)).then_inc(l1_consts, 1)
        normalise()

        def keep_causal(buf, j, signal):
            v = buf[:, z_at[j]:z_at[j] + P]
            ins = pool.affine_select(out=v, in_=v, compare_op=ALU.is_gt, fill=0.0, base=0,
                                     pattern=[[1, P]], channel_multiplier=-1)
            ins.then_inc(signal, 1)

        for step in range(H + 1):
            if step >= 1:
                for j in range(NB):
                    pool.wait_ge(w_exp, NB * (step - 1) + j + 1)
                    keep_causal(z_sb[(step - 1) % 2], j, w_ready)
            if step < H:
                pool.wait_ge(sp_diag, step + 1)
                for j in range(NB):
                    keep_causal(sp_sb[step % 2], j, sp_ready)

        for k in range(SQ):
            d = drains[first_tile[CD_OUT] + k]
            square_tile(k, lambda: pool.wait_ge(dve_drain, d[1]))
        normalise()
        mlp(1)

    @block.scalar
    def _(act):
        def own(ins):
            act_n[0] += 1
            ins.then_inc(act_own, 1)

        def settle():
            act.wait_ge(act_own, act_n[0])

        def rows(v):
            return v.rearrange("(r c) -> r c", c=P)

        act.dma_start(raw_c[:, :], rows(c[0])).then_inc(c_in, 16)
        act.dma_start(raw_dt2[:, :], ssm_log_dt[0].rearrange("(t g) -> t g", g=2)).then_inc(dt_in, 16)
        act.dma_start(raw_a[0:32, :], norm_g.rearrange("l s (r c) -> (l s r) c", c=P)).then_inc(small_in, 16)
        act.dma_start(raw_a[32:P, :], ada_b.rearrange("l s (r c) -> (l s r) c", c=P)).then_inc(small_in, 16)
        for ri, src in enumerate((ssm_c_re, ssm_c_im)):
            for twice in range(2):
                act.dma_start(c_nat[ri][:, :, twice, :],
                              src[0].rearrange("(b g) c p -> (g c) b p", b=4)).then_inc(cn_in, 16)
        for ri, src in enumerate((ssm_b_re, ssm_b_im)):
            act.dma_start(bb[ri][:, :, :], src[0].rearrange("(t g) p c -> (g p) t c", g=2)).then_inc(b_in, 16)
        act.dma_start(skip[:, :], ssm_d[0].rearrange("(t q) -> q t", q=2 * C),
                      allow_slow_non_contiguous=True).then_inc(d_in, 16)
        act.dma_start(pool_w_t[:, :, :], pool_w[0].rearrange("g c d -> c g d")).then_inc(poolw_in, 16)

        def prep(n, q=None):
            m, over = n, 0
            if q is not None:
                over = q
            act.wait_ge(raw_in[n % 2], landed[n] + 64 * over)
            if n >= 2:
                act.wait_ge(tile_done, first_tile[n - 1] + 16 * over)
            w = 2 * HD + 8 if n == KI else SLOT
            act.activation(w_hi[n % 2][:, :, 0:w], raw[n % 2][:, :, 0:w], ACT.Copy).then_inc(hi_ready, 1)

        act.wait_ge(params, 1)
        act.activation(sm[:, 0, :], pb[:, 56:72], ACT.Exp).then_inc(setup_act, 1)
        act.wait_ge(setup_dve, 1)
        act.activation(sm[:, 4, :], sm[:, 1, :], ACT.Exp).then_inc(setup_act, 1)
        act.activation(sm[:, 5, :], sm[:, 1, :], ACT.Exp, scale=float(RUN)).then_inc(setup_act, 1)
        act.activation(sm[:, 6, :], sm[:, 3, :], ACT.Sin).then_inc(setup_act, 1)
        act.activation(sm[:, 7, :], sm[:, 3, :], ACT.Sin, scale=0.5).then_inc(setup_act, 1)

        for k in range(KC):
            act.wait_ge(xT_ps, k + 1)
            own(act.activation(xT[:, k, :], bank[k % 4], ACT.Copy))
            if k >= 4:
                act.wait_ge(norm_part, k - 3)
            act.activation(sq_x[:, k % 4, :], bank[k % 4], ACT.Square).then_inc(x_squared, 1)

        norms = [0]

        def norm_rstd(last_tile=None):
            norms[0] += 1
            if last_tile is not None:
                act.wait_ge(dve_drain, drains[last_tile][1])
                act.activation(work[2][:, 0:L], xT[:, KC - 1, :], ACT.Square).then_inc(last_square, 1)
            act.wait_ge(norm_sum, norms[0])
            own(act.activation(rstd[:, :], bank[6], ACT.Ln, scale=1.0 / D, bias=eps_t[:, 0:1]))
            settle()
            act.activation(rstd[:, :], rstd[:, :], ACT.Exp, scale=-0.5).then_inc(rstd_ready, 1)

        def modulate(a):
            act.wait_ge(mods_ready, a + 1)
            for k in range(KC):
                act.wait_ge(xn_ready, 8 * a + k + 1)
                act.activation(h_hi[:, k, :], work[k % 2][:, 0:L], ACT.Identity,
                               scale=mods[:, a, 8 + k:9 + k], bias=mods[:, a, k:k + 1]).then_inc(hh_ready, 1)

        norm_rstd()
        for i in range(8):
            act.wait_ge(mats_ps, i + 1)
            dst = (e_re, e_im)[i // 4][:, (i % 4) * 4:(i % 4) * 4 + 4, :]
            act.activation(dst.rearrange("p t n -> p (t n)"), bank[4 + i % 2], ACT.Copy).then_inc(mats_out, 1)
        for i in range(8, 12):
            act.wait_ge(mats_ps, i + 1)
            t = (i - 8) * 4
            act.activation(kr[:, t:t + 4, :].rearrange("p t n -> p (t n)"), bank[4 + i % 2][0:2 * C, :],
                           ACT.Copy).then_inc(mats_out, 1)
        act.wait_ge(ada_used_pe, ADA_PE)
        act.wait_ge(ada_used, ADA_EARLY - ADA_PE)
        prep(0)
        modulate(0)
        def copy_tile(t, dst, src=None, **kw):
            act.wait_ge(tile_done, t + 1)
            act.activation(dst, bank[t % 4] if src is None else src, ACT.Copy, **kw).then_inc(act_drain, 1)

        def u_by_runs():
            act.wait_ge(u_out, 16 * 4)
            act.wait_ge(kr_ready, 1)
            for m in range(RUN):
                j = RUN - 1 - m
                act.dma_start(u_run[m * C:(m + 1) * C, :, :],
                              u_dram.rearrange("(g c) t -> c g t", c=C)[:, :, j * NRUN:(j + 1) * NRUN])\
                   .then_inc(u_in, 16)

        for n in range(AB_IN, GLU):
            if n == AB_IN + 2:
                u_by_runs()
            prep(n + 1)
            for r in range(2):
                t = first_tile[n] + r
                if n < AB_IN + 2:
                    ct = 2 * (n - AB_IN) + r
                    copy_tile(t, ub[:, ct, :, :], bank[t % 4].rearrange("p (k j) -> p j k", j=RUN))
                    act.wait_ge(act_drain, drains[t][1])
                    act.dma_start(u_dram[ct * P:(ct + 1) * P, :],
                                  ub[:, ct, :, :].rearrange("p j k -> p (j k)")).then_inc(u_out, 16)
                else:
                    act.wait_ge(toep_in, 16 * 2 * RUN)
                    copy_tile(t, ua[:, 2 * (n - AB_IN - 2) + r, PAD:])
        prep(AB_OUT)
        for half in range(2):
            for b in (2 * half, 2 * half + 1):
                act.wait_ge(y_ps, b + 1)
                act.activation(y_run[:, b * 8:b * 8 + 8, :].rearrange("p g k -> p (g k)"), bank[b],
                               ACT.Copy).then_inc(y_copied, 1)
            act.wait_ge(y_copied, 2 * half + 2)
            g0 = half * G // 2
            for i in range(RUN):
                act.dma_start(
                    y_dram.rearrange("(g c) t -> c g t", c=C)[:, g0:g0 + G // 2, i * NRUN:(i + 1) * NRUN],
                    y_run[i * C:(i + 1) * C, g0:g0 + G // 2, :]).then_inc(y_out_s[half], 16)
        for ct in range(4):
            if ct % 2 == 0:
                act.wait_ge(y_out_s[ct // 2], 16 * RUN)
            act.dma_start(y_t[:, ct, :], y_dram[ct * P:(ct + 1) * P, :]).then_inc(y_in[ct // 2], 16)
        for ct in range(4):
            act.wait_ge(y_in[ct // 2], 16 * 2)
            own(act.activation(y_act[:, ct, :], y_t[:, ct, :], ACT.Gelu_apprx_tanh))
            settle()
            act.activation(yg_hi[:, ct, :], y_act[:, ct, :], ACT.Copy).then_inc(gelu_hi, 1)
        for g in range(4):
            act.wait_ge(pool_ps, g + 1)
            act.activation(h_hi[:, g, :], bank[4 + g], ACT.Identity, scale=pb[:, 16 + g:17 + g])\
               .then_inc(cat_hi, 1)
        for m in range(4):
            t = first_tile[GLU] + m
            act.wait_ge(tile_done, t + 1)
            act.activation(gate_t[:, m, :], bank[t % 4], ACT.Sigmoid, bias=pb[:, 20 + m:21 + m])\
               .then_inc(act_drain, 1)
        for m in range(4):
            act.wait_ge(cat_mid, m + 1)
            act.activation(h_hi[:, 4 + m, :], cat_f[:, m, :], ACT.Copy).then_inc(cat_hi, 1)
        for n in range(AB_OUT, MLP[0]):
            prep(n + 1)
        norm_rstd(first_tile[MLP[0]] - 1)
        modulate(1)

        def quarter(layer, q, last=False):
            n0, t0 = MLP[layer], first_tile[MLP[layer]]
            a0 = 32 * layer
            for i in range(8):
                if not (last and i == 7):
                    prep(n0 + i + 1, q)
                if i < 4:
                    for r in range(2):
                        t = 2 * i + r
                        act.wait_ge(tile_done, t0 + t + 1 + 16 * q)
                        if t >= 2:
                            act.wait_ge(a_ready, a0 + t - 1 + 8 * q)
                        act.activation(work[t % 2][:, 0:L], bank[(t0 + t) % 4], ACT.Relu)\
                           .then_inc(act_drain, 1)
                        act.wait_ge(act_drain, drains[t0 + t][1] + 8 * q)
                        act.activation(a_hi[:, t, :], work[t % 2][:, 0:L], ACT.Square)\
                           .then_inc(square_done, 1)

        with act.Fori(0, QUARTERS) as q:
            quarter(0, q)

        norm_rstd(first_tile[CD_IN] - 1)
        modulate(2)

        def index_relu(group):
            for cnt in group:
                i, h = INDEX[cnt]
                act.wait_ge(idx_ps, cnt + 1)
                if cnt >= 2:
                    act.wait_ge(idx_acc, cnt - 1)
                act.activation(work[cnt % 2][:, 0:(i + 1) * P], bank[4 + cnt % 4][:, 0:(i + 1) * P],
                               ACT.Relu).then_inc(idx_rel, 1)

        for j, (name, half) in enumerate(cd_slots):
            n = CD_IN + j
            prep(n + 1)
            t0 = first_tile[n]
            if name == "ki":
                copy_tile(t0, ki_t[:, :])
                copy_tile(t0 + 1, wi_row[:, :], bank[(t0 + 1) % 4][0:8, :], scale=IDX_SCALE)
            elif name in ("vd", "vc"):
                for b in range(NB):
                    copy_tile(t0 + b, qk[name][:, b, half * SLOT:(half + 1) * SLOT],
                              bank[(t0 + b) % 4][:, 0:SLOT])
            else:
                dst = qi_t if name == "qi" else qk[name]
                for r in range(2):
                    copy_tile(t0 + r, dst[:, 2 * half + r, :], scale=HD ** -0.5 if name in ("qd", "qc") else 1.0)
                    if n == index_first and r == 0:
                        act.wait_ge(wi_ps, 1)
                        act.activation(wi_t[:, :, :].rearrange("p b h -> p (b h)"), bank[7][:, 0:NB * 8],
                                       ACT.Copy).then_inc(wi_ready, 1)
                    index_relu(index_group(n, r))

        def out_hi(pair):
            for tile, b, signal in ((pair, 7, oc_ps), (4 + pair, 6, o_ps)):
                act.wait_ge(signal, 2 * pair + 2)
                act.activation(h_hi[:, tile, :], bank[b], ACT.Copy).then_inc(cat_hi, 1)

        act.wait_ge(tile_done, first_tile[CD_OUT])
        for step in range(H + 1):
            if step < H:
                z, s_ = z_sb[step % 2], sp_sb[step % 2]
                if step == 0:
                    act.wait_ge(dsel_ready, 1)
                if step >= 2:
                    act.wait_ge(o_ps, step - 1)
                for j in range(NB):
                    act.wait_ge(z_ps, NB * step + j + 1)
                    act.activation(z[:, z_at[j]:z_at[j] + (NB - j) * P], bank[j % 2][:, 0:(NB - j) * P],
                                   ACT.Copy).then_inc(z_copied, 1)
            if step >= 1:
                for i in range(NB):
                    act.wait_ge(t_ps, NB * (step - 1) + i + 1)
                    if i == 0 and step >= 2:
                        act.wait_ge(oc_ps, step - 1)
                    act.activation(pT[:, 0:i + 1, i * P:(i + 1) * P],
                                   bank[4 + i % 2][:, 0:(i + 1) * P].rearrange("p (j q) -> p j q", q=P),
                                   ACT.Copy).then_inc(t_copied, 1)
            if step >= 3 and step % 2 == 1:
                out_hi((step - 3) // 2)
            for i in range(NB):
                if step < H:
                    act.wait_ge(max_ready, NB * step + i + 1)
                    act.activation(probs(step, i), probs(step, i), ACT.Exp, bias=small[:, i:i + 1],
                                   accum_out=small[:, 8 + i:9 + i]).then_inc(p_exp, 1)
            if step >= 1:
                z = z_sb[(step - 1) % 2]
                for j in range(NB):
                    act.wait_ge(r_used, NB * (step - 1) + j + 1)
                    v_ = z[:, z_at[j]:z_at[j] + (NB - j) * P]
                    act.activation(v_, v_, ACT.Exp).then_inc(w_exp, 1)
            if step < H:
                act.wait_ge(z_abs, step + 1)
                own(act.activation(s_[:, :], s_[:, :], ACT.Exp, scale=-1.0))
                settle()
                act.activation(s_[:, :], s_[:, :], ACT.Ln, bias=eps_t[:, 1:2]).then_inc(z_soft, 1)
        out_hi(H // 2 - 1)
        for n in range(CD_OUT, MLP[1]):
            prep(n + 1)
        norm_rstd(first_tile[MLP[1]] - 1)
        modulate(3)
        with act.Fori(0, QUARTERS - 1) as q:
            quarter(1, q)
        quarter(1, QUARTERS - 1, last=True)
        norm_rstd(-1)
        for k in range(KC):
            act.wait_ge(fin_ps, k + 1)
            act.activation(y_out[:, :, k * P:(k + 1) * P], bank[k % 4].rearrange("p (t n) -> p t n", n=P),
                           ACT.Copy).then_inc(fin_copied, 1)

    @block.vector
    def _(dve):
        def own(ins):
            dve_n[0] += 1
            ins.then_inc(dve_own, 1)

        def settle():
            dve.wait_ge(dve_own, dve_n[0])

        def tt(o, a, b, op):
            own(dve.tensor_tensor(o, a, b, op))
            settle()

        def ts(o, a, s1, s2, op0, op1=ALU.bypass):
            own(dve.tensor_scalar(o, a, s1, s2, op0, op1))
            settle()

        def stt(o, a, s1, b, op0, op1):
            own(dve.scalar_tensor_tensor(out=o, in0=a, scalar=s1, in1=b, op0=op0, op1=op1))
            settle()

        ada_e = [ADA_PE]

        def ada_step():
            e = ada_e[0]
            ada_e[0] += 1
            k = e % 8
            if e < ADA_EARLY:
                buf, at_, signal = ada_first, e % ADA_FIRST, ada_in0
                dve.wait_ge(signal[at_], 16 * (e // ADA_FIRST + 1))
            else:
                buf, at_, signal = ada_ring, (e - ADA_EARLY) % ADA_RING, ada_in
                dve.wait_ge(signal[at_], 16 * ((e - ADA_EARLY) // ADA_RING + 1))
            acc = ada_acc_b if e // 8 in (2, 5) else ada_acc
            if k == 0:
                ins = dve.tensor_scalar(acc[:, :], buf[:, at_, :], pb[:, 0:1], None, ALU.mult)
            else:
                dve.wait_ge(ada_used, e - ADA_PE)
                ins = dve.scalar_tensor_tensor(out=acc[:, :], in0=buf[:, at_, :], scalar=pb[:, k:k + 1],
                                               in1=acc[:, :], op0=ALU.mult, op1=ALU.add)
            ins.then_inc(ada_used, 1)

        def ada_steps(count):
            for _ in range(count):
                ada_step()

        own(dve.memset(eps_t[:, 0:1], EPS))
        own(dve.memset(eps_t[:, 1:2], 1.0))
        dve.wait_ge(c_ps, 1)
        own(dve.tensor_copy(pb[:, 0:8], bank[7][:, 0:8]))
        settle()
        dve.wait_ge(dt_in, 16)
        dve.tensor_copy(raw_dt[:, :].rearrange("t (g p) -> t g p", g=2),
                        raw_dt2[:, :].unsqueeze(2).to_broadcast([GT, 2, S])).then_inc(dt_rows, 1)
        dve.wait_ge(consts, 2)
        own(dve.reciprocal(recip[:, :], recip[:, :]))
        tt(fold[:, :], ident[0:2 * C, 0:C], ident[0:2 * C, C:2 * C], ALU.add)
        for t in bd:
            own(dve.memset(t[:, :, :], 0.0))
        dve.wait_ge(params_ps, 1)
        own(dve.tensor_copy(pa[:, :], bank[4][:, 0:P]))
        own(dve.tensor_copy(pb[:, 8:72], bank[4][:, P:P + 64]))
        settle()
        dve.sem_inc(params, 1)

        DT, LRDT, TH, RED, MAG, MAG8, SIN, SINH, COS, AR, AI, DEN, RD, X1, X2, ZR, ZI, K_, CU, SU, \
            RC, RS = (0, 1, 2, 3, 4, 5, 6, 7, 8, 9, 10, 11, 12, 13, 14, 15, 16, 17, 18, 19, 20, 21)

        def v(i):
            return sm[:, i, :]

        lr, li = pb[:, 24:40], pb[:, 40:56]
        M, A, SB = ALU.mult, ALU.add, ALU.subtract
        dve.wait_ge(setup_act, 1)
        tt(v(LRDT), lr, v(DT), M)
        tt(v(TH), li, v(DT), M)
        magic = 1.5 * 2.0 ** 23
        c1 = 6.28125
        c2 = 0.0019350051879882812
        c3 = 2 * math.pi - c1 - c2
        ts(v(K_), v(TH), 1.0 / (2 * math.pi), None, M)
        ts(v(K_), v(K_), magic, None, A)
        ts(v(K_), v(K_), -magic, None, A)
        stt(v(RED), v(K_), -c1, v(TH), M, A)
        stt(v(RED), v(K_), -c2, v(RED), M, A)
        stt(v(RED), v(K_), -c3, v(RED), M, A)
        dve.tensor_scalar(v(RED), v(RED), 3.1415925, -3.1415925, ALU.min, ALU.max).then_inc(setup_dve, 1)
        dve.wait_ge(setup_act, 5)
        tt(v(COS), v(SINH), v(SINH), M)
        ts(v(COS), v(COS), -2.0, 1.0, M, A)
        tt(v(AR), v(MAG), v(COS), M)
        tt(v(AI), v(MAG), v(SIN), M)
        tt(v(X1), lr, lr, M)
        tt(v(X2), li, li, M)
        tt(v(DEN), v(X1), v(X2), A)
        own(dve.reciprocal(v(RD), v(DEN)))
        ts(v(X1), v(AR), -1.0, None, A)
        tt(v(ZR), v(X1), lr, M)
        tt(v(X2), v(AI), li, M)
        tt(v(ZR), v(ZR), v(X2), A)
        tt(v(ZR), v(ZR), v(RD), M)
        tt(v(ZI), v(AI), lr, M)
        tt(v(X2), v(X1), li, M)
        tt(v(ZI), v(ZI), v(X2), SB)
        tt(v(ZI), v(ZI), v(RD), M)
        own(dve.memset(pw_re[:, :, 0:1], 1.0))
        own(dve.memset(pw_im[:, :, 0:1], 0.0))
        own(dve.tensor_copy(pw_re[:, :, 1:2], v(AR).unsqueeze(2)))
        own(dve.tensor_copy(pw_im[:, :, 1:2], v(AI).unsqueeze(2)))
        settle()
        t1 = work[2][:, 0:GT * 4].rearrange("p (t m) -> p t m", t=GT)
        t2 = work[2][:, GT * 4:GT * 8].rearrange("p (t m) -> p t m", t=GT)
        for m in (1, 2, 4):
            ar = pw_re[:, :, m:m + 1].to_broadcast([P, GT, m])
            ai = pw_im[:, :, m:m + 1].to_broadcast([P, GT, m])
            pr, pi = pw_re[:, :, 1:m + 1], pw_im[:, :, 1:m + 1]
            nr, ni = pw_re[:, :, m + 1:2 * m + 1], pw_im[:, :, m + 1:2 * m + 1]
            tt(t1[:, :, 0:m], pr, ar, M)
            tt(t2[:, :, 0:m], pi, ai, M)
            tt(nr, t1[:, :, 0:m], t2[:, :, 0:m], SB)
            tt(t1[:, :, 0:m], pr, ai, M)
            tt(t2[:, :, 0:m], pi, ar, M)
            tt(ni, t1[:, :, 0:m], t2[:, :, 0:m], A)
        ts(pw_ni[:, :, :], pw_im[:, :, :], -1.0, None, M)
        dve.sem_inc(powers, 1)
        dve.wait_ge(params_ps, 2)
        for ri in range(2):
            for g2 in range(2):
                part = slice(S * g2, S * g2 + S)
                own(dve.tensor_copy(cb[ri][part, :, :],
                                    bank[5 + ri].rearrange("p (t g c) -> p g t c", g=2, c=C)[part, g2]))
        settle()
        dve.sem_inc(c_ready, 1)

        def ada_collect_early():
            n = 6 * ADA_EARLY // 8
            dve.wait_ge(ada_sum, ADA_EARLY // 8)
            dve.tensor_tensor(mods[:, 0, 0:n], bank[7][:, 0:n], pa[:, 32:32 + n], A)\
               .then_inc(mods_part, ADA_EARLY // 8)

        def ada_collect(u):
            a, qt = u // 4, u % 4
            dve.wait_ge(ada_sum, u + 1)
            dve.tensor_tensor(mods[:, a, qt * 6:qt * 6 + 6], bank[7][:, 0:6],
                              pa[:, 32 + a * 24 + qt * 6:32 + a * 24 + qt * 6 + 6], A)\
               .then_inc(mods_part, 1)

        def ada_scale(a, parts):
            dve.wait_ge(mods_part, parts)
            dve.scalar_tensor_tensor(out=mods[:, a, 8:16], in0=mods[:, a, 8:16], scalar=1.0,
                                     in1=pa[:, a * 8:a * 8 + 8], op0=A, op1=M).then_inc(mods_ready, 1)
            dve.wait_ge(mods_ready, a + 1)

        def ada_gate(a, parts):
            dve.wait_ge(mods_part, parts)
            own(dve.tensor_scalar(mods[:, a, 16:24], mods[:, a, 16:24], 1.0, None, A))
            settle()

        dve.wait_ge(b_in, 32)
        zr = v(ZR).unsqueeze(2).to_broadcast([P, GT, C])
        zi = v(ZI).unsqueeze(2).to_broadcast([P, GT, C])
        w3 = work[2][:, 0:GT * C].rearrange("p (t c) -> p t c", t=GT)
        tt(bz[0][:, :, :], bb[0][:, :, :], zr, M)
        tt(w3, bb[1][:, :, :], zi, M)
        tt(bz[0][:, :, :], bz[0][:, :, :], w3, SB)
        tt(bz[1][:, :, :], bb[1][:, :, :], zr, M)
        tt(w3, bb[0][:, :, :], zi, M)
        tt(bz[1][:, :, :], bz[1][:, :, :], w3, A)
        for ri in range(2):
            for g2 in range(2):
                part = slice(S * g2, S * g2 + S)
                own(dve.tensor_copy(bd[ri][part, :, g2 * C:(g2 + 1) * C], bz[ri][part, :, :]))
        settle()
        dve.sem_inc(bd_ready, 1)

        def fb(b):
            return b[:, :, :].unsqueeze(2).to_broadcast([P, GT, RUN, C])

        def fp(p):
            return p[:, :, 0:RUN].unsqueeze(3).to_broadcast([P, GT, RUN, C])

        ftmp = f_tmp[:, :, :, :]
        tt(f_re[:, :, :, :], fb(bz[0]), fp(pw_re), M)
        tt(ftmp, fb(bz[1]), fp(pw_im), M)
        tt(f_re[:, :, :, :], f_re[:, :, :, :], ftmp, SB)
        ada_steps(2)
        tt(f_im[:, :, :, :], fb(bz[1]), fp(pw_re), M)
        ada_steps(2)
        tt(ftmp, fb(bz[0]), fp(pw_im), M)
        dve.tensor_tensor(f_im[:, :, :, :], f_im[:, :, :, :], ftmp, A).then_inc(f_ready, 1)
        ada_steps(12)
        ada_collect_early()
        ada_scale(0, 3)

        def prep(n, q=None):
            dve.wait_ge(hi_ready, n + 1 + (0 if q is None else 8 * q))
            w = 2 * HD + 8 if n == KI else SLOT
            dve.tensor_tensor(w_lo[n % 2][:, :, 0:w], raw[n % 2][:, :, 0:w],
                              w_hi[n % 2][:, :, 0:w].bitcast(F32), SB).then_inc(lo_ready, 1)

        prep(0)

        def modulate(a):
            for k in range(KC):
                dve.wait_ge(xn_ready, 8 * a + k + 1)
                own(dve.tensor_scalar(work[2 + k % 2][:, 0:L], work[k % 2][:, 0:L],
                                      mods[:, a, 8 + k:9 + k], mods[:, a, k:k + 1], M, A))
                settle()
                dve.wait_ge(hh_ready, 8 * a + k + 1)
                dve.tensor_tensor(h_lo[:, k, :], work[2 + k % 2][:, 0:L], h_hi[:, k, :].bitcast(F32), SB)\
                   .then_inc(h_ready, 1)

        modulate(0)
        dve.wait_ge(mats_out, 12)
        dve.wait_ge(d_in, 16)
        tt(skip_d[:, :, :], skip[:, :].unsqueeze(2).to_broadcast([2 * C, GT, C]),
           fold[:, :].unsqueeze(1).to_broadcast([2 * C, GT, C]), M)
        dve.tensor_tensor(kr[:, :, 0:C], kr[:, :, 0:C], skip_d[:, :, :], A).then_inc(kr_ready, 1)
        prep(1)
        tt(v(X1), v(COS), v(COS), M)
        tt(v(X2), v(SIN), v(SIN), M)
        tt(v(CU), v(X1), v(X2), SB)
        tt(v(SU), v(COS), v(SIN), M)
        ts(v(SU), v(SU), 2.0, None, M)

        def double():
            tt(v(X1), v(CU), v(CU), M)
            tt(v(X2), v(SU), v(SU), M)
            tt(v(SU), v(CU), v(SU), M)
            ts(v(SU), v(SU), 2.0, None, M)
            tt(v(CU), v(X1), v(X2), SB)

        double()
        double()
        own(dve.tensor_copy(v(RC), v(MAG8)))
        keep = small
        dve.wait_ge(kr_ready, 1)
        own(dve.memset(rot_c[:, :, 0:1], 1.0))
        own(dve.memset(rot_s[:, :, 0:1], 0.0))
        own(dve.tensor_copy(keep[:, 16:32], v(MAG8)))
        settle()
        m = 1
        while m < NRUN:
            cu = v(CU).unsqueeze(2).to_broadcast([P, GT, m])
            su = v(SU).unsqueeze(2).to_broadcast([P, GT, m])
            x1 = work[2][:, 0:GT * m].rearrange("p (t m) -> p t m", t=GT)
            x2 = work[3][:, 0:GT * m].rearrange("p (t m) -> p t m", t=GT)
            tt(x1, rot_c[:, :, 0:m], cu, M)
            tt(x2, rot_s[:, :, 0:m], su, M)
            tt(rot_c[:, :, m:2 * m], x1, x2, SB)
            tt(x1, rot_c[:, :, 0:m], su, M)
            tt(x2, rot_s[:, :, 0:m], cu, M)
            tt(rot_s[:, :, m:2 * m], x1, x2, A)
            if 2 * m < NRUN:
                double()
            m *= 2
            if m == 4:
                prep(2)
        prep(3)
        dve.wait_ge(toep_in, 16 * 2 * RUN)
        own(dve.memset(ua[:, :, 0:PAD], 0.0))
        settle()
        dve.sem_inc(ua_pad, 1)
        ada_steps(8)

        def flat(t):
            return t[:, :, :].rearrange("p t k -> p (t k)")

        xr, xi = psum[:, 4 * L:6 * L], psum[:, 6 * L:8 * L]
        dve.wait_ge(u_out, 64)
        own(dve.memset(b_re[:, :, :, :], 0.0))
        dve.wait_ge(inj_ps, 1)
        tt(flat(s_re), xr, flat(rot_c), M)
        tt(flat(s_t1), xi, flat(rot_s), M)
        tt(flat(s_im), xi, flat(rot_c), M)
        tt(flat(s_t2), xr, flat(rot_s), M)
        dve.sem_inc(inj_read, 1)
        tt(flat(s_re), flat(s_re), flat(s_t1), A)
        tt(flat(s_im), flat(s_im), flat(s_t2), SB)
        for s_ in (s_re, s_im):
            for t in range(GT):
                own(dve.tensor_tensor_scan(s_[:, t, :], keep[:, 16 + t:17 + t].to_broadcast([P, NRUN]),
                                           s_[:, t, :], 0.0, M, A))
        settle()
        dve.wait_ge(tile_done, first_tile[GLU])
        own(dve.memset(b_im[:, :, :, :], 0.0))

        def to_blocks(b, op, last=False):
            for g2 in range(2):
                part = slice(S * g2, S * g2 + S)
                ins = dve.tensor_tensor(b[part, :, g2, 1:], s_t1[part, :, 0:NRUN - 1],
                                        s_t2[part, :, 0:NRUN - 1], op)
                if last and g2 == 1:
                    ins.then_inc(states, 1)
                else:
                    own(ins)
            if not last:
                settle()

        tt(flat(s_t1), flat(s_re), flat(rot_c), M)
        tt(flat(s_t2), flat(s_im), flat(rot_s), M)
        to_blocks(b_re, SB)
        tt(flat(s_t1), flat(s_re), flat(rot_s), M)
        tt(flat(s_t2), flat(s_im), flat(rot_c), M)
        to_blocks(b_im, A, last=True)
        ada_collect(3)
        ada_gate(0, 4)
        ada_steps(8)
        prep(GLU)
        ada_steps(4)
        ada_collect(4)
        ada_steps(2)
        for ct in range(4):
            dve.wait_ge(gelu_hi, ct + 1)
            dve.tensor_tensor(yg_lo[:, ct, :], y_act[:, ct, :], yg_hi[:, ct, :].bitcast(F32), SB)\
               .then_inc(gelu_lo, 1)
        for g in range(4):
            dve.wait_ge(cat_hi, g + 1)
            dve.scalar_tensor_tensor(out=h_lo[:, g, :], in0=bank[4 + g], scalar=pb[:, 16 + g:17 + g],
                                     in1=h_hi[:, g, :].bitcast(F32), op0=M, op1=SB).then_inc(cat_ready, 1)
        prep(AB_OUT)
        ada_steps(6)
        for m in range(4):
            dve.wait_ge(act_drain, drains[first_tile[GLU] + m][1])
            dve.tensor_tensor(cat_f[:, m, :].rearrange("p (k j) -> p j k", j=RUN),
                              gate_t[:, m, :].rearrange("p (j k) -> p j k", j=RUN),
                              y_act[:, m, :].rearrange("p (j k) -> p j k", j=RUN), M).then_inc(cat_mid, 1)
        for m in range(4):
            dve.wait_ge(cat_hi, 4 + m + 1)
            dve.tensor_tensor(h_lo[:, 4 + m, :], cat_f[:, m, :], h_hi[:, 4 + m, :].bitcast(F32), SB)\
               .then_inc(cat_ready, 1)
        ada_collect(5)

        def residual(t, k, a, q=None):
            over = 0 if q is None else q
            dve.wait_ge(tile_done, t + 1 + 16 * over)
            dve.scalar_tensor_tensor(out=xT[:, k, :], in0=bank[t % 4], scalar=mods[:, a, 16 + k:17 + k],
                                     in1=xT[:, k, :], op0=M, op1=A).then_inc(dve_drain, 1)

        for i in range(4):
            n = AB_OUT + i
            if i < 3:
                prep(n + 1)
            for r in range(2):
                residual(first_tile[n] + r, 2 * i + r, 0)
            if i == 1:
                ada_collect(6)
                ada_scale(1, 7)
            if i < 3:
                ada_steps(4)
        prep(MLP[0])
        ada_collect(7)
        ada_gate(1, 8)
        modulate(1)

        def quarter(layer, q, last=False):
            n0, t0 = MLP[layer], first_tile[MLP[layer]]
            a0 = 32 * layer
            for i in range(8):
                if not (last and i == 7):
                    prep(n0 + i + 1, q)
                if layer == 0:
                    for r in range(2):
                        e = 2 * i + r
                        k = e % 8
                        dve.wait_ge(ada_l1[i], 32 * q + 32)
                        src = ada_l1_ring[:, e, :]
                        if k == 0:
                            ins = dve.tensor_scalar(ada_acc[:, :], src, pb[:, 0:1], None, M)
                        else:
                            dve.wait_ge(ada_used, 2 * ADA_STEPS - ADA_PE + e + 16 * q)
                            ins = dve.scalar_tensor_tensor(out=ada_acc[:, :], in0=src,
                                                           scalar=pb[:, k:k + 1], in1=ada_acc[:, :],
                                                           op0=M, op1=A)
                        ins.then_inc(ada_used, 1)
                for r in range(2):
                    t = 2 * i + r
                    if i < 4:
                        dve.wait_ge(act_drain, drains[t0 + t][1] + 8 * q)
                        if t >= 1:
                            dve.wait_ge(a_ready, a0 + t + 8 * q)
                        dve.tensor_tensor(work[2][:, 0:L], work[t % 2][:, 0:L], work[t % 2][:, 0:L], M)\
                           .then_inc(sq_ready, 1)
                        dve.wait_ge(sq_ready, a0 + t + 1 + 8 * q)
                        dve.wait_ge(square_done, a0 + t + 1 + 8 * q)
                        dve.tensor_tensor(a_lo[:, t, :], work[2][:, 0:L], a_hi[:, t, :].bitcast(F32), SB)\
                           .then_inc(a_ready, 1)
                    else:
                        if t == 8:
                            dve.wait_ge(sumsq_ready, SQ * (1 if layer == 0 else 2 + QUARTERS) + SQ * q)
                        residual(t0 + t, t - 8, 2 * layer + 1, q)
                if layer == 0 and i % 4 == 3:
                    s = i // 4
                    dve.wait_ge(ada_sum, 8 + s + 1 + 2 * q)
                    dve.tensor_tensor(mods[:, 2 + s, bass.ds(q * 6, 6)], bank[7][:, 0:6],
                                      pa[:, bass.ds(q * 6 + 32 + (2 + s) * 24, 6)], A).then_inc(mods_part, 1)

        with dve.Fori(0, QUARTERS) as q:
            quarter(0, q)
        for a in (2, 3):
            ada_scale(a, 16)
            ada_gate(a, 16)
        modulate(2)

        top8 = small[:, 32:40]

        def block_score(i):
            return score[:, sc_at[i]:sc_at[i] + (i + 1) * P]

        def index_scores(group):
            for cnt in group:
                i, h = INDEX[cnt]
                if cnt == 0:
                    dve.wait_ge(wi_ready, 1)
                dve.wait_ge(idx_rel, cnt + 1)
                rel, w = work[cnt % 2][:, 0:(i + 1) * P], wi_t[:, i, h:h + 1]
                if h == 0:
                    ins = dve.tensor_scalar(block_score(i), rel, w, None, M)
                else:
                    dve.wait_ge(idx_acc, cnt)
                    ins = dve.scalar_tensor_tensor(out=block_score(i), in0=rel, scalar=w,
                                                   in1=block_score(i), op0=M, op1=A)
                ins.then_inc(idx_acc, 1)
                if h == 7:
                    dve.wait_ge(idx_acc, cnt + 1)
                    own(dve.memset(block_score(i)[0:CHUNK, i * P + CHUNK:(i + 1) * P], UNSEEN))
                    settle()

        rounds = [(i, r) for i in range(1, NB) for r in range(TOPK // 8)]

        def take_round(i):
            own(dve.max(out=top8, in_=block_score(i)))
            settle()
            own(dve.match_replace(out=block_score(i), in_to_replace=top8, in_values=block_score(i),
                                  imm_value=TAKEN))
            settle()

        def selected_distances():
            dve.wait_ge(l1_consts, 1)
            own(dve.scalar_tensor_tensor(out=dist[:, :], in0=dist[:, :], scalar=-1.0, in1=dist[:, :],
                                         op0=M, op1=ALU.max))
            settle()
            own(dve.tensor_copy(dsel[:, 0:P], dist[:, L - P:L]))
            settle()
            own(dve.memset(dsel[0:CHUNK, CHUNK:P], FAR))
            for i in range(1, NB):
                w = (i + 1) * P
                ts(block_score(i), block_score(i), TAKEN / 2, FAR, ALU.is_gt, M)
                off = L - P - i * P
                tt(dsel[:, sel_at[i]:sel_at[i] + w], block_score(i), dist[:, off:off + w], A)
            dve.sem_inc(dsel_ready, 1)

        for j, (name, half) in enumerate(cd_slots):
            n = CD_IN + j
            prep(n + 1)
            for r in range(2):
                index_scores(index_group(n, r))
            if n >= index_first + 3:
                for _ in range(6):
                    if rounds:
                        take_round(rounds.pop(0)[0])
        assert not rounds
        selected_distances()

        def out_lo(pair):
            for r, (tile, b) in enumerate(((pair, 7), (4 + pair, 6))):
                dve.wait_ge(cat_hi, 8 + 2 * pair + r + 1)
                dve.tensor_tensor(h_lo[:, tile, :], bank[b], h_hi[:, tile, :].bitcast(F32), SB)\
                   .then_inc(cat_ready, 1)

        def softplus_sum(head):
            dve.wait_ge(z_soft, head + 1)
            dve.scalar_tensor_tensor(out=sp_sb[head % 2][:, :], in0=z_sb[head % 2][:, :], scalar=0.0,
                                     in1=sp_sb[head % 2][:, :], op0=ALU.max, op1=A).then_inc(sp_diag, 1)

        for step in range(H + 1):
            if step == H:
                softplus_sum(step - 1)
            if step < H:
                for i in range(NB):
                    w = (i + 1) * P
                    dve.wait_ge(s_ps, NB * step + i + 1)
                    if step >= 2:
                        dve.wait_ge(t_ps, NB * (step - 2) + i + 1)
                    dve.scalar_tensor_tensor(out=probs(step, i), in0=dsel[:, sel_at[i]:sel_at[i] + w],
                                             scalar=-SLOPES[step], in1=bank[4 + i % 2][:, 0:w],
                                             op0=M, op1=A).then_inc(s_used, 1)
                    dve.wait_ge(s_used, NB * step + i + 1)
                    dve.reduce_max(small[:, i:i + 1], probs(step, i), AX_X, negate=True)\
                       .then_inc(max_ready, 1)
                    if i == 1 and step >= 1:
                        softplus_sum(step - 1)
                z, s_ = z_sb[step % 2], sp_sb[step % 2]
                dve.wait_ge(z_copied, NB * (step + 1))
                dve.scalar_tensor_tensor(out=s_[:, :], in0=z[:, :], scalar=-1.0, in1=z[:, :],
                                         op0=M, op1=ALU.max).then_inc(z_abs, 1)
            if step >= 3 and step % 2 == 1:
                out_lo((step - 3) // 2)
            if step >= 1:
                zp = z_sb[(step - 1) % 2]
                for j in range(NB):
                    dve.wait_ge(r_ps, NB * (step - 1) + j + 1)
                    v_ = zp[:, z_at[j]:z_at[j] + (NB - j) * P]
                    dve.tensor_tensor(v_, v_, bank[2 + j % 2][:, 0:(NB - j) * P], SB).then_inc(r_used, 1)
            if step < H:
                for i in range(NB):
                    dve.wait_ge(p_exp, NB * step + i + 1)
                    own(dve.reciprocal(small[:, 12 + i:13 + i], small[:, 8 + i:9 + i]))
                    settle()
                    dve.tensor_scalar(probs(step, i), probs(step, i), small[:, 12 + i:13 + i], None, M)\
                       .then_inc(p_ready, 1)
        out_lo(H // 2 - 1)

        for i in range(4):
            n = CD_OUT + i
            if i < 3:
                prep(n + 1)
            for r in range(2):
                residual(first_tile[n] + r, 2 * i + r, 2)
        prep(MLP[1])
        modulate(3)
        with dve.Fori(0, QUARTERS - 1) as q:
            quarter(1, q)
        quarter(1, QUARTERS - 1, last=True)
        dve.wait_ge(rstd_ready, 5)
        for k in range(KC):
            if k >= 4:
                dve.wait_ge(fin_ps, k - 3)
            dve.scalar_tensor_tensor(out=work[k % 4][:, 0:L], in0=xT[:, k, :], scalar=pb[:, 8 + k:9 + k],
                                     in1=rstd[:, :], op0=M, op1=M).then_inc(fin_t, 1)

    @block.tensor
    def _(pe):
        def mm(o, lhsT, rhs, start, stop, **kw):
            return nc.tensor.matmul(o, lhsT, rhs, start=start, stop=stop, **kw)

        def transpose(o, in_):
            n = in_.shape[0]
            return nc.tensor.transpose(o, in_, ident[0:n, 0:n])

        def product(o, w, x_, first, last):
            (w_h, w_l), (x_h, x_l) = w, x_
            mm(o, w_h, x_h, first, False)
            mm(o, w_h, x_l, False, False)
            return mm(o, w_l, x_h, False, last)

        pe.wait_ge(consts, 2)
        pe.wait_ge(c_in, 16)
        transpose(bank[7][:, 0:KC], raw_c[:, :]).then_inc(c_ps, 1)
        pe.wait_ge(small_in, 16 * 7)
        transpose(bank[4][:, 0:P], raw_a[:, :])
        transpose(bank[4][:, P:P + 48], raw_b[:, :])
        pe.wait_ge(dt_rows, 1)
        transpose(bank[4][:, P + 48:P + 64], raw_dt[:, :]).then_inc(params_ps, 1)
        pe.wait_ge(cn_in, 16 * 4)
        for ri in range(2):
            for b in range(4):
                last = transpose(bank[5 + ri][:, b * P:(b + 1) * P],
                                 c_nat[ri][:, b, :, :].rearrange("p w s -> p (w s)"))
        last.then_inc(params_ps, 1)

        def x_squares(k):
            if k == 0:
                pe.wait_ge(c_ready, 1)
            pe.wait_ge(x_squared, k + 1)
            mm(bank[6], ones[:, :], sq_x[:, k % 4, :], k == 0, k == KC - 1)\
                .then_inc(norm_sum if k == KC - 1 else norm_part, 1)

        def ada_early(e):
            pe.wait_ge(ada_in0[e % ADA_FIRST], 16 * (e // ADA_FIRST + 1))
            for j in range(6):
                o = bank[7][:, e // 8 * 6 + j:e // 8 * 6 + j + 1]
                last = mm(o, ada_first[:, e % ADA_FIRST, j * P:(j + 1) * P], pb[:, e % 8:e % 8 + 1],
                          e == 0 and j == 0, e == ADA_PE - 1 and j == 5, skip_group_check=True)
            last.then_inc(ada_used_pe, 1)
            if e == ADA_PE - 1:
                pe.wait_ge(ada_used_pe, ADA_PE)
                pe.sem_inc(ada_sum, 1)

        for e in range(4):
            ada_early(e)
        pe.wait_ge(x_in, 16)
        for k in range(KC):
            if k >= 4:
                pe.wait_ge(x_squared, k - 3)
                x_squares(k - 4)
            for b in range(NB):
                last = transpose(bank[k % 4][:, b * P:(b + 1) * P], x_nat[:, b, k * P:(k + 1) * P])
            last.then_inc(xT_ps, 1)
        for k in range(KC - 4, KC):
            x_squares(k)

        def ada_sums(value, unit, q=None):
            early = unit < ADA_EARLY // 8
            if not early:
                pe.wait_ge(mods_part, unit)
            pe.wait_ge(ada_used, value - ADA_PE)
            acc = ada_acc_b if q is None and unit in (2, 5) else ada_acc
            c0 = 6 * unit if early else 0
            for j in range(6):
                last = mm(bank[7][:, c0 + j:c0 + j + 1], acc[:, j * P:(j + 1) * P], ones[:, 0:1], True, True)
            last.then_inc(ada_sum, 1)

        norms = [1]

        def norm(value):
            pe.wait_ge(sumsq_ready, value)
            pe.wait_ge(rstd_ready, norms[0])
            mm(bank[6], ones[:, :], sumsq[:, :], True, False)
            pe.wait_ge(last_square, norms[0])
            mm(bank[6], ones[:, :], work[2][:, 0:L], False, True).then_inc(norm_sum, 1)
            norms[0] += 1

        for e in range(4, ADA_PE):
            ada_early(e)
        pe.wait_ge(f_ready, 1)
        for i in range(8):
            if i >= 2:
                pe.wait_ge(mats_out, i - 1)
            f = (f_re, f_im)[i // 4]
            for r in range(4):
                t = (i % 4) * 4 + r
                last = transpose(bank[4 + i % 2][:, r * P:(r + 1) * P],
                                 f[:, t, :, :].rearrange("p m c -> p (m c)"))
            last.then_inc(mats_ps, 1)
        ada_sums(16, 1)
        pe.wait_ge(g_ready, 1)
        pe.wait_ge(bd_ready, 1)
        for i in range(8, 12):
            pe.wait_ge(mats_out, i - 1)
            for r in range(4):
                t = (i - 8) * 4 + r
                o = bank[4 + i % 2][0:2 * C, r * P:(r + 1) * P]
                for n_, (b_, g_) in enumerate(((bd[0], g_re), (bd[1], g_ni))):
                    last = mm(o, b_[:, t, :], g_[:, t, 0:RUN, :].rearrange("p m c -> p (m c)"),
                              n_ == 0, n_ == 1)
            last.then_inc(mats_ps, 1)
        ada_sums(24, 2)

        def slot_ready(n, q=None):
            pe.wait_ge(lo_ready, n + 1 + (0 if q is None else 8 * q))

        def tile_free(t, q=None):
            if t >= 4:
                by_dve, count = drains[t - 4]
                pe.wait_ge(dve_drain if by_dve else act_drain, count + (0 if q is None else 8 * q))

        def weight(n, k, c0, w=P):
            return w_hi[n % 2][:, k, c0:c0 + w], w_lo[n % 2][:, k, c0:c0 + w]

        def h(k, c0=0, w=L):
            return h_hi[:, k, c0:c0 + w], h_lo[:, k, c0:c0 + w]

        def tile(n, t, r, q=None, moving=h):
            tile_free(t, q)
            for k in range(8):
                last = product(bank[t % 4], weight(n, k, r * P), moving(k), k == 0, k == 7)
            last.then_inc(tile_done, 1)

        def first_tiles(n, t, ready, value, q=None, moving=h):
            for r in range(2):
                tile_free(t + r, q)
            for k in range(8):
                pe.wait_ge(ready, value(k))
                for r in range(2):
                    last = product(bank[(t + r) % 4], weight(n, k, r * P), moving(k), k == 0, k == 7)
                    if k == 7:
                        last.then_inc(tile_done, 1)

        def plain_slots(n0, count, ready, base):
            for n in range(n0, n0 + count):
                slot_ready(n)
                if n == n0:
                    first_tiles(n, first_tile[n], ready, lambda k: base + k + 1)
                else:
                    for r in range(2):
                        tile(n, first_tile[n] + r, r)

        def injections():
            pe.wait_ge(u_in, 16 * RUN)
            pe.wait_ge(mods_part, 3)
            for g in range(G):
                t, p0 = g // 2, S * (g % 2)
                for e_, b0 in ((e_re, 4), (e_im, 6)):
                    o = bank[b0 + t // 8][p0:p0 + S, (t % 8) * NRUN:(t % 8 + 1) * NRUN]
                    last = mm(o, e_[:, t, p0:p0 + S], u_run[:, g, :], True, True)
            last.then_inc(inj_ps, 1)

        plain_slots(AB_IN, 3, h_ready, 0)
        injections()
        plain_slots(AB_IN + 3, 1, h_ready, 0)
        pe.wait_ge(toep_in, 16 * 2 * RUN)
        pe.wait_ge(act_drain, drains[first_tile[GLU] - 1][1])

        def y_at(g, count=1):
            return bank[g // 8][:, (g % 8) * NRUN:(g % 8 + count) * NRUN]

        for g in range(G):
            mm(y_at(g), toep[:, g, :], u_run[:, g, :], g % 8 == 0, False, skip_group_check=True)
        pe.wait_ge(inj_read, 1)
        ada_sums(8 * 4, 3)
        pe.wait_ge(states, 1)
        for t in range(GT):
            for g_, b_ in ((g_re, b_re), (g_ni, b_im)):
                last = mm(y_at(2 * t, 2), g_[:, t, 1:, :].rearrange("p m c -> p (m c)"),
                          b_[:, t, :, :].rearrange("p g k -> p (g k)"),
                          False, g_ is g_ni and t % 4 == 3, skip_group_check=True)
            if t % 4 == 3:
                last.then_inc(y_ps, 1)
        ada_sums(8 * 5, 4)
        pe.wait_ge(poolw_in, 16)
        for g in range(4):
            pe.wait_ge(pooled, g + 1)
            if g == 3:
                pe.wait_ge(mods_part, 5)
            mm(bank[4 + g], pool_w_t[:, g, :], ua[:, g, PAD:], True, True).then_inc(pool_ps, 1)
        slot_ready(GLU)
        pe.wait_ge(y_copied, 4)
        glu_h = w_hi[GLU % 2][:, :, :].rearrange("p a b -> p (a b)").rearrange("p (k n) -> p k n", k=4)
        glu_l = w_lo[GLU % 2][:, :, :].rearrange("p a b -> p (a b)").rearrange("p (k n) -> p k n", k=4)
        t = first_tile[GLU]
        for m in range(4):
            tile_free(t + m)
        for k in range(4):
            pe.wait_ge(gelu_lo, k + 1)
            for m in range(4):
                last = product(bank[(t + m) % 4],
                               (glu_h[:, k, m * P:(m + 1) * P], glu_l[:, k, m * P:(m + 1) * P]),
                               (yg_hi[:, k, :], yg_lo[:, k, :]), k == 0, k == 3)
                if k == 3:
                    last.then_inc(tile_done, 1)
        pe.wait_ge(cat_ready, 4)
        ada_sums(8 * 6, 5)
        for i in range(4):
            n = AB_OUT + i
            slot_ready(n)
            if i == 0:
                first_tiles(n, first_tile[n], cat_ready, lambda k: k + 1)
            else:
                for r in range(2):
                    tile(n, first_tile[n] + r, r)
            if i % 2 == 1:
                ada_sums(8 * (7 + i // 2), 6 + i // 2)
        norm(SQ)

        def a(k):
            return a_hi[:, k, :], a_lo[:, k, :]

        def quarter(layer, q):
            n0, t0 = MLP[layer], first_tile[MLP[layer]]
            a0 = 32 * layer
            for i in range(8):
                slot_ready(n0 + i, q)
                t, moving = t0 + 2 * i, h if i < 4 else a
                if i == 0:
                    first_tiles(n0, t, h_ready, lambda k: 8 * (2 * layer + 1) + k + 1, q)
                elif i == 4:
                    first_tiles(n0 + 4, t, a_ready, lambda k: a0 + k + 1 + 8 * q, q, a)
                else:
                    for r in range(2):
                        tile(n0 + i, t + r, r, q, moving)
                if layer == 0 and i % 4 == 3:
                    ada_sums(2 * ADA_STEPS + 8 * (i // 4 + 1) + 16 * q, 8 + i // 4 + 2 * q, q)

        with pe.Fori(0, QUARTERS) as q:
            quarter(0, q)
        norm(SQ * (1 + QUARTERS))

        def index_products(group):
            for cnt in group:
                i, hh = INDEX[cnt]
                if cnt == 3:
                    pe.wait_ge(wi_ready, 1)
                if cnt >= 4:
                    pe.wait_ge(idx_rel, cnt - 3)
                p0 = HD * (hh % 2)
                mm(bank[4 + cnt % 4][:, 0:(i + 1) * P], qi_t[p0:p0 + HD, hh // 2, i * P:(i + 1) * P],
                   ki_t[p0:p0 + HD, 0:(i + 1) * P], True, True).then_inc(idx_ps, 1)

        for j, (name, half) in enumerate(cd_slots):
            n = CD_IN + j
            slot_ready(n)
            t0 = first_tile[n]
            if name == "ki":
                tile(n, t0, 0)
                tile_free(t0 + 1)
                for k in range(8):
                    last = product(bank[(t0 + 1) % 4][0:8, :], weight(n, k, P, 8), h(k), k == 0, k == 7)
                last.then_inc(tile_done, 1)
            elif name in ("vd", "vc"):
                for b in range(NB):
                    tile_free(t0 + b)
                    for k in range(8):
                        last = product(bank[(t0 + b) % 4][:, 0:SLOT], h(k, b * P, P),
                                       weight(n, k, 0, SLOT), k == 0, k == 7)
                    last.then_inc(tile_done, 1)
            else:
                if j == 0:
                    first_tiles(n, t0, h_ready, lambda k: 16 + k + 1)
                else:
                    for r in range(2):
                        tile(n, t0 + r, r)
                        if n == index_first and r == 0:
                            pe.wait_ge(act_drain, drains[first_tile[KI] + 1][1])
                            for b in range(NB):
                                last = transpose(bank[7][:, b * 8:(b + 1) * 8], wi_row[:, b * P:(b + 1) * P])
                            last.then_inc(wi_ps, 1)
                        index_products(index_group(n, r))

        def dsa_cat(pair):
            return 8 + 2 * pair + 1

        def stick_cat(pair):
            return 8 + 2 * pair + 2

        qd, kd, vd, qc, kc, vc = (qk[x_] for x_ in ("qd", "kd", "vd", "qc", "kc", "vc"))
        pe.wait_ge(act_drain, drains[first_tile[CD_OUT] - 1][1])
        for step in range(H + 1):
            p0 = HD * (step % 2)
            pr = step - 1
            po = HD * (pr % 2)
            if step < H:
                for i in range(NB):
                    if step >= 2 and i < 2:
                        pe.wait_ge(t_copied, NB * (step - 2) + i + 3)
                    elif step or i >= 2:
                        pe.wait_ge(s_used, NB * step + i - 1)
                    mm(bank[4 + i % 2][:, 0:(i + 1) * P], qc[p0:p0 + HD, step // 2, i * P:(i + 1) * P],
                       kc[p0:p0 + HD, step // 2, 0:(i + 1) * P], True, True).then_inc(s_ps, 1)
                for j in range(NB):
                    if step or j >= 2:
                        pe.wait_ge(z_copied, NB * step + j - 1)
                    mm(bank[j % 2][:, 0:(NB - j) * P], kd[p0:p0 + HD, step // 2, j * P:(j + 1) * P],
                       qd[p0:p0 + HD, step // 2, j * P:], True, True).then_inc(z_ps, 1)
            if step >= 1:
                for i in range(NB):
                    pe.wait_ge(p_ready, NB * pr + i + 1)
                    if step < H and i < 2:
                        pe.wait_ge(s_used, NB * step + i + 3)
                    else:
                        pe.wait_ge(t_copied, NB * pr + i - 1)
                    for j in range(i + 1):
                        last = transpose(bank[4 + i % 2][:, j * P:(j + 1) * P], probs(pr, i)[:, j * P:(j + 1) * P])
                    last.then_inc(t_ps, 1)
                s_, z = sp_sb[pr % 2], z_sb[pr % 2]
                pe.wait_ge(sp_ready, NB * step)
                for j in range(NB):
                    if pr or j >= 2:
                        pe.wait_ge(r_used, NB * pr + j - 1)
                    o = bank[2 + j % 2]
                    w = (NB - j) * P
                    last = mm(o[:, 0:w], tri[:, :], s_[:, z_at[j]:z_at[j] + w], True, j == NB - 1)
                    for j2 in range(j + 1, NB):
                        w2 = (NB - j2) * P
                        last = mm(o[:, w - w2:w], ones[:, :], s_[:, z_at[j2]:z_at[j2] + w2], False,
                                  j2 == NB - 1)
                    last.then_inc(r_ps, 1)
                if pr >= 2 and pr % 2 == 0:
                    pe.wait_ge(cat_ready, dsa_cat(pr // 2 - 1))
                pe.wait_ge(t_copied, NB * (pr + 1))
                for j in range(NB):
                    last = mm(bank[7][po:po + HD, j * P:], vc[:, j, pr * HD:(pr + 1) * HD],
                              pT[:, j, j * P:], j == 0, j == NB - 1)
                last.then_inc(oc_ps, 1)
                if pr >= 2 and pr % 2 == 0:
                    pe.wait_ge(cat_ready, stick_cat(pr // 2 - 1))
                for j in range(NB):
                    pe.wait_ge(w_ready, NB * pr + j + 1)
                    last = mm(bank[6][po:po + HD, j * P:], vd[:, j, pr * HD:(pr + 1) * HD],
                              z[:, z_at[j]:z_at[j] + (NB - j) * P], j == 0, j == NB - 1)
                last.then_inc(o_ps, 1)
        pe.wait_ge(cat_ready, 16)
        plain_slots(CD_OUT, 4, cat_ready, 8)
        norm(SQ * (2 + QUARTERS))
        with pe.Fori(0, QUARTERS) as q:
            quarter(1, q)
        norm(SQ * (2 + 2 * QUARTERS))
        for k in range(KC):
            pe.wait_ge(fin_t, k + 1)
            if k >= 4:
                pe.wait_ge(fin_copied, k - 3)
            for b in range(NB):
                last = transpose(bank[k % 4][:, b * P:(b + 1) * P], work[k % 4][:, b * P:(b + 1) * P])
            last.then_inc(fin_ps, 1)

    block.__exit__(None, None, None)


INPUTS = ["x", "c", "norm_g", "ada_w", "ada_b", "mlp_w1", "mlp_w2", "ab_w_in", "ab_w_out", "pool_w",
          "pool_scale", "ssm_lam_re", "ssm_lam_im", "ssm_log_dt", "ssm_b_re", "ssm_b_im", "ssm_c_re",
          "ssm_c_im", "ssm_d", "glu_w", "glu_b", "cd_w_in", "cd_w_out", "final_g"]


def kernel(**inputs):
    import numpy as np
    import concourse.bacc as bacc
    from concourse.bass_utils import run_bass_kernel_spmd

    nc = bacc.Bacc("TRN2", target_bir_lowering=False, num_devices=1)
    arrays, args = {}, []
    for name in INPUTS:
        a = np.ascontiguousarray(inputs[name])
        arrays[f"in_{name}"] = a
        args.append(nc.dram_tensor(f"in_{name}", a.shape, mybir.dt.from_np(a.dtype),
                                   kind="ExternalInput").ap())
    out = nc.dram_tensor("out", (1, L, D), F32, kind="ExternalOutput")
    trunk(nc, *args, out.ap())
    r = run_bass_kernel_spmd(nc, [arrays], core_ids=[0])
    return r.results[0]["out"]
```
